# Optimizing a Trainium2 kernel written in Bass

```python
import jax, jax.numpy as jnp
from jax import lax
import numpy as np

D_MODEL = 1024
BATCH = 1
SEQ = 512
DEPTH = 2
DEC_BATCH = 8
DEC_SEQ = 1
PAST_LEN = 2048
PAGE_SIZE = 128

N_A = DEPTH // 2
N_B = DEPTH - N_A
D_FF = 4 * D_MODEL
RMS_EPS = 1e-6
HG_EXPAND = 128
HG_HEADS = D_MODEL // HG_EXPAND
HG_K = HG_EXPAND
HG_V = D_MODEL // HG_HEADS
HG_CHUNK = 64
NSA_HEADS = 16
NSA_HEAD_DIM = D_MODEL // NSA_HEADS
NSA_KV_GROUPS = 4
NSA_HPG = NSA_HEADS // NSA_KV_GROUPS
NSA_SCALE = NSA_HEAD_DIM ** -0.5
CMP_LEN = 32
CMP_STRIDE = 16
CMP_HID = NSA_HEAD_DIM
SLC_BLOCK = 64
SLC_TOPK = 16
WINDOW = 512
Q_BLOCK = 64
FORCED_SCORE = 1e4
NEG_INF = -1e30
TINY = 1e-30

kernel_name = "hgrn2_nsa_yoco_decoder_step"

def rmsnorm(x, g):
    xf = x.astype(jnp.float32)
    y = xf * lax.rsqrt(jnp.mean(xf * xf, axis=-1, keepdims=True) + RMS_EPS)
    return (y * g.astype(jnp.float32)).astype(x.dtype)

def sq_relu_mlp(h, w_up, w_down):
    return jnp.square(jax.nn.relu(h @ w_up)) @ w_down

def masked_softmax(s, mask):
    s = jnp.where(mask, s.astype(jnp.float32), NEG_INF)
    e = jnp.exp(s - jnp.max(s, axis=-1, keepdims=True)) * mask
    return e / jnp.maximum(jnp.sum(e, axis=-1, keepdims=True), TINY)

def hgrn_lower_bounds(lb_logits):
    cum = jnp.cumsum(jax.nn.softmax(lb_logits.astype(jnp.float32), axis=0), axis=0)
    return cum - cum[:1]

def hgrn_chunk(S0, q, k, v, logf):
    C = q.shape[1]
    b = jnp.cumsum(logf, axis=1)
    causal = jnp.tril(jnp.ones((C, C), dtype=bool))[None, :, :, None, None]
    dec = jnp.exp(jnp.where(causal, b[:, :, None] - b[:, None, :], -jnp.inf))
    a = jnp.einsum('btshk,bshk->bhts', q[:, :, None] * dec, k)
    o = jnp.einsum('bhts,bshv->bthv', a, v) + jnp.einsum('bthk,bhkv->bthv', q * jnp.exp(b), S0)
    b_end = b[:, -1]
    S = jnp.exp(b_end)[..., None] * S0 + jnp.einsum('bshk,bshv->bhkv', k * jnp.exp(b_end[:, None] - b), v)
    return S, o

def hgrn_mix(h, S0, w_in, lb, onorm, w_out):
    B, T, _ = h.shape
    hk, hv = HG_HEADS * HG_K, HG_HEADS * HG_V
    proj = (h @ w_in).astype(jnp.float32)
    zq, zf, zi, zg = jnp.split(proj, [hk, 2 * hk, 2 * hk + hv], axis=-1)
    lb = lb.reshape(HG_HEADS, HG_K)
    logf = jnp.logaddexp(jnp.log(lb), jnp.log1p(-lb) + jax.nn.log_sigmoid(zf.reshape(B, T, HG_HEADS, HG_K)))
    q = zq.reshape(B, T, HG_HEADS, HG_K)
    k = 1.0 - jnp.exp(logf)
    v = zi.reshape(B, T, HG_HEADS, HG_V)
    C = HG_CHUNK if T % HG_CHUNK == 0 else T
    n = T // C

    def to_chunks(a):
        return jnp.moveaxis(a.reshape(B, n, C, *a.shape[2:]), 1, 0)

    def step(S, xs):
        return hgrn_chunk(S, *xs)

    S, o = lax.scan(step, S0.astype(jnp.float32), (to_chunks(q), to_chunks(k), to_chunks(v), to_chunks(logf)))
    o = jnp.moveaxis(o, 0, 1).reshape(B, T, HG_HEADS, HG_V)
    o = o * lax.rsqrt(jnp.mean(o * o, axis=-1, keepdims=True) + RMS_EPS) * onorm.astype(jnp.float32).reshape(HG_HEADS, HG_V)
    o = o.reshape(B, T, hv) * jax.nn.silu(zg)
    return o.astype(h.dtype) @ w_out, S.astype(S0.dtype)

def compress(kv, pe, w1, w2):
    B, T, G, dk = kv.shape
    n_cmp = (T - CMP_LEN) // CMP_STRIDE + 1
    r = CMP_LEN // CMP_STRIDE
    sub = kv[:, :(n_cmp + r - 1) * CMP_STRIDE].reshape(B, n_cmp + r - 1, CMP_STRIDE, G, dk)
    blocks = jnp.concatenate([sub[:, i:i + n_cmp] for i in range(r)], axis=2)
    blocks = blocks + pe[None, None, :, None, :]
    flat = jnp.moveaxis(blocks, 3, 2).reshape(B, n_cmp, G, CMP_LEN * dk)
    return jax.nn.silu(flat @ w1) @ w2

def nsa_attend(q, gates, t_pos, kc, vc, ks_b, vs_b, M, kw, vw, w_pos):
    B, Q = q.shape[:2]
    qg = q.reshape(B, Q, NSA_KV_GROUPS, NSA_HPG, NSA_HEAD_DIM) * NSA_SCALE
    n_cmp = kc.shape[1]
    n_slc = ks_b.shape[2]
    e_pos = jnp.arange(n_cmp) * CMP_STRIDE + CMP_LEN - 1
    mask_c = (e_pos[None, :] <= t_pos[:, None])[None, :, None, None, :]
    p_c = masked_softmax(jnp.einsum('bqghd,bigd->bqghi', qg, kc), mask_c)
    o_c = jnp.einsum('bqghi,bigd->bqghd', p_c.astype(vc.dtype), vc)
    imp = jnp.einsum('bqghi,ij->bqgj', p_c, M)
    blk = jnp.arange(n_slc)[None, :]
    cur = (t_pos // SLC_BLOCK)[:, None]
    forced = (blk == 0) | (blk == cur) | (blk == cur - 1)
    score = jnp.where(forced[None, :, None], FORCED_SCORE, jnp.where((blk <= cur)[None, :, None], imp, -1.0))
    _, idx = lax.top_k(score, min(SLC_TOPK, n_slc))
    n_sel = idx.shape[-1]
    bi = jnp.arange(B)[:, None, None, None]
    gi = jnp.arange(NSA_KV_GROUPS)[None, None, :, None]
    k_sel = ks_b[bi, gi, idx]
    v_sel = vs_b[bi, gi, idx]
    pos_sel = idx[..., None] * SLC_BLOCK + jnp.arange(SLC_BLOCK)
    s_s = jnp.einsum('bqghd,bqgnrd->bqghnr', qg, k_sel).reshape(B, Q, NSA_KV_GROUPS, NSA_HPG, n_sel * SLC_BLOCK)
    mask_s = (pos_sel <= t_pos[None, :, None, None, None]).reshape(B, Q, NSA_KV_GROUPS, 1, n_sel * SLC_BLOCK)
    p_s = masked_softmax(s_s, mask_s).reshape(B, Q, NSA_KV_GROUPS, NSA_HPG, n_sel, SLC_BLOCK)
    o_s = jnp.einsum('bqghnr,bqgnrd->bqghd', p_s.astype(v_sel.dtype), v_sel)
    mask_w = (w_pos[None, :] <= t_pos[:, None]) & (w_pos[None, :] > t_pos[:, None] - WINDOW) & (w_pos[None, :] >= 0)
    p_w = masked_softmax(jnp.einsum('bqghd,bkgd->bqghk', qg, kw), mask_w[None, :, None, None, :])
    o_w = jnp.einsum('bqghk,bkgd->bqghd', p_w.astype(vw.dtype), vw)
    g = gates.reshape(B, Q, 3, NSA_KV_GROUPS, NSA_HPG)[..., None]
    o = g[:, :, 0] * o_c + g[:, :, 1] * o_s + g[:, :, 2] * o_w
    return o.reshape(B, Q, NSA_HEADS * NSA_HEAD_DIM)

def nsa_mix(h, ctx, attend, w_q, w_o):
    B, T, _ = h.shape
    nq = NSA_HEADS * NSA_HEAD_DIM
    proj = h @ w_q
    q = proj[..., :nq].reshape(B, T, NSA_HEADS, NSA_HEAD_DIM)
    gates = jax.nn.sigmoid(proj[..., nq:].astype(jnp.float32)).reshape(B, T, 3, NSA_HEADS)
    return attend(q, gates, ctx).astype(h.dtype) @ w_o

def setup_inputs(seed: int = 0) -> dict:
    key = jax.random.key(seed)
    ks = jax.random.split(key, 32)
    n_pages = PAST_LEN // PAGE_SIZE
    n_pool = (DEC_BATCH * n_pages * 5) // 4
    w_buf = min(WINDOW, PAST_LEN)
    G, dk = NSA_KV_GROUPS, NSA_HEAD_DIM
    hk, hv = HG_HEADS * HG_K, HG_HEADS * HG_V

    def nrm(k, shape, scale):
        return jax.random.normal(k, shape, jnp.float32) * scale

    return {
        "x_prompt": nrm(ks[0], (BATCH, SEQ, D_MODEL), 1.0),
        "x_sample": nrm(ks[1], (DEC_BATCH, DEC_SEQ, D_MODEL), 1.0),
        "cache_nsa_kv": nrm(ks[2], (n_pool, PAGE_SIZE, 4, G, dk), 1.0),
        "cache_win_kv": nrm(ks[3], (DEC_BATCH, w_buf, 2, G, dk), 1.0),
        "state_hgrn": nrm(ks[4], (N_A, DEC_BATCH, HG_HEADS, HG_K, HG_V), 0.5),
        "page_table": jax.random.permutation(ks[5], n_pool)[:DEC_BATCH * n_pages].reshape(DEC_BATCH, n_pages).astype(jnp.int32),
        "norm_mix": 1.0 + nrm(ks[6], (DEPTH, D_MODEL), 0.02),
        "norm_mlp": 1.0 + nrm(ks[7], (DEPTH, D_MODEL), 0.02),
        "w_mlp_up": nrm(ks[8], (DEPTH, D_MODEL, D_FF), D_MODEL ** -0.5),
        "w_mlp_down": nrm(ks[9], (DEPTH, D_FF, D_MODEL), D_FF ** -0.5),
        "w_hgrn_in": nrm(ks[10], (N_A, D_MODEL, 2 * hk + 2 * hv), D_MODEL ** -0.5),
        "hgrn_lb_logits": nrm(ks[11], (N_A, hk), 1.0),
        "hgrn_onorm": 1.0 + nrm(ks[12], (N_A, hv), 0.02),
        "w_hgrn_out": nrm(ks[13], (N_A, hv, D_MODEL), hv ** -0.5),
        "norm_kv": 1.0 + nrm(ks[14], (D_MODEL,), 0.02),
        "w_kv": nrm(ks[15], (D_MODEL, 6 * G * dk), D_MODEL ** -0.5),
        "cmp_pe_k": nrm(ks[16], (CMP_LEN, dk), 0.1),
        "cmp_w1_k": nrm(ks[17], (CMP_LEN * dk, CMP_HID), (CMP_LEN * dk) ** -0.5),
        "cmp_w2_k": nrm(ks[18], (CMP_HID, dk), CMP_HID ** -0.5),
        "cmp_pe_v": nrm(ks[19], (CMP_LEN, dk), 0.1),
        "cmp_w1_v": nrm(ks[20], (CMP_LEN * dk, CMP_HID), (CMP_LEN * dk) ** -0.5),
        "cmp_w2_v": nrm(ks[21], (CMP_HID, dk), CMP_HID ** -0.5),
        "w_nsa_q": nrm(ks[22], (N_B, D_MODEL, NSA_HEADS * dk + 3 * NSA_HEADS), D_MODEL ** -0.5),
        "w_nsa_out": nrm(ks[23], (N_B, NSA_HEADS * dk, D_MODEL), (NSA_HEADS * dk) ** -0.5),
        "norm_final": 1.0 + nrm(ks[24], (D_MODEL,), 0.02),
    }

def reference(x_prompt, x_sample, cache_nsa_kv, cache_win_kv, state_hgrn, page_table,
              norm_mix, norm_mlp, w_mlp_up, w_mlp_down,
              w_hgrn_in, hgrn_lb_logits, hgrn_onorm, w_hgrn_out,
              norm_kv, w_kv, cmp_pe_k, cmp_w1_k, cmp_w2_k, cmp_pe_v, cmp_w1_v, cmp_w2_v,
              w_nsa_q, w_nsa_out, norm_final):
    lbs = hgrn_lower_bounds(hgrn_lb_logits)
    G, dk = NSA_KV_GROUPS, NSA_HEAD_DIM

    def shared_kv(x):
        B, T, _ = x.shape
        return (rmsnorm(x, norm_kv) @ w_kv).reshape(B, T, 6, G, dk)

    def nsa_context(kv4):
        B, T = kv4.shape[:2]
        kc = compress(kv4[:, :, 0], cmp_pe_k, cmp_w1_k, cmp_w2_k)
        vc = compress(kv4[:, :, 1], cmp_pe_v, cmp_w1_v, cmp_w2_v)
        n_slc = -(-T // SLC_BLOCK)
        slc = jnp.pad(kv4[:, :, 2:4], ((0, 0), (0, n_slc * SLC_BLOCK - T), (0, 0), (0, 0), (0, 0)))
        slc = slc.reshape(B, n_slc, SLC_BLOCK, 2, G, dk).transpose(3, 0, 4, 1, 2, 5)
        ci = jnp.arange(kc.shape[1])[:, None] * CMP_STRIDE
        sj = jnp.arange(n_slc)[None, :] * SLC_BLOCK
        M = ((ci < sj + SLC_BLOCK) & (ci + CMP_LEN > sj)).astype(jnp.float32)
        return kc, vc, slc[0], slc[1], M

    def trunk(x, S_init, make_ctx, attend):
        new_S = []
        ctx = None
        new_kv = None
        for l in range(DEPTH):
            if l == N_A:
                ctx, new_kv = make_ctx(x)
            h = rmsnorm(x, norm_mix[l])
            if l < N_A:
                o, S = hgrn_mix(h, S_init[l], w_hgrn_in[l], lbs[l], hgrn_onorm[l], w_hgrn_out[l])
                new_S.append(S)
            else:
                o = nsa_mix(h, ctx, attend, w_nsa_q[l - N_A], w_nsa_out[l - N_A])
            x = x + o
            x = x + sq_relu_mlp(rmsnorm(x, norm_mlp[l]), w_mlp_up[l], w_mlp_down[l])
        return rmsnorm(x, norm_final), jnp.stack(new_S), new_kv

    def prompt_ctx(x):
        kv = shared_kv(x)
        pad = ((0, 0), (WINDOW, 0), (0, 0), (0, 0))
        kc, vc, ks_b, vs_b, M = nsa_context(kv[:, :, :4])
        ctx = (kc, vc, ks_b, vs_b, M, jnp.pad(kv[:, :, 4], pad), jnp.pad(kv[:, :, 5], pad))
        return ctx, (kv[:, :, :4], kv[:, -min(WINDOW, x.shape[1]):, 4:])

    def prompt_attend(q, gates, ctx):
        kc, vc, ks_b, vs_b, M, kw_pad, vw_pad = ctx
        B, T = q.shape[:2]
        nb = T // Q_BLOCK

        def to_blocks(a):
            return jnp.moveaxis(a.reshape(B, nb, Q_BLOCK, *a.shape[2:]), 1, 0)

        def one(args):
            qi, gi, s0 = args
            kw = lax.dynamic_slice_in_dim(kw_pad, s0, WINDOW + Q_BLOCK, axis=1)
            vw = lax.dynamic_slice_in_dim(vw_pad, s0, WINDOW + Q_BLOCK, axis=1)
            w_pos = s0 - WINDOW + jnp.arange(WINDOW + Q_BLOCK)
            t_pos = s0 + jnp.arange(Q_BLOCK)
            return nsa_attend(qi, gi, t_pos, kc, vc, ks_b, vs_b, M, kw, vw, w_pos)

        o = lax.map(one, (to_blocks(q), to_blocks(gates), jnp.arange(nb) * Q_BLOCK))
        return jnp.moveaxis(o, 0, 1).reshape(B, T, -1)

    past_len = page_table.shape[1] * cache_nsa_kv.shape[1]
    w_buf = cache_win_kv.shape[1]

    def sample_ctx(x):
        kv = shared_kv(x)
        B, T = x.shape[:2]
        past = cache_nsa_kv[page_table].reshape(B, past_len, 4, G, dk)
        full = jnp.concatenate([past, kv[:, :, :4].astype(past.dtype)], axis=1)
        win = jnp.concatenate([cache_win_kv, kv[:, :, 4:].astype(cache_win_kv.dtype)], axis=1)
        w_pos = jnp.concatenate([past_len - w_buf + jnp.arange(w_buf), past_len + jnp.arange(T)])
        kc, vc, ks_b, vs_b, M = nsa_context(full)
        ctx = (kc, vc, ks_b, vs_b, M, win[:, :, 0], win[:, :, 1], w_pos)
        return ctx, (kv[:, :, :4], win[:, -w_buf:])

    def sample_attend(q, gates, ctx):
        kc, vc, ks_b, vs_b, M, kw, vw, w_pos = ctx
        t_pos = past_len + jnp.arange(q.shape[1])
        return nsa_attend(q, gates, t_pos, kc, vc, ks_b, vs_b, M, kw, vw, w_pos)

    S0_prompt = jnp.zeros((N_A, x_prompt.shape[0], HG_HEADS, HG_K, HG_V), x_prompt.dtype)
    y_prompt, hgrn_state_prompt, (nsa_kv_prompt, win_kv_prompt) = trunk(x_prompt, S0_prompt, prompt_ctx, prompt_attend)
    y_sample, hgrn_state_sample, (nsa_kv_sample, win_kv_sample) = trunk(x_sample, state_hgrn, sample_ctx, sample_attend)
    return (y_prompt, y_sample, nsa_kv_prompt, nsa_kv_sample, win_kv_prompt, win_kv_sample, hgrn_state_prompt, hgrn_state_sample)


_drawn_inputs = setup_inputs


def setup_inputs(seed=0):
    import zlib

    import numpy as np

    out = dict(_drawn_inputs(seed))
    spreads = {}
    factors = {'hgrn_onorm': 4.943,
     'norm_kv': 23.405,
     'cmp_pe_k': 26.745,
     'cmp_pe_v': 25.208,
     'norm_final': 23.068,
     'cache_nsa_kv': 4.361,
     'norm_mlp': 4.321}
    for name, (base, spread) in spreads.items():
        noise = np.random.default_rng([zlib.crc32(name.encode()), seed]).standard_normal(out[name].shape)
        drawn = base * np.exp(spread * noise) if base else spread * noise
        out[name] = __import__('jax').numpy.asarray(drawn.astype(out[name].dtype))
    for name, factor in factors.items():
        out[name] = (out[name] * factor).astype(out[name].dtype)
    return out
```

```python
from contextlib import ExitStack, contextmanager

import concourse.bass as bass
from concourse import mybir

F32 = mybir.dt.float32
I32 = mybir.dt.int32
ALU = mybir.AluOpType
ACT = mybir.ActivationFunctionType
AX = mybir.AxisListType
ds = bass.ds

P = 128
EPS = 1e-6
NEG_INF = -1e30
TINY = 1e-30
FORCED_SCORE = 1e4


class Chain:

    def __init__(self, eng, sem):
        self.eng, self.sem, self.n, self.turn = eng, sem, 0, 0

    def add(self, ins):
        ins.then_inc(self.sem, 1)
        self.n += 1

    def settle(self):
        self.eng.wait_ge(self.sem, self.turn + self.n)

    def link(self, ins):
        self.add(ins)
        self.settle()

    @contextmanager
    def loop(self, turns, steps):
        start = self.n
        with self.eng.Fori(0, turns) as i:
            self.turn = i * steps
            yield i
        assert self.n - start == steps, (self.n - start, steps)
        self.turn, self.n = 0, start + steps * turns


def hybrid_step(nc, ins, outs):
    x_prompt, x_sample = ins["x_prompt"], ins["x_sample"]
    T = x_prompt.shape[1]
    B = x_sample.shape[0]
    D = x_prompt.shape[2]
    KD = D // P
    N = T + B
    NH = N // 2
    TT = T // P
    heads = ins["state_hgrn"].shape[2]
    FF = ins["w_mlp_up"].shape[2]
    KF = FF // P
    assert heads == KD and N % 2 == 0
    G, DK = ins["w_kv"].shape[1] // 6 // 64, 64
    HEADS = D // DK
    HPG = HEADS // G
    GD = G * DK
    SCALE = DK ** -0.5
    SUB = 16
    PAGE = ins["cache_nsa_kv"].shape[1]
    PAGES = ins["page_table"].shape[1]
    PAST = PAGES * PAGE
    HT = 8
    HALF = P * HT
    NB_P, NB_S = T // SUB - 1, PAST // SUB - 1
    NSLC = PAST // 64 + 1
    assert T // 64 <= 16 and T <= ins["cache_win_kv"].shape[1] and PAST == 2 * HALF

    ctx = ExitStack()
    with ctx:
        def sb(name, shape, dt=F32):
            return ctx.enter_context(nc.sbuf_tensor(name, shape, dt))

        def sem(name):
            return ctx.enter_context(nc.semaphore(name))

        x = sb("x", [P, KD, N])
        h = sb("h", [P, KD, N])
        big = sb("big", [P, 4 * KD, N])
        stream = sb("stream", [P, 4, 8 * 512])
        scratch = sb("scratch", [P, 8736])
        ident = sb("ident", [P, P])
        ones = sb("ones", [P, P])
        eps = sb("eps", [P, 1])
        vec = sb("vec", [P, 64])
        lnb = sb("lnb", [P, 4, KD])
        rstd = sb("rstd", [P, N])
        ps = ctx.enter_context(nc.psum_tensor("ps", [P, 8, 512], F32))

        GAIN_MIX, GAIN_MLP, GAIN_KV, GAIN_FINAL, GAIN_O, LOGITS = 0, 16, 32, 40, 48, 56

        slot = [stream[:, s, :] for s in range(4)]

        def halves(ap):
            return ap.rearrange("p (a t) -> p a t", a=2)

        def pair(c):
            return ps[:, 2 * (c % 2):2 * (c % 2) + 2, 0:NH]

        def row(buf, k):
            return buf[:, ds(k, 1), :].rearrange("p a t -> p (a t)")

        at = [0]

        def cut(n, *shape):
            a = scratch[:, at[0]:at[0] + n]
            at[0] += n
            assert at[0] <= 8736, at[0]
            if len(shape) == 2:
                return a.rearrange("p (a b) -> p a b", a=shape[0])
            return a

        reset = cut(T)
        masks = cut(8 * P, 8, P)
        Fb = cut(N)
        Kb = cut(N)
        Bc = cut(T)
        EB = cut(T)
        Dr = [cut(T) for _ in range(2)]
        Lv = [cut(T) for _ in range(2)]
        AT = cut(T)
        Vs = cut(T)
        vtok = cut(T)
        ktok = cut(T)
        kd = cut(T)
        qd = cut(T)
        at_end = at[0]
        at[0] = at_end - 5 * T
        Mz = [cut(N), cut(N)]
        Nz = [cut(N), cut(N)]
        at[0] = at_end
        St = sb("St", [P, TT, P])
        Er = [slot[2][:, 1024 + T * i:1024 + T * i + T] for i in range(2)]

        Eend, Dend = (slot[2][:, 2048 + T * i:2048 + T * i + T] for i in range(2))
        S0 = [slot[2 + p][:, 0:B * P].rearrange("p (b v) -> p b v", b=B) for p in range(2)]
        small = slot[3]
        Fs, Ks, Vs8, Q8 = (small[:, 1024 + 16 * i:1032 + 16 * i] for i in range(4))
        Ktok8 = small[0:B, 1200:1200 + P]
        Vsel = small[0:B, 1400:1400 + B * P].rearrange("p (b v) -> p b v", b=B)

        KVT = big[:, 0:12, :]
        QT = big[:, 12:20, :]
        h2 = big[:, 20:28, :]
        kvtok = big[:, 20:32, :].rearrange("p k t -> p (k t)")[:, 0:TT * 6 * GD].rearrange("p (a n) -> p a n", a=TT)
        W1 = [big[:, 2 * i:2 * i + 2, :].rearrange("p k t -> p (k t)")[:, 0:8 * P].rearrange("p (k a n) -> p k a n", k=8, a=2)
              for i in range(2)]
        KD2 = slot[2].rearrange("p (g b t) -> p g b t", g=G, b=2)
        psrc = slot[3][0:T // HT, :].rearrange("p (r n) -> p r n", r=HT)
        at[0] = 0
        W2 = [cut(DK)[0:DK, :] for _ in range(2)]
        pe_rows, pe_cols, cbias = cut(2 * P, 2, P), cut(2 * 16, 2, 16), cut(2)
        gT = cut(N)[0:3 * HEADS, :]
        kvs = cut(6 * GD)[0:B, :]
        TK = [cut(512) for _ in range(2)]
        RG = [cut(512, G, P) for _ in range(2)]
        At = cut(2 * G * P)[0:DK, :].rearrange("p (a s) -> p a s", s=P)
        Bt = cut(2 * G * P)[0:DK, :].rearrange("p (a s) -> p a s", s=P)
        QP = cut(B * 2 * HEADS).rearrange("p (b a h) -> p b a h", b=B, a=2)
        QZ = cut(B * G * HEADS)[0:DK, :].rearrange("p (b g h) -> p b g h", b=B, g=G)
        GS = cut(3 * B)[0:HEADS, :].rearrange("p (r b) -> p r b", r=3)
        KN = cut(2 * B, 2, B)
        kcT = cut(G * NB_P, G, NB_P)
        Vc = cut(GD)[0:NB_P, :]
        diag = cut(P)
        cm_add, cm_one = cut(TT * NB_P, TT, NB_P), cut(TT * NB_P, TT, NB_P)
        gtok = cut(TT * 3 * HEADS, TT, 3 * HEADS)
        PcT = TK[0][0:NB_P, :]
        kcg = cut(NB_P)
        gg = cut(TT * 3 * HPG).rearrange("p (a r j) -> p a r j", a=TT, r=3)
        Vc_g = cut(DK)[0:NB_P, :]
        nmax = [cut(2) for _ in range(2)]
        sums = cut(2 * HPG, 2, HPG)
        csum, cmx = cut(HPG), cut(HPG)
        wts = cut(3 * HPG, 3, HPG)
        free_b = big[:, 4:12, :].rearrange("p k t -> p (k t)")
        Pb = [free_b[:, 1024 * i:1024 * i + 1024].rearrange("p (b s) -> p b s", b=2) for i in range(2)]
        PT = [free_b[:, 2048:3072].rearrange("p (b s t) -> p b s t", b=2, s=TT),
              slot[3][:, 1024:2048].rearrange("p (b s t) -> p b s t", b=2, s=TT)]
        Kg = free_b[:, 3072:4096].rearrange("p (b s) -> p b s", b=2)
        qg = slot[3][:, 0:1024].rearrange("p (c t) -> p c t", c=2)
        Vg = slot[3][:, 2048:2560].rearrange("p (a b d) -> p a b d", a=TT, b=2)
        mix = slot[3][:, 2560:3328].rearrange("p (r j d) -> p r j d", r=3, j=HPG)
        otok = slot[3][:, 3328:3584].rearrange("p (j d) -> p j d", j=HPG)
        Scm = [slot[3][:, 3584 + 128 * i:3584 + 128 * i + HPG * NB_P].rearrange("p (j s) -> p j s", j=HPG)
               for i in range(2)]
        Zp = slot[3][0:DK, 0:2 * G * NB_P].rearrange("p (a s) -> p a s", s=NB_P)
        Hp = slot[3][0:DK, 1024:1024 + 2 * G * NB_P].rearrange("p (a s) -> p a s", s=NB_P)
        free_s = big[:, 4:32, :].rearrange("p k t -> p (k t)")
        sat = [0]

        def cut_s(n):
            sat[0] += n
            assert sat[0] <= 28 * N
            return free_s[:, sat[0] - n:sat[0]]

        NK = PAST + 1
        S = cut_s(NK + 7)[0:HEADS, :]
        Sw = cut_s(512)[0:HEADS, :]
        Wt = cut_s(4 * 512).rearrange("p (j n) -> p j n", j=4)
        Zs = cut_s(2 * G * NB_S)[0:DK, :].rearrange("p (a s) -> p a s", s=NB_S)
        Hs = cut_s(2 * G * NB_S)[0:DK, :].rearrange("p (a s) -> p a s", s=NB_S)
        kcS = cut_s(G * NB_S)[0:DK, :].rearrange("p (g s) -> p g s", g=G)
        VcS = cut_s(GD)[0:NB_S, :]
        PTs = cut_s(22 * HEADS)
        PnT = cut_s(HEADS)[0:NB_S, :]
        Pc = cut_s(P)[0:HEADS, :]
        Qp, Qz = cut_s(2 * HEADS).rearrange("p (a h) -> p a h", a=2), cut_s(G * HEADS)[0:DK, :].rearrange("p (g h) -> p g h", g=G)
        Kn, Vn = cut_s(2), cut_s(GD)[0:1, :]
        Msel, Gsel = cut_s(NSLC)[0:NB_S, :], cut_s(HEADS)[0:HEADS, :]
        U, score, score2, madd = (cut_s(NSLC)[0:HEADS, :] for _ in range(4))
        top = [cut_s(8)[0:HEADS, :] for _ in range(2)]
        smax, ssum, sw = (cut_s(4)[0:HEADS, :] for _ in range(3))
        Dg = cut_s(3 * HEADS)[0:HEADS, :].rearrange("p (r h) -> p r h", r=3)
        OS = cut_s(B * 2 * HEADS).rearrange("p (b a h) -> p b a h", b=B, a=2)

        x_in, xs_in, vec_in = sem("x_in"), sem("xs_in"), sem("vec_in")
        const_ready = sem("const_ready")
        turned, turn_taken = sem("turned"), sem("turn_taken")
        lb_done = sem("lb_done")
        slab_in = [sem(f"slab_in{s}") for s in range(4)]
        chunk_ready = sem("chunk_ready")
        chunk_taken = [sem(f"chunk_taken{s}") for s in range(2)]
        pool_chain, act_chain, dve_chain = sem("pool_chain"), sem("act_chain"), sem("dve_chain")
        stored = sem("stored")
        relu_done = sem("relu_done")
        relu_base = {"up0": 0, "up1": KF}

        norm = {k: sem("norm_" + k) for k in ("sq_dve", "sq_act", "sum", "sqrt", "out")}
        turn_of = {name: n for n, name in enumerate(("mix0", "mlp0", "attn", "mlp1", "final"))}
        out_count = {"mix0": KD, "mlp0": 2 * KD, "attn": 4 * KD, "mlp1": 5 * KD, "final": 6 * KD}

        fz_ready, fe_ready = sem("fz_ready"), sem("fe_ready")
        gz_ready, ge_ready = sem("gz_ready"), sem("ge_ready")
        hg = {k: sem("hg_" + k) for k in (
            "scan", "f", "vs", "k", "d", "e", "dend", "eend", "eb", "kd", "lv", "vt", "kt", "vtok", "ktok",
            "prod", "prod_taken", "u", "s", "at", "o", "o_taken", "qd", "s_stored", "take")}
        hs = {k: sem("hs_" + k) for k in (
            "f", "kv", "turned", "tok", "outer", "state", "o", "o_taken", "s_in0", "s_in1", "s_out0", "s_out1")}
        on = {k: sem("on_" + k) for k in ("sq", "sum", "sqrt", "out")}

        passed = sem("passed")

        def hold(eng, s, value):
            eng.wait_ge(s, value)
            eng.sem_inc(passed, 1)

        kt_ready = sem("kt_ready")
        kt_taken = [sem("kt_taken0"), sem("kt_taken1")]
        gate_ready, gate_done, gturned, gtaken = sem("gate_ready"), sem("gate_done"), sem("gturned"), sem("gtaken")
        kvs_turned, kvs_ready, kv_stored, kvs_stored = (sem(n) for n in ("kvs_turned", "kvs_ready", "kv_stored", "kvs_stored"))
        w1_in, small_in, psrc_in = sem("w1_in"), sem("small_in"), sem("psrc_in")
        attn_const, kd_ready = sem("attn_const"), sem("kd_ready")
        pc = {k: sem("pc_" + k) for k in ("rg", "pe_turned", "pe_cols", "bias_ready", "bias", "turned", "ev0", "ev1", "mul",
                                          "ab_a", "ab_b", "z", "tanh", "h", "kc", "kc_taken", "vc_taken")}
        pa = {k: sem("pa_" + k) for k in ("ce", "k", "q", "cs", "cmax", "cexp", "csum", "s", "max", "p", "ts", "tw", "es", "ew",
                                          "o", "ct", "ect", "oc", "mixed", "ot", "h")}
        ends = [(hg[k], 7 * heads + 1) for k in ("d", "e", "lv")] + [(hg["prod"], 8 * heads + 1), (hg["s"], 4 * heads + 1),
               (hg["prod_taken"], 8 * heads + 4)]
        ends += [(hg[k], heads + 1) for k in ("scan", "f", "vs", "k", "dend", "eend", "eb", "kd", "vt", "kt", "vtok",
                                              "ktok", "u", "at", "o", "o_taken", "qd")]
        ends += [(hs[k], heads + 1) for k in ("f", "kv", "turned", "tok", "outer", "state", "o", "o_taken")]
        ends.append((sem("os_done"), 0))
        sa, past = {"rg": sem("sa_rg")}, {}
        for (s_, end), k in zip(ends, (
                "own", "turned", "ev0", "ev1", "mul", "ab_a", "ab_b", "z", "tanh", "h", "kc", "kc_taken", "vc_taken", "cs", "cmax", "cexp", "pn", "pnt", "pnt_taken", "u", "u_taken", "imp", "smax", "sexp", "wmax", "wexp", "new", "dg", "pt", "pt_taken", "o", "os"), strict=True):
            sa[k], past[k] = s_, end - (k != "os")
        cmp_in = [sem("cmp_in0"), sem("cmp_in1")]
        slc_in = [sem("slc_in0"), sem("slc_in1")]
        win_in, own_in, vn_in, pt_in = sem("win_in"), sem("own_in"), sem("vn_in"), sem("pt_in")
        pages_in = sem("pages_in")

        def start_counts(eng, sems, names):
            for name in names:
                eng.sem_inc(sems[name], 1)

        block = ctx.enter_context(nc.Block())

        hready = sem("hready")
        ydone, ysdone = [sem("ydone0"), sem("ydone1")], sem("ysdone")
        yturned = sem("yturned")
        yrows = big[:, 0:8, :].rearrange("p k t -> p (k t)")[:, 0:TT * D].rearrange("p (a n) -> p a n", a=TT)
        ysrows = big[0:B, 8:10, :].rearrange("p k t -> p (k t)")[:, 0:D]
        pages = sb("pages", [1, B * PAGES], I32)
        def cslot(kind, half):
            return slot[2 * kind + half].rearrange("p (r n) -> p r n", r=HT)

        slabs = []
        chunk_base, slab_base = {}, {}
        chunks = [0]

        def plan(name, w, cols, k_rows, first=0, order=None):
            slab_base[name], chunk_base[name] = len(slabs), chunks[0]
            n = -(-w.shape[1] // cols) if order is None else len(order)
            for s in (range(n) if order is None else order):
                c0, c1 = s * cols, min((s + 1) * cols, w.shape[1])
                src = w[:, c0:c1].rearrange("(k p) n -> p k n", p=P)
                chunks[0] += -(-(c1 - c0) // P)
                slabs.append((src, k_rows, c1 - c0, chunks[0]))

        plan("in", ins["w_hgrn_in"][0], 512, KD, order=(2, 3, 6, 7, 0, 1, 4, 5))
        plan("out", ins["w_hgrn_out"][0], 512, KD)
        plan("up0", ins["w_mlp_up"][0], 512, KD)
        plan("down0", ins["w_mlp_down"][0], P, KF)
        wq = ins["w_nsa_q"][0]
        plan("kv", ins["w_kv"], 512, KD)
        plan("gate", wq[:, D:D + 3 * HEADS], 3 * HEADS, KD)
        plan("q", wq[:, 0:D], 512, KD)
        plan("nsa_out", ins["w_nsa_out"][0], 512, KD)
        plan("up1", ins["w_mlp_up"][1], 512, KD)
        plan("down1", ins["w_mlp_down"][1], P, KF)

        def taken(p, n):
            return (n + 1 - p) // 2 + 1

        def slab_slot(j):
            return j % 2

        def slab_count(j):
            return 16 * (j // 2 + 1)

        state = ins["state_hgrn"]
        y_prompt, y_sample, kv_prompt, kv_sample, win_prompt, win_sample, state_prompt, state_sample = outs

        @block.sync
        def _(sp):
            sp.dma_start(big[:, 0:8, :].rearrange("p k t -> p (k t)")[:, 0:TT * D].rearrange("p (a n) -> p a n", a=TT),
                         x_prompt[0].rearrange("(a p) n -> p a n", p=P)).then_inc(x_in, 16)
            sp.dma_start(big[0:B, 8:10, :].rearrange("p k t -> p (k t)")[:, 0:D],
                         x_sample.rearrange("b a n -> (b a) n")).then_inc(xs_in, 16)
            for r, src in ((GAIN_MIX, ins["norm_mix"]), (GAIN_MLP, ins["norm_mlp"])):
                sp.dma_start(big[r:r + 16, 10, 0:P], src.rearrange("l (k n) -> (l k) n", n=P)).then_inc(vec_in, 16)
            for r, src in ((GAIN_KV, ins["norm_kv"]), (GAIN_FINAL, ins["norm_final"]),
                           (GAIN_O, ins["hgrn_onorm"][0]), (LOGITS, ins["hgrn_lb_logits"][0])):
                sp.dma_start(big[r:r + 8, 10, 0:P], src.rearrange("(k n) -> k n", n=P)).then_inc(vec_in, 16)

            def load_slabs(first, last):
                for j in range(first, last):
                    src, k_rows, cols, _ = slabs[j]
                    if j >= 2:
                        sp.wait_ge(chunk_ready, slabs[j - 2][3])
                    dst = slot[slab_slot(j)][:, 0:k_rows * cols].rearrange("p (k n) -> p k n", k=k_rows)
                    sp.dma_start(dst, src).then_inc(slab_in[slab_slot(j)], 16)

            load_slabs(0, slab_base["out"] + 2)
            with sp.Fori(0, heads) as i:
                at_h = sp.snap(i)
                sp.wait_ge(hg["s"], 4 * at_h + 4 + 1)
                sp.dma_start(state_prompt[0, 0, ds(at_h, 1), :, :].rearrange("a k v -> k (a v)"),
                             St[:, TT - 1, :]).then_inc(hg["s_stored"], 16)
            for g in range(heads + 2):
                if g >= 2:
                    sp.wait_ge(hs["state"], g )
                    sp.dma_start(state_sample[0, :, g - 2, :, :].rearrange("b k v -> k b v"), S0[g % 2])\
                      .then_inc(hs[f"s_out{g % 2}"], 16)
                if g < heads:
                    if g >= 2:
                        sp.wait_ge(hs["o"], g )
                        sp.wait_ge(hs[f"s_out{g % 2}"], 16 * (g // 2) + 16)
                    sp.dma_start(S0[g % 2], state[0, :, g, :, :].rearrange("b k v -> k b v"))\
                      .then_inc(hs[f"s_in{g % 2}"], 16)
            sp.wait_ge(hg["s_stored"], 16 * heads + 16)
            load_slabs(slab_base["out"] + 2, slab_base["nsa_out"])
            cache_win = ins["cache_win_kv"]
            W = cache_win.shape[1]
            for b in range(B):
                sp.dma_start(win_sample[b].rearrange("w c g d -> (w c g d)")[0:(W - 1) * 2 * GD].rearrange("(a n) -> a n", a=16),
                             cache_win[b].rearrange("w c g d -> (w c g d)")[2 * GD:W * 2 * GD].rearrange("(a n) -> a n", a=16))\
                  .then_inc(stored, 16)
            sp.dma_start(pages[:], ins["page_table"].rearrange("b n -> (b n)").rearrange("(a n) -> a n", a=1))\
              .then_inc(pages_in, 16)
            sp.wait_ge(kt_taken[0], 6)
            sp.wait_ge(kt_taken[1], 6)
            sp.dma_start(kv_prompt[0].rearrange("(a p) c g d -> p a (c g d)", p=P), kvtok[:, :, 0:4 * GD])\
              .then_inc(kv_stored, 16)
            sp.dma_start(win_prompt[0].rearrange("(a p) c g d -> p a (c g d)", p=P), kvtok[:, :, 4 * GD:6 * GD])\
              .then_inc(stored, 16)
            sp.wait_ge(kvs_ready, 1)
            for i, name in enumerate("kv"):
                for a in range(2):
                    sp.dma_start(W1[i][:, :, a, :], ins["cmp_w1_" + name][a * 1024:a * 1024 + 1024, :]
                                 .rearrange("(k p) n -> p k n", p=P)).then_inc(w1_in, 16)
                sp.dma_start(W2[i], ins["cmp_w2_" + name]).then_inc(small_in, 16)
                sp.dma_start(pe_rows[0:16, i, :], ins["cmp_pe_" + name].rearrange("(k r) d -> k (r d)", r=2))\
                  .then_inc(small_in, 16)
            sp.dma_start(kv_sample.rearrange("b a c g d -> (b a) (c g d)"), kvs[:, 0:4 * GD]).then_inc(kvs_stored, 16)
            sp.dma_start(win_sample[:, W - 1, :, :, :].rearrange("b c g d -> b (c g d)"), kvs[:, 4 * GD:6 * GD])\
              .then_inc(kvs_stored, 16)
            sp.wait_ge(kv_stored, 16)
            sp.dma_start(psrc, kv_prompt[0, :, 0:2, :, :].rearrange("(i r) c g d -> i r (c g d)", r=HT))\
              .then_inc(psrc_in, 16)
            sp.wait_ge(pages_in, 16)
            sp.wait_ge(kvs_stored, 32)
            if True:
                sp.wait_ge(chunk_ready, slabs[slab_base["nsa_out"] - 1][3])
            pool_kv = ins["cache_nsa_kv"]
            with sp.Fori(0, B) as b:
                for kind in range(2):
                    for half in range(2):
                        if kind == 0:
                            if half == 0:
                                sp.wait_ge(pc["rg"], 8)
                            hold(sp, sa["rg"], b * 16 + 1)
                        else:
                            hold(sp, sa["os"], b + 1 + past["os"])
                        dst = cslot(kind, half)
                        for k in range(PAGES // 2):
                            page = sp.value_load(pages[0:1, ds(b * PAGES + half * (PAGES // 2) + k, 1)],
                                                 min_val=0, max_val=pool_kv.shape[0] - 1)
                            sp.dma_start(dst[16 * k:16 * k + 16, :, :],
                                         pool_kv[ds(page, 1), :, 2 * kind:2 * kind + 2, :, :]
                                         .rearrange("a (i r) c g d -> (a i) r (c g d)", r=HT))\
                              .then_inc((cmp_in, slc_in)[kind][half], 16)
                hold(sp, sa["os"], b + 1 + past["os"])
                sp.dma_start(Vn, kv_sample[ds(b, 1), 0, 3, :, :].rearrange("b g d -> b (g d)")).then_inc(vn_in, 16)
                sp.dma_start(Wt, cache_win[ds(b, 1)].rearrange("a (p j) c g d -> (a p) j (c g d)", j=4)).then_inc(win_in, 16)
                hold(sp, win_in, b * 16 + 16)
                sp.dma_start(Wt[0:1, 0, :], win_sample[ds(b, 1), W - 1, :, :, :].rearrange("a c g d -> a (c g d)"))\
                  .then_inc(own_in, 16)
            sp.wait_ge(sa["rg"], B * 16 + 1)
            load_slabs(slab_base["nsa_out"], len(slabs))
            sp.wait_ge(ydone[0], TT)
            sp.wait_ge(ydone[1], TT)
            sp.dma_start(y_prompt[0].rearrange("(a p) n -> p a n", p=P), yrows).then_inc(stored, 16)
            sp.wait_ge(ysdone, 1)
            sp.dma_start(y_sample.rearrange("b a n -> (b a) n"), ysrows).then_inc(stored, 16)
            for p in range(2):
                sp.wait_ge(hs[f"s_out{p}"], 16 * heads // 2 + 16)
            sp.wait_ge(stored, 16 * (B + 3))

        @block.gpsimd
        def _(pool):
            ch = Chain(pool, pool_chain)
            start_counts(pool, hg, ("kd", "lv", "qd"))
            start_counts(pool, sa, ("rg",))
            ch.add(nc.gpsimd.memset(ident[:], 0.0))
            ch.add(nc.gpsimd.memset(eps[:], EPS))
            ch.add(nc.gpsimd.memset(masks, 1.0))
            ch.add(nc.gpsimd.memset(AT, 0.0))
            ch.add(nc.gpsimd.memset(reset, 1.0))
            ch.add(nc.gpsimd.memset(ones[:], 1.0))
            ch.settle()
            ch.add(nc.gpsimd.affine_select(out=ident[:], in_=ident[:], compare_op=ALU.not_equal, fill=1.0, base=0,
                                           pattern=[[-1, P]], channel_multiplier=1))
            ch.add(nc.gpsimd.memset(reset.rearrange("p (c t) -> p c t", c=TT)[:, :, 0:1], 0.0))
            for l in range(7):
                m = 64 >> l
                v = masks[:, l, :].rearrange("p (j u) -> p j u", u=2 * m)
                nb = P // (2 * m)
                for base, pat, mul in ((0, [[-2 * m, nb], [0, 2 * m]], 1),
                                       (m - 1, [[2 * m, nb], [0, 2 * m]], -1),
                                       (-m, [[0, nb], [1, 2 * m]], 0)):
                    ch.link(nc.gpsimd.affine_select(out=v, in_=v, compare_op=ALU.is_ge, fill=0.0, base=base,
                                                    pattern=pat, channel_multiplier=mul))
            ch.add(nc.gpsimd.affine_select(out=masks[:, 7, :], in_=masks[:, 7, :], compare_op=ALU.is_equal, fill=0.0,
                                           base=0, pattern=[[-1, P]], channel_multiplier=1))
            ch.settle()
            pool.sem_inc(const_ready, 1)

            with pool.Fori(0, heads) as i:
                q = row(big, i)[:, 0:T]
                pool.wait_ge(hg["k"], i + 2)
                pool.wait_ge(hg["eend"], i + 2)
                pool.wait_ge(hg["kt"], i + 1)
                nc.gpsimd.tensor_tensor(kd, Kb[:, 0:T], Eend, ALU.mult).then_inc(hg["kd"], 1)
                pool.wait_ge(hg["eb"], i + 2)
                pool.wait_ge(hg["o"], i + 1)
                nc.gpsimd.tensor_tensor(qd, q, EB, ALU.mult).then_inc(hg["qd"], 1)
                for l in range(7):
                    m = 64 >> l
                    ev = Er[l % 2].rearrange("p (j a u) -> p j a u", a=2, u=m)
                    lv = Lv[l % 2].rearrange("p (j a u) -> p j a u", a=2, u=m)
                    kv = Kb[:, 0:T].rearrange("p (j a u) -> p j a u", a=2, u=m)
                    qv = q.rearrange("p (j a u) -> p j a u", a=2, u=m)
                    pool.wait_ge(hg["e"], i * 7 + l + 2)
                    pool.wait_ge(hg["prod"], i * 8 + (l if l >= 2 else 0) + 1)
                    nc.gpsimd.tensor_tensor(lv[:, :, 0, :], kv[:, :, 0, :], ev[:, :, 0, :], ALU.mult)
                    nc.gpsimd.tensor_tensor(lv[:, :, 1, :], qv[:, :, 1, :], ev[:, :, 1, :], ALU.mult)\
                        .then_inc(hg["lv"], 1)

            pool.wait_ge(norm["out"], out_count["attn"])
            ch.add(nc.gpsimd.memset(diag, 0.0))
            ch.add(nc.gpsimd.memset(cm_one, 1.0))
            ch.add(nc.gpsimd.memset(cm_add, 0.0))
            ch.add(nc.gpsimd.memset(QP[:], 0.0))
            ch.add(nc.gpsimd.memset(QZ[:], 0.0))
            ch.settle()
            ch.add(nc.gpsimd.affine_select(out=diag, in_=diag, compare_op=ALU.is_ge, fill=NEG_INF, base=0,
                                           pattern=[[-1, P]], channel_multiplier=1))
            for m, fill in ((cm_one, 0.0), (cm_add, NEG_INF)):
                ch.add(nc.gpsimd.affine_select(out=m, in_=m, compare_op=ALU.is_ge, fill=fill, base=-(2 * SUB - 1),
                                               pattern=[[P, TT], [-SUB, NB_P]], channel_multiplier=1))
            ch.settle()
            pool.sem_inc(attn_const, 1)
            def regroup(src, n, kv, rp, out):
                return nc.gpsimd.tensor_copy(
                    out[0:n].rearrange("p g (r d) -> p g r d", r=2),
                    src[0:n, 2 * rp:2 * rp + 2, kv * GD:kv * GD + GD].rearrange("p r (g d) -> p g r d", g=G))

            pool.wait_ge(psrc_in, 16)
            for u in range(8):
                if u >= 2:
                    pool.wait_ge(pc["turned"], u - 1)
                regroup(psrc, T // HT, u // 4, u % 4, RG[u % 2]).then_inc(pc["rg"], 1)
            pool.wait_ge(pc["kc_taken"], 1)
            pool.wait_ge(pc["vc_taken"], 1)
            pool.wait_ge(kd_ready, 3)
            with pool.Fori(0, G) as g:
                hold(pool, pa["o"], g * 16 + 1)
                nc.gpsimd.tensor_copy(Kg, KD2[:, ds(g, 1), :, :].rearrange("p a b t -> p (a b) t"))
                for br, f in enumerate((3 * GD, 5 * GD)):
                    nc.gpsimd.tensor_copy(Vg[:, :, br, :], kvtok[:, :, ds(g * DK + f, DK)])
                nc.gpsimd.tensor_copy(kcg, kcT[:, ds(g, 1), :].rearrange("p a s -> p (a s)")).then_inc(pa["k"], 1)
            pool.wait_ge(pa["h"], G * TT + 1)
            ch.add(nc.gpsimd.memset(Msel, 1.0))
            ch.add(nc.gpsimd.memset(Gsel, 1.0))
            ch.settle()
            ch.link(nc.gpsimd.affine_select(out=Msel, in_=Msel, compare_op=ALU.is_ge, fill=0.0, base=1,
                                            pattern=[[-4, NSLC]], channel_multiplier=1))
            ch.add(nc.gpsimd.affine_select(out=Msel, in_=Msel, compare_op=ALU.is_ge, fill=0.0, base=3,
                                           pattern=[[4, NSLC]], channel_multiplier=-1))
            gv = Gsel.rearrange("p (g j) -> p g j", g=G)
            ch.link(nc.gpsimd.affine_select(out=gv, in_=gv, compare_op=ALU.is_ge, fill=0.0, base=0,
                                            pattern=[[-HPG, G], [0, HPG]], channel_multiplier=1))
            ch.add(nc.gpsimd.affine_select(out=gv, in_=gv, compare_op=ALU.is_ge, fill=0.0, base=HPG - 1,
                                           pattern=[[HPG, G], [0, HPG]], channel_multiplier=-1))
            ch.settle()
            pool.sem_inc(attn_const, 1)
            with pool.Fori(0, B) as b:
                for u in range(16):
                    if u % 8 == 0:
                        pool.wait_ge(cmp_in[u // 8], b * 16 * (PAGES // 2) + 16 * (PAGES // 2))
                    hold(pool, sa["turned"], b * 26 + (u if u >= 2 else u - 10) + past["turned"])
                    regroup(cslot(0, u // 8), P, u % 8 // 4, u % 4, RG[u % 2]).then_inc(sa["rg"], 1)

        @block.tensor
        def _(pe):
            start_counts(pe, hg, ("vt", "kt", "prod", "u", "o"))
            start_counts(pe, hs, ("turned", "outer", "o"))
            pe.wait_ge(const_ready, 1)
            pe.wait_ge(vec_in, 16 * 6)
            nc.tensor.transpose(ps[:, 7, 0:64], big[0:64, 10, 0:P], ident[0:64, 0:64]).then_inc(turned, 1)
            pe.wait_ge(xs_in, 16)
            xs_rows = big[0:B, 8:10, :].rearrange("p k t -> p (k t)")
            for k in range(KD):
                m = nc.tensor.transpose(ps[:, 6, B * k:B * k + B], xs_rows[:, P * k:P * k + P], ident[0:B, 0:B])
            m.then_inc(turned, 1)
            pe.wait_ge(x_in, 16)
            x_rows = big[:, 0:8, :].rearrange("p k t -> p (k t)")[:, 0:TT * D].rearrange("p (a n) -> p a n", a=TT)
            for k in range(KD):
                if k >= 4:
                    pe.wait_ge(turn_taken, 2 + k - 3)
                for a in range(TT):
                    m = nc.tensor.transpose(ps[:, k % 4, P * a:P * a + P], x_rows[:, a, P * k:P * k + P], ident[:])
                m.then_inc(turned, 1)

            def norm_sum(name, sq):
                n = turn_of[name]
                for k in range(KD):
                    pe.wait_ge(norm["sq_dve" if k % 2 == 0 else "sq_act"], n * KD // 2 + k // 2 + 1)
                    for a in range(2):
                        m = nc.tensor.matmul(ps[:, 6 + a, 0:NH], ones[:], sq[:, k, NH * a:NH * a + NH],
                                             start=(k == 0), stop=(k == KD - 1))
                m.then_inc(norm["sum"], 1)

            def chunk_products(slab, cols, k_rows, rhs, c_local, c, c_turn, wait_turn):
                pe.wait_ge(chunk_taken[c % 2], wait_turn + c // 2 + 1)
                w = slab[:, 0:k_rows * cols].rearrange("p (k n) -> p k n", k=k_rows)
                n1 = min(P, cols - P * c_local)
                for a in range(2):
                    for k in range(k_rows):
                        m = nc.tensor.matmul(pair(c)[0:n1, a, :], w[:, k, P * c_local:P * c_local + n1],
                                             rhs[:, k, NH * a:NH * a + NH], start=(k == 0), stop=(k == k_rows - 1))
                m.then_inc(chunk_ready, 1)

            def dense(name, count, rhs, k_rows, cols, turns=1):
                per = count // turns
                c_slab = -(-cols // P)
                c_per = c_slab * per

                def body(i):
                    for s in range(per):
                        j = slab_base[name] + s
                        got = slab_count(j)
                        pe.wait_ge(slab_in[slab_slot(j)], got if i is None else i * (16 * per // 2) + got)
                        for n in range(c_slab):
                            c = chunk_base[name] + s * c_slab + n
                            chunk_products(slot[slab_slot(j)], cols, k_rows, rhs, n, c, None,
                                           0 if i is None else i * (c_per // 2))
                if turns == 1:
                    body(None)
                else:
                    assert per % 2 == 0 and c_per % 2 == 0
                    with pe.Fori(0, turns) as i:
                        body(i)

            norm_sum("mix0", h)
            pe.wait_ge(norm["out"], out_count["mix0"])
            dense("in", 8, h, KD, 512, turns=4)

            pe.wait_ge(chunk_taken[0], 16 + 1)
            pe.wait_ge(chunk_taken[1], 16 + 1)
            with pe.Fori(0, heads) as i:
                pe.wait_ge(hg["vs"], i + 2)
                pe.wait_ge(hg["vtok"], i + 1)
                for c in range(TT):
                    m = nc.tensor.transpose(ps[:, 4, P * c:P * c + P], Vs[:, P * c:P * c + P], ident[:])
                m.then_inc(hg["vt"], 1)
                pe.wait_ge(hg["k"], i + 2)
                pe.wait_ge(hg["prod_taken"], i * 8 + 1)
                for c in range(TT):
                    m = nc.tensor.matmul(ps[:, 0, P * c:P * c + P], Kb[:, P * c:P * c + P],
                                         row(big, i)[:, P * c:P * c + P], start=True, stop=True)
                m.then_inc(hg["prod"], 1)
                pe.wait_ge(hg["kd"], i + 2)
                pe.wait_ge(hg["ktok"], i + 1)
                for c in range(TT):
                    m = nc.tensor.transpose(ps[:, 5, P * c:P * c + P], kd[:, P * c:P * c + P], ident[:])
                m.then_inc(hg["kt"], 1)
                for l in range(7):
                    pe.wait_ge(hg["lv"], i * 7 + l + 2)
                    pe.wait_ge(hg["prod_taken"], i * 8 + l + 2)
                    for c in range(TT):
                        m = nc.tensor.matmul(ps[:, (l + 1) % 4, P * c:P * c + P], Lv[l % 2][:, P * c:P * c + P],
                                             Lv[l % 2][:, P * c:P * c + P], start=True, stop=True)
                    m.then_inc(hg["prod"], 1)
                    if l == 1:
                        pe.wait_ge(hg["vtok"], i + 2)
                        pe.wait_ge(hg["ktok"], i + 2)
                        pe.wait_ge(hg["s"], i * 4 + 1)
                        for c in range(TT):
                            m = nc.tensor.matmul(ps[:, 6, P * c:P * c + P], ktok[:, P * c:P * c + P],
                                                 vtok[:, P * c:P * c + P], start=True, stop=True)
                        m.then_inc(hg["u"], 1)
                pe.wait_ge(hg["o_taken"], i + 1)
                pe.wait_ge(hg["at"], i + 2)
                pe.wait_ge(hg["qd"], i + 2)
                pe.wait_ge(hg["s"], i * 4 + 4 + 1)
                for c in range(TT):
                    m = nc.tensor.matmul(ps[:, 7, P * c:P * c + P], vtok[:, P * c:P * c + P],
                                         AT[:, P * c:P * c + P], start=True, stop=(c == 0))
                    if c:
                        m = nc.tensor.matmul(ps[:, 7, P * c:P * c + P], St[:, c - 1, :],
                                             qd[:, P * c:P * c + P], start=False, stop=True)
                m.then_inc(hg["o"], 1)

            with pe.Fori(0, heads // 2) as i:
                for p in range(2):
                    g = 2 * i + p
                    pe.wait_ge(hs["kv"], g + 2)
                    nc.tensor.transpose(ps[0:B, 4, 0:P], Ks, ident[:])
                    nc.tensor.transpose(ps[0:B, 4, P:2 * P], Vs8, ident[:]).then_inc(hs["turned"], 1)
                    pe.wait_ge(hs["tok"], g + 2)
                    for a in range(2):
                        m = nc.tensor.matmul(ps[:, 5 + a, 0:4 * P], Ktok8,
                                             Vsel[:, 4 * a:4 * a + 4, :].rearrange("p b v -> p (b v)"),
                                             start=True, stop=True)
                    m.then_inc(hs["outer"], 1)
                    pe.wait_ge(hs["state"], g + 2)
                    pe.wait_ge(hs["o_taken"], g + 1)
                    for b in range(B):
                        m = nc.tensor.matmul(ps[:, 7, b:b + 1], S0[p][:, b, :], Q8[:, b:b + 1],
                                             start=True, stop=True)
                    m.then_inc(hs["o"], 1)

            pe.wait_ge(on["sq"], 1)
            for k in range(heads):
                if k >= 2:
                    pe.wait_ge(on["sqrt"], k - 1)
                for a in range(2):
                    m = nc.tensor.matmul(ps[:, 2 * (k % 2) + a, 0:NH], ones[:], big[:, KD + k, NH * a:NH * a + NH],
                                         start=True, stop=True)
                m.then_inc(on["sum"], 1)
            pe.wait_ge(on["out"], heads)
            dense("out", 2, h, KD, 512)
            norm_sum("mlp0", h)
            pe.wait_ge(norm["out"], out_count["mlp0"])
            dense("up0", 8, h, KD, 512, turns=4)
            for c in range(2):
                pe.wait_ge(chunk_taken[c], (chunk_base["down0"]) // 2 + 1)
            dense("down0", 8, big, KF, P, turns=4)

            norm_sum("attn", h)
            pe.wait_ge(norm["out"], out_count["attn"])
            dense("kv", 3, h, KD, 512)
            dense("gate", 1, h2, KD, 3 * HEADS)
            dense("q", 2, h2, KD, 512)
            n_chunks = chunk_base["nsa_out"]
            for p in range(2):
                pe.wait_ge(chunk_taken[p], taken(p, n_chunks))
            for u in range(3 * TT):
                a, cg = u // 3, u % 3
                if u >= 4:
                    pe.wait_ge(kt_taken[u % 2], (u - 4) // 2 + 1)
                for c in range(4):
                    m = nc.tensor.transpose(ps[:, u % 4, P * c:P * c + P], KVT[:, 4 * cg + c, P * a:P * a + P], ident[:])
                m.then_inc(kt_ready, 1)
            for c in range(12):
                m = nc.tensor.transpose(ps[0:B, 4 + c // 4, P * (c % 4):P * (c % 4) + P], KVT[:, c, T:N], ident[:])
            m.then_inc(kvs_turned, 1)
            pe.wait_ge(gate_done, 1)
            for a in range(TT):
                nc.tensor.transpose(ps[:, 7, 3 * HEADS * a:3 * HEADS * a + 3 * HEADS], gT[:, P * a:P * a + P],
                                    ident[0:3 * HEADS, 0:3 * HEADS])
            for r in range(3):
                m = nc.tensor.matmul(ps[0:HEADS, 7, 192 + B * r:192 + B * r + B],
                                     ident[0:3 * HEADS, HEADS * r:HEADS * r + HEADS], gT[:, T:N], start=True, stop=True)
            m.then_inc(gturned, 1)

            def comp_turn(src, n, bank):
                for g in range(G):
                    m = nc.tensor.transpose(ps[:, bank, P * g:P * g + n], src[0:n, g, :], ident[0:n, 0:n])
                return m

            def comp_mul(tk, n, kv, rp, bank):
                for par in range(2):
                    kk = 4 * par + rp
                    m = nc.tensor.matmul(ps[:, bank, 0:G * n // 2], W1[kv][:, kk, :, :].rearrange("p a n -> p (a n)"),
                                         tk.rearrange("p (g s a) -> p g s a", g=G, a=2)[:, :, 0:n // 2, par],
                                         start=(rp == 0 and par == 0), stop=(rp == 3 and par == 1),
                                         skip_group_check=True)
                return m

            pe.wait_ge(small_in, 64)
            pe.wait_ge(kvs_ready, 1)
            for i in range(2):
                m = nc.tensor.transpose(ps[:, 4, 16 * i:16 * i + 16], pe_rows[0:16, i, :], ident[0:16, 0:16])
            m.then_inc(pc["pe_turned"], 1)
            pe.wait_ge(pc["pe_cols"], 1)
            pe.wait_ge(w1_in, 64)
            for i in range(2):
                for k in range(16):
                    m = nc.tensor.matmul(ps[0:DK, 5, i:i + 1], W1[i][:, k % 8, k // 8, :], pe_cols[:, i, k:k + 1],
                                         start=(k == 0), stop=(k == 15))
            m.then_inc(pc["bias_ready"], 1)
            n_p = T // HT
            pe.wait_ge(psrc_in, 16)
            for p in range(2):
                pe.wait_ge(kt_taken[p], 6)
            for u in range(9):
                if u < 8:
                    if u >= 2:
                        pe.wait_ge(pc[f"ev{u % 2}"], (u - 2) // 2 + 1)
                    pe.wait_ge(pc["rg"], u + 1)
                    comp_turn(RG[u % 2], n_p, u % 2).then_inc(pc["turned"], 1)
                if u:
                    v = u - 1
                    pe.wait_ge(pc[f"ev{v % 2}"], v // 2 + 1)
                    comp_mul(TK[v % 2], n_p, v // 4, v % 4, 2 + v // 4).then_inc(pc["mul"], 1)
            pe.wait_ge(pc["h"], 1)
            nc.tensor.matmul(ps[0:DK, 4, 0:G * NB_P], W2[0], Hp[:, 0:G, :].rearrange("p g s -> p (g s)"), start=True, stop=True)
            for g in range(G):
                m = nc.tensor.matmul(ps[0:NB_P, 5, DK * g:DK * g + DK], Hp[:, G + g, :], W2[1], start=True, stop=True)
            m.then_inc(pc["kc"], 1)

            for p in range(1):
                pe.wait_ge(kd_ready, 3)
            pe.wait_ge(gtaken, 2)
            with pe.Fori(0, G) as g:
                pe.wait_ge(pa["k"], g * 2 + 3)
                pe.wait_ge(pa["q"], g + 2)

                def scores(u):
                    t, j = u // HPG, u % HPG
                    o, w = DK * (j % 2), P * (t + 1)
                    if j == 0:
                        pe.wait_ge(pa["mixed"], g * TT + t + 1)
                        for jj in range(0, HPG, 2), range(1, HPG, 2):
                          for jj in jj:
                            oo = DK * (jj % 2)
                            m = nc.tensor.matmul(ps[:, 7, 32 * jj:32 * jj + NB_P],
                                                 qg[oo:oo + DK, jj // 2, P * t:P * t + P], kcg[oo:oo + DK, :],
                                                 start=True, stop=True)
                          if oo == 0:
                            m.then_inc(pa["ce"], 1)
                            hold(pe, pa["ce"], g * TT + t + 2)
                        m.then_inc(pa["cs"], 1)
                    pe.wait_ge(pa["p"], g * 16 + u + (0 if u else 1))
                    for br in range(2):
                        m = nc.tensor.matmul(ps[:, 2 * (u % 2) + br, 0:w], qg[o:o + DK, j // 2, P * t:P * t + P],
                                             Kg[o:o + DK, br, 0:w], start=True, stop=True)
                    m.then_inc(pa["s"], 1)

                def turn(u):
                    t = u // HPG
                    pe.wait_ge(pa["p"], g * 16 + u + 2)
                    for br, (rd, ev) in enumerate((("ts", "es"), ("tw", "ew"))):
                        pe.wait_ge(pa[ev], g * 16 + u + 1)
                        if br == 1:
                            pe.wait_ge(pa["h"], g * TT + t + 1)
                        for s_ in range(t + 1):
                            m = nc.tensor.transpose(ps[:, 4 + br, P * s_:P * s_ + P], Pb[u % 2][:, br, P * s_:P * s_ + P],
                                                    ident[:])
                        m.then_inc(pa[rd], 1)

                def values(u):
                    t, j = u // HPG, u % HPG
                    pe.wait_ge(pa["es"], g * 16 + u + 2)
                    pe.wait_ge(pa["ew"], g * 16 + u + 2)
                    for br in range(2):
                        for s_ in range(t + 1):
                            m = nc.tensor.matmul(ps[:, 6, 256 * br + DK * j:256 * br + DK * j + DK], PT[u % 2][:, br, s_, :],
                                                 Vg[:, s_, br, :], start=(s_ == 0), stop=(s_ == t))
                    m.then_inc(pa["o"], 1)
                    if j == HPG - 1:
                        pe.wait_ge(pa["csum"], g * TT + t + 2)
                        pe.wait_ge(pa["es"], g * 16 + u + 2)
                        for jj in range(HPG):
                            m = nc.tensor.transpose(ps[0:NB_P, 7, 128:256] if False else ps[0:NB_P, 4, P * jj:P * jj + P],
                                                    Scm[0][:, jj, :], ident[:])
                        m.then_inc(pa["ct"], 1)
                        pe.wait_ge(pa["ect"], g * TT + t + 2)
                        for jj in range(HPG):
                            m = nc.tensor.matmul(ps[:, 7, 256 + DK * jj:256 + DK * jj + DK], PcT[:, P * jj:P * jj + P],
                                                 Vc_g, start=True, stop=True)
                        m.then_inc(pa["oc"], 1)
                        pe.wait_ge(pa["mixed"], g * TT + t + 2)
                        for cc in range(2):
                            m = nc.tensor.transpose(ps[:, 5, P * cc:P * cc + P],
                                                    otok[:, 2 * cc:2 * cc + 2, :], ident[:])
                        m.then_inc(pa["ot"], 1)

                scores(0)
                for u in range(4 * HPG):
                    last = u % HPG == HPG - 1
                    if u + 1 < 4 * HPG and not last:
                        scores(u + 1)
                    turn(u)
                    values(u)
                    if u + 1 < 4 * HPG and last:
                        scores(u + 1)

            pe.wait_ge(attn_const, 2)
            UN = 26
            with pe.Fori(0, B) as b:
                def turn_unit(u):
                    if u == 0:
                        pe.wait_ge(sa["pt_taken"], b + 1 + past["pt_taken"])
                    pe.wait_ge(sa[f"ev{u % 2}"], b * 13 + u // 2 + 1 + past[f"ev{u % 2}"])
                    if u < 16:
                        pe.wait_ge(sa["rg"], b * 16 + u + 2)
                        m = comp_turn(RG[u % 2], P, u % 2)
                    elif u < 24:
                        q, pr = (u - 16) // 2, u % 2
                        if u in (16, 20):
                            pe.wait_ge(slc_in[q // 2], b * 16 * (PAGES // 2) + 16 * (PAGES // 2))
                        for c in range(4):
                            m = nc.tensor.transpose(ps[:, u % 2, P * c:P * c + P],
                                                    cslot(1, q // 2)[:, 4 * (q % 2) + c, P * pr:P * pr + P], ident[:])
                    else:
                        if u == 24:
                            pe.wait_ge(own_in, b * 16 + 16)
                        for c in range(4):
                            m = nc.tensor.transpose(ps[:, u % 2, P * c:P * c + P],
                                                    Wt[:, c, P * (u % 2):P * (u % 2) + P], ident[:])
                    m.then_inc(sa["turned"], 1)

                def mul_unit(u):
                    pe.wait_ge(sa[f"ev{u % 2}"], b * 13 + u // 2 + 2 + past[f"ev{u % 2}"])
                    if u < 16:
                        e = u // 4
                        if u % 4 == 0:
                            if e < 2:
                                pe.wait_ge(sa["os"], b + 1 + past["os"])
                            else:
                                pe.wait_ge(sa["ab_a"], b * 4 + e + past["ab_a"])
                                pe.wait_ge(sa["ab_b"], b * 4 + e + past["ab_b"])
                        m = comp_mul(TK[u % 2], P, e % 2, u % 4, 2 + e % 2)
                    elif u < 24:
                        q, pr = (u - 16) // 2, u % 2
                        m = nc.tensor.matmul(ps[0:HEADS, 4 + q, :], Qp[:, pr, :], TK[u % 2], start=(pr == 0), stop=(pr == 1))
                    else:
                        m = nc.tensor.matmul(ps[0:HEADS, 3, :], Qp[:, u % 2, :], TK[u % 2], start=(u == 24), stop=(u == 25))
                    m.then_inc(sa["mul"], 1)

                pe.wait_ge(sa["own"], b + 2 + past["own"])
                turn_unit(0)
                for u in range(UN):
                    if u + 1 < UN:
                        if u + 1 == 24:
                            pe.wait_ge(sa["vc_taken"], b + 2 + past["vc_taken"])
                        turn_unit(u + 1)
                    mul_unit(u)
                    if u == 19:
                        hold(pe, sa["h"], b + 2 + past["h"])
                        nc.tensor.matmul(ps[0:DK, 2, 0:G * NB_S], W2[0], Hs[:, 0:G, :].rearrange("p g s -> p (g s)"),
                                         start=True, stop=True)
                        for g in range(G):
                            m = nc.tensor.matmul(ps[0:NB_S, 3, DK * g:DK * g + DK], Hs[:, G + g, :], W2[1],
                                                 start=True, stop=True)
                        m.then_inc(sa["kc"], 1)
                    if u == 21:
                        hold(pe, sa["kc_taken"], b + 2 + past["kc_taken"])
                        for g in range(G):
                            m = nc.tensor.matmul(ps[0:HEADS, 2, 0:NB_S], Qz[:, g, :], kcS[:, g, :],
                                                 start=(g == 0), stop=(g == G - 1))
                        for pr in range(2):
                            m = nc.tensor.matmul(ps[0:HEADS, 2, 240:241], Qp[:, pr, :], Kn[:, pr:pr + 1],
                                                 start=(pr == 0), stop=(pr == 1))
                        m.then_inc(sa["cs"], 1)
                hold(pe, sa["pn"], b + 2 + past["pn"])
                nc.tensor.transpose(ps[0:NB_S, 2, 128:128 + HEADS], Pc[:, 0:NB_S], ident[0:HEADS, 0:HEADS]).then_inc(sa["pnt"], 1)
                pe.wait_ge(sa["pnt_taken"], b + 2 + past["pnt_taken"])
                nc.tensor.matmul(ps[0:HEADS, 2, 160:160 + NSLC], PnT, Msel, start=True, stop=True).then_inc(sa["u"], 1)
                hold(pe, sa["u_taken"], b + 2 + past["u_taken"])
                nc.tensor.matmul(ps[0:HEADS, 2, 200:200 + NSLC], Gsel, U, start=True, stop=True).then_inc(sa["imp"], 1)
                pe.wait_ge(sa["dg"], b + 2 + past["dg"])
                pe.wait_ge(sa["ev0"], b * 13 + 14 + past["ev0"])
                for n in range(16):
                    nc.tensor.matmul(ps[:, 0, HEADS * n:HEADS * n + HEADS], S[:, P * n:P * n + P], Dg[:, 1, :],
                                     start=True, stop=True)
                for n in range(4):
                    nc.tensor.matmul(ps[:, 0, 256 + HEADS * n:256 + HEADS * n + HEADS], Sw[:, P * n:P * n + P], Dg[:, 2, :],
                                     start=True, stop=True)
                nc.tensor.matmul(ps[0:1, 0, 320:320 + HEADS], S[:, PAST:PAST + 1], Dg[:, 1, :], start=True, stop=True)
                nc.tensor.matmul(ps[0:NB_S, 0, 336:336 + HEADS], Pc[:, 0:NB_S], Dg[:, 0, :], start=True, stop=True)\
                    .then_inc(sa["pt"], 1)
                pe.wait_ge(sa["pt_taken"], b + 2 + past["pt_taken"])
                pe.wait_ge(vn_in, b * 16 + 16)
                for pr in range(2):
                    o = ps[:, 2, 256 + HEADS * pr:256 + HEADS * pr + HEADS]
                    f = GD + P * pr
                    for n in range(16):
                        nc.tensor.matmul(o, cslot(1, n // 8)[:, n % 8, f:f + P], PTs[:, HEADS * n:HEADS * n + HEADS],
                                         start=(n == 0), stop=False)
                    for n in range(4):
                        nc.tensor.matmul(o, Wt[:, n, f:f + P], PTs[:, 256 + HEADS * n:256 + HEADS * n + HEADS],
                                         start=False, stop=False)
                    nc.tensor.matmul(o, Vn[:, P * pr:P * pr + P], PTs[0:1, 320:320 + HEADS], start=False, stop=False)
                    m = nc.tensor.matmul(o, VcS[:, P * pr:P * pr + P], PTs[0:NB_S, 336:336 + HEADS], start=False, stop=True)
                m.then_inc(sa["o"], 1)

            pe.wait_ge(hready, 8)
            pe.wait_ge(pa["h"], G * TT + 1)
            dense("nsa_out", 2, h, KD, 512)
            norm_sum("mlp1", h)
            pe.wait_ge(norm["out"], out_count["mlp1"])
            dense("up1", 8, h, KD, 512, turns=4)
            for p in range(2):
                pe.wait_ge(chunk_taken[p], taken(p, chunk_base["down1"]))
            dense("down1", 8, big, KF, P, turns=4)
            norm_sum("final", h)
            pe.wait_ge(norm["out"], out_count["final"])
            for u in range(2 * TT):
                a, cg = u // 2, u % 2
                if u >= 4:
                    pe.wait_ge(ydone[u % 2], (u - 4) // 2 + 1)
                for c in range(4):
                    m = nc.tensor.transpose(ps[:, u % 4, P * c:P * c + P], h[:, 4 * cg + c, P * a:P * a + P], ident[:])
                m.then_inc(yturned, 1)
            for c in range(KD):
                m = nc.tensor.transpose(ps[0:B, 4 + c // 4, P * (c % 4):P * (c % 4) + P], h[:, c, T:N], ident[:])
            m.then_inc(yturned, 1)

        @block.scalar
        def _(act):
            ch = Chain(act, act_chain)
            start_counts(act, hg, ("f", "vs", "e", "eend", "eb", "vtok", "ktok", "o_taken"))
            start_counts(act, hs, ("f", "o_taken"))
            act.wait_ge(lb_done, 1)
            ch.link(nc.scalar.activation(lnb[:, 1, :], lnb[:, 0, :], ACT.Exp))
            act.sem_inc(lb_done, 1)
            act.wait_ge(lb_done, 3)
            ch.link(nc.scalar.activation(lnb[:, 3, :], lnb[:, 2, :], ACT.Ln))
            act.sem_inc(lb_done, 1)

            def norm_act(name, sq):
                n = turn_of[name]
                for k in range(1, KD, 2):
                    nc.scalar.activation(sq[:, k, :], x[:, k, :], ACT.Square).then_inc(norm["sq_act"], 1)
                act.wait_ge(norm["sum"], n + 1)
                nc.scalar.activation(halves(rstd[:]), ps[:, 6:8, 0:NH], ACT.Sqrt, bias=eps[:], scale=1.0 / D)\
                    .then_inc(norm["sqrt"], 1)

            act.wait_ge(turn_taken, 2 + KD)
            norm_act("mix0", h)
            with ch.loop(4, 2) as i:
                for p in range(2):
                    act.wait_ge(fz_ready, 2 * i + p + 1)
                    ch.link(nc.scalar.activation(Nz[p], Nz[p], ACT.Exp))
                    nc.scalar.activation(Nz[p], Nz[p], ACT.Ln, bias=1.0).then_inc(fe_ready, 1)
            with act.Fori(0, 4) as i:
                for p in range(2):
                    act.wait_ge(gz_ready, 2 * i + p + 1)
                    nc.scalar.activation(Nz[p], Mz[p], ACT.Tanh, scale=0.5).then_inc(ge_ready, 1)
            for first, c0 in ((0, 16), (16, 24)):
                with act.Fori(0, 4) as i:
                    for p in range(2):
                        act.wait_ge(chunk_ready, 2 * i + c0 + p + 1)
                        nc.scalar.activation(halves(row(big, 2 * i + first + p)), pair(p), ACT.Copy)\
                            .then_inc(chunk_taken[p], 1)
            act.wait_ge(chunk_taken[0], 17)
            act.wait_ge(chunk_taken[1], 17)
            with act.Fori(0, heads) as i:
                act.wait_ge(hg["lv"], i * 7 + 1)
                act.wait_ge(hg["prod"], i * 8 + 1)
                nc.scalar.activation(Fb, row(big, KD + i), ACT.Exp).then_inc(hg["f"], 1)
                nc.scalar.activation(Vs, row(big, 2 * KD + i)[:, 0:T], ACT.Copy).then_inc(hg["vs"], 1)
                act.wait_ge(hg["dend"], i + 2)
                act.wait_ge(hg["kd"], i + 1)
                nc.scalar.activation(Eend, Dend, ACT.Exp).then_inc(hg["eend"], 1)
                act.wait_ge(hg["s"], i * 4 + 1)
                act.wait_ge(hg["qd"], i + 1)
                nc.scalar.activation(EB, Bc, ACT.Exp).then_inc(hg["eb"], 1)
                for l in range(7):
                    act.wait_ge(hg["d"], i * 7 + l + 2)
                    if l >= 2:
                        act.wait_ge(hg["lv"], i * 7 + l )
                    nc.scalar.activation(Er[l % 2], Dr[l % 2], ACT.Exp).then_inc(hg["e"], 1)
                    if l == 1:
                        act.wait_ge(hg["vt"], i + 2)
                        act.wait_ge(hg["o"], i + 1)
                        nc.scalar.activation(vtok, ps[:, 4, :], ACT.Copy).then_inc(hg["vtok"], 1)
                        act.wait_ge(hg["kt"], i + 2)
                        nc.scalar.activation(ktok, ps[:, 5, :], ACT.Copy).then_inc(hg["ktok"], 1)
                act.wait_ge(hg["o"], i + 2)
                nc.scalar.activation(row(h, i)[:, 0:T], ps[:, 7, :], ACT.Copy).then_inc(hg["o_taken"], 1)
            with act.Fori(0, heads) as i:
                act.wait_ge(hs["state"], i + 1)
                nc.scalar.activation(Fs, row(big, KD + i)[:, T:N], ACT.Exp).then_inc(hs["f"], 1)
                act.wait_ge(hs["o"], i + 2)
                nc.scalar.activation(row(h, i)[:, T:N], ps[:, 7, 0:B], ACT.Copy).then_inc(hs["o_taken"], 1)
            act.wait_ge(hs["o_taken"], heads + 1)
            act.wait_ge(hg["o_taken"], heads + 1)
            nc.scalar.activation(big[:, KD:2 * KD, :], h[:], ACT.Square).then_inc(on["sq"], 1)
            for k in range(heads):
                act.wait_ge(on["sum"], k + 1)
                nc.scalar.activation(halves(big[:, KD + k, :]), pair(k), ACT.Sqrt, bias=eps[:], scale=1.0 / P)\
                    .then_inc(on["sqrt"], 1)
            for c in range(2):
                act.wait_ge(chunk_taken[c], chunk_base["up0"] // 2 + 1)
            norm_act("mlp0", h)

            def settle_chunks(eng, n):
                for p in range(2):
                    eng.wait_ge(chunk_taken[p], taken(p, n))

            settle_chunks(act, chunk_base["kv"])
            norm_act("attn", h)
            act.wait_ge(norm["out"], out_count["attn"])
            for n in range(12):
                c = chunk_base["kv"] + n
                act.wait_ge(chunk_ready, c + 1)
                nc.scalar.activation(halves(KVT[:, n, :]), pair(c), ACT.Copy).then_inc(chunk_taken[c % 2], 1)
            c = chunk_base["gate"]
            act.wait_ge(chunk_ready, c + 1)
            nc.scalar.activation(halves(gT), pair(c)[0:3 * HEADS], ACT.Tanh, scale=0.5).then_inc(chunk_taken[c % 2], 1)
            act.wait_ge(chunk_taken[c % 2], taken(c % 2, c + 1))
            act.sem_inc(gate_ready, 1)
            for n in range(8):
                c = chunk_base["q"] + n
                act.wait_ge(chunk_ready, c + 1)
                nc.scalar.activation(halves(QT[:, n, :]), pair(c), ACT.Copy).then_inc(chunk_taken[c % 2], 1)
            settle_chunks(act, chunk_base["nsa_out"])
            start_counts(act, pa, ("q", "cexp", "p", "ew", "h"))
            for u in range(1, 3 * TT, 2):
                act.wait_ge(kt_ready, u + 1)
                nc.scalar.activation(kvtok[:, u // 3, 512 * (u % 3):512 * (u % 3) + 512], ps[:, u % 4, :], ACT.Copy)\
                    .then_inc(kt_taken[1], 1)
            for g in range(2):
                for dup in range(2):
                    m = nc.scalar.activation(KD2[DK * dup:DK * dup + DK, g, :, :],
                                             KVT[DK * (g % 2):DK * (g % 2) + DK, 4 + g // 2:9 + g // 2:4, 0:T], ACT.Copy)
            m.then_inc(kd_ready, 1)
            for u in range(0, 8, 2):
                act.wait_ge(pc["turned"], u + 1)
                if u >= 2:
                    act.wait_ge(pc["mul"], u - 1)
                nc.scalar.activation(TK[0].rearrange("p (g s) -> p g s", g=G)[:, :, 0:T // HT],
                                     ps[:, 0, :].rearrange("p (g s) -> p g s", g=G)[:, :, 0:T // HT], ACT.Copy)\
                    .then_inc(pc["ev0"], 1)
            for kv in range(2):
                act.wait_ge(pc["mul"], 4 * kv + 4)
                nc.scalar.activation(Bt[:, G * kv:G * kv + G, 0:T // SUB],
                                     ps[DK:2 * DK, 2 + kv, 0:G * T // SUB].rearrange("p (g s) -> p g s", g=G), ACT.Copy)\
                    .then_inc(pc["ab_b"], 1)
            act.wait_ge(pc["z"], 1)
            nc.scalar.activation(Hp, Zp, ACT.Tanh, scale=0.5).then_inc(pc["tanh"], 1)
            act.wait_ge(pc["kc"], 1)
            for dup in range(2):
                m = nc.scalar.activation(kcT[DK * dup:DK * dup + DK, :, :],
                                         ps[0:DK, 4, 0:G * NB_P].rearrange("p (g s) -> p g s", g=G), ACT.Copy, scale=0.5)
            m.then_inc(pc["kc_taken"], 1)
            act.wait_ge(pc["kc_taken"], 1)
            act.wait_ge(pc["vc_taken"], 1)
            act.wait_ge(kd_ready, 2)
            act.sem_inc(kd_ready, 1)
            with act.Fori(0, G) as g:
                hold(act, pa["o"], g * 16 + 1)
                nc.scalar.activation(qg, QT[:, ds(g * 2, 2), 0:T], ACT.Copy, scale=SCALE).then_inc(pa["q"], 1)

                def exps(u):
                    t, j = u // HPG, u % HPG
                    if j == 0:
                        act.wait_ge(pa["cmax"], g * TT + t + 2)
                        nc.scalar.activation(Scm[0], Scm[0], ACT.Exp).then_inc(pa["cexp"], 1)
                    w = P * (t + 1)
                    act.wait_ge(pa["max"], g * 16 + u + 2)
                    act.wait_ge(pa["tw"], g * 16 + max(u, 1))
                    if j == 0:
                        act.wait_ge(pa["mixed"], g * TT + t + 1)
                    for br in range(2):
                        m = nc.scalar.activation(Pb[u % 2][:, br, 0:w], ps[:, 2 * (u % 2) + br, 0:w], ACT.Exp,
                                                 bias=nmax[u % 2][:, br:br + 1], accum_out=sums[:, br, j:j + 1])
                    m.then_inc(pa["p"], 1)

                exps(0)
                for u in range(4 * HPG):
                    t, j = u // HPG, u % HPG
                    last = j == HPG - 1
                    if u + 1 < 4 * HPG and not last:
                        exps(u + 1)
                    act.wait_ge(pa["tw"], g * 16 + u + 2)
                    act.wait_ge(pa["o"], g * 16 + max(u, 1))
                    nc.scalar.activation(PT[u % 2][:, 1, 0:t + 1, :],
                                         ps[:, 5, 0:P * (t + 1)].rearrange("p (s t) -> p s t", t=P), ACT.Copy)\
                        .then_inc(pa["ew"], 1)
                    if last:
                        hold(act, pa["ot"], g * TT + t + 2)
                        nc.scalar.activation(h[:, ds(g * 2, 2), P * t:P * t + P],
                                             ps[:, 5, 0:2 * P].rearrange("p (c t) -> p c t", c=2), ACT.Copy)\
                            .then_inc(pa["h"], 1)
                        if u + 1 < 4 * HPG:
                            exps(u + 1)

            with act.Fori(0, B) as b:
                def evac(u):
                    act.wait_ge(sa["turned"], b * 26 + u + 2 + past["turned"])
                    act.wait_ge(sa["mul"], b * 26 + max(u, 1) + past["mul"])
                    nc.scalar.activation(TK[0], ps[:, 0, :], ACT.Copy).then_inc(sa["ev0"], 1)

                def part_b(e):
                    act.wait_ge(sa["mul"], b * 26 + 4 * e + 5 + past["mul"])
                    act.wait_ge(sa["z"], b + 1 + past["z"])
                    o = G * (e % 2)
                    nc.scalar.activation(Bt[:, o:o + G, 64 * (e // 2):64 * (e // 2) + 64],
                                         ps[DK:2 * DK, 2 + e % 2, 0:256].rearrange("p (g s) -> p g s", g=G), ACT.Copy)\
                        .then_inc(sa["ab_b"], 1)

                for u in range(0, 18, 2):
                    evac(u)
                    if u % 4 == 0 and u >= 4:
                        part_b(u // 4 - 1)
                act.wait_ge(sa["z"], b + 2 + past["z"])
                nc.scalar.activation(Hs, Zs, ACT.Tanh, scale=0.5).then_inc(sa["tanh"], 1)
                evac(18)
                evac(20)
                act.wait_ge(sa["kc"], b + 2 + past["kc"])
                nc.scalar.activation(kcS.rearrange("p g s -> p (g s)"), ps[0:DK, 2, 0:G * NB_S], ACT.Copy, scale=0.5)\
                    .then_inc(sa["kc_taken"], 1)
                evac(22)
                evac(24)
                act.wait_ge(sa["cmax"], b + 2 + past["cmax"])
                act.wait_ge(sa["new"], b + 2 + past["new"])
                nc.scalar.activation(Pc[:, 0:NB_S], ps[0:HEADS, 2, 0:NB_S], ACT.Exp, bias=smax[:, 0:1],
                                     accum_out=ssum[:, 0:1]).then_inc(sa["cexp"], 1)
                act.wait_ge(sa["wmax"], b + 2 + past["wmax"])
                nc.scalar.activation(Sw, ps[0:HEADS, 3, :], ACT.Exp, bias=smax[:, 2:3],
                                     accum_out=ssum[:, 2:3]).then_inc(sa["wexp"], 1)
                act.wait_ge(sa["smax"], b + 2 + past["smax"])
                nc.scalar.activation(S[:, 0:NK], S[:, 0:NK], ACT.Exp, bias=smax[:, 1:2],
                                     accum_out=ssum[:, 1:2]).then_inc(sa["sexp"], 1)

            settle_chunks(act, chunk_base["up1"])
            norm_act("mlp1", h)
            settle_chunks(act, chunks[0])
            norm_act("final", h)
            for u in range(1, 2 * TT, 2):
                act.wait_ge(yturned, u + 1)
                nc.scalar.activation(yrows[:, u // 2, 512 * (u % 2):512 * (u % 2) + 512], ps[:, u % 4, :], ACT.Copy)\
                    .then_inc(ydone[1], 1)

        @block.vector
        def _(dve):
            ch = Chain(dve, dve_chain)
            start_counts(dve, hg, ("scan", "k", "d", "dend", "s", "at"))
            start_counts(dve, hs, ("kv", "tok", "state"))
            dve.sem_inc(hg["s_stored"], 16)
            for p in range(2):
                dve.sem_inc(hs[f"s_in{p}"], 16)
                dve.sem_inc(hs[f"s_out{p}"], 16)
            dve.sem_inc(chunk_taken[0], 1)
            dve.sem_inc(chunk_taken[1], 1)
            dve.sem_inc(hg["prod_taken"], 4)
            dve.wait_ge(turned, 1)
            nc.vector.tensor_copy(vec[:], ps[:, 7, 0:64]).then_inc(turn_taken, 1)
            dve.wait_ge(turned, 2)
            nc.vector.tensor_copy(x[:, :, T:N], ps[:, 6, 0:B * KD].rearrange("p (k b) -> p k b", k=KD))\
                .then_inc(turn_taken, 1)
            for k in range(KD):
                dve.wait_ge(turned, 3 + k)
                nc.vector.tensor_copy(x[:, k, 0:T], ps[:, k % 4, :]).then_inc(turn_taken, 1)
            dve.wait_ge(turn_taken, 1)
            z = vec[:, LOGITS:LOGITS + KD]
            ch.link(nc.vector.tensor_tensor(lnb[:, 0, :], z, z, ALU.subtract))
            dve.sem_inc(lb_done, 1)
            dve.wait_ge(lb_done, 2)
            ch.link(nc.vector.reciprocal(lnb[:, 2, :], lnb[:, 1, :]))
            ch.link(nc.vector.tensor_tensor(lnb[:, 1, :], lnb[:, 1, :], lnb[:, 2, :], ALU.mult))
            ch.link(nc.vector.tensor_tensor(lnb[:, 1, :], lnb[:, 1, :], lnb[:, 1, :], ALU.subtract))
            ch.link(nc.vector.tensor_scalar(lnb[:, 2, :], lnb[:, 1, :], -1.0, 1.0, ALU.mult, ALU.add))
            dve.sem_inc(lb_done, 1)

            def norm_dve(name, sq, outputs):
                n = turn_of[name]
                for k in range(0, KD, 2):
                    nc.vector.tensor_tensor(sq[:, k, :], x[:, k, :], x[:, k, :], ALU.mult).then_inc(norm["sq_dve"], 1)
                dve.wait_ge(norm["sqrt"], n + 1)
                ch.link(nc.vector.reciprocal(rstd[:], rstd[:]))
                for gain, out in outputs:
                    for k in range(KD):
                        nc.vector.scalar_tensor_tensor(out=out[:, k, :], in0=x[:, k, :],
                                                       scalar=vec[:, gain + k:gain + k + 1], in1=rstd[:],
                                                       op0=ALU.mult, op1=ALU.mult).then_inc(norm["out"], 1)

            dve.wait_ge(turn_taken, 2 + KD)
            norm_dve("mix0", h, [(GAIN_MIX, h)])
            dve.wait_ge(lb_done, 4)
            with ch.loop(4, 2) as i:
                for p in range(2):
                    dve.wait_ge(chunk_ready, 2 * i + p + 1)
                    ch.link(nc.vector.tensor_scalar(halves(Mz[p]), pair(p), 0.0, None, ALU.min))
                    nc.vector.scalar_tensor_tensor(out=halves(Nz[p]), in0=halves(Mz[p]), scalar=2.0, in1=pair(p),
                                                   op0=ALU.mult, op1=ALU.subtract).then_inc(fz_ready, 1)
                    dve.wait_ge(fz_ready, 2 * i + p + 1)
                    dve.sem_inc(chunk_taken[p], 1)
                    dve.wait_ge(fe_ready, 2 * i + p + 1)
                    nc.vector.scalar_tensor_tensor(out=row(big, 2 * i + KD + p), in0=Mz[p],
                                                   scalar=lnb[:, 3, ds(2 * i + p, 1)], in1=Nz[p],
                                                   op0=ALU.add, op1=ALU.subtract)
            with ch.loop(4, 2) as i:
                for p in range(2):
                    dve.wait_ge(chunk_ready, 2 * i + 8 + p + 1)
                    nc.vector.tensor_copy(halves(Mz[p]), pair(p)).then_inc(gz_ready, 1)
                    dve.wait_ge(gz_ready, 2 * i + p + 1)
                    dve.sem_inc(chunk_taken[p], 1)
                    dve.wait_ge(ge_ready, 2 * i + p + 1)
                    ch.link(nc.vector.tensor_scalar(Nz[p], Nz[p], 0.5, 0.5, ALU.mult, ALU.add))
                    nc.vector.tensor_tensor(row(big, 2 * i + 3 * KD + p), Mz[p], Nz[p], ALU.mult)
            dve.wait_ge(chunk_taken[0], 17)
            dve.wait_ge(chunk_taken[1], 17)
            bc = Bc.rearrange("p (c t) -> p c t", c=TT)
            with ch.loop(heads, 7) as i:
                dve.wait_ge(hg["eb"], i + 1)
                nc.vector.tensor_tensor_scan(Bc, reset, row(big, KD + i)[:, 0:T], 0.0, ALU.mult, ALU.add)\
                    .then_inc(hg["scan"], 1)
                dve.wait_ge(hg["f"], i + 2)
                dve.wait_ge(hg["lv"], i * 7 + 1)
                nc.vector.tensor_scalar(Kb, Fb, -1.0, 1.0, ALU.mult, ALU.add).then_inc(hg["k"], 1)
                dve.wait_ge(hg["scan"], i + 2)
                dve.wait_ge(hg["eend"], i + 1)
                nc.vector.tensor_tensor(Dend.rearrange("p (c t) -> p c t", c=TT),
                                        bc[:, :, P - 1:P].to_broadcast([P, TT, P]), bc, ALU.subtract)\
                    .then_inc(hg["dend"], 1)

                def take(n, mask):
                    dve.wait_ge(hg["prod"], i * 8 + n + 2)
                    if n == 0:
                        dve.wait_ge(hg["o"], i + 1)
                    dve.wait_ge(hg["prod_taken"], i * 8 + 4 + n)
                    dve.sem_inc(hg["take"], 1)
                    nc.vector.copy_predicated(
                        AT.rearrange("p (c t) -> p c t", c=TT),
                        masks[:, mask:mask + 1, :].to_broadcast([P, TT, P]).bitcast(I32),
                        ps[:, n % 4, :].rearrange("p (c t) -> p c t", c=TT)).then_inc(hg["prod_taken"], 1)

                for l in range(7):
                    m = 64 >> l
                    b4 = Bc.rearrange("p (j a u) -> p j a u", a=2, u=m)
                    d4 = Dr[l % 2].rearrange("p (j a u) -> p j a u", a=2, u=m)
                    nb = T // (2 * m)
                    ref = b4[:, :, 0, m - 1:m].to_broadcast([P, nb, m])
                    if l >= 2:
                        dve.wait_ge(hg["e"], i * 7 + l )
                    ch.add(nc.vector.tensor_tensor(d4[:, :, 0, :], ref, b4[:, :, 0, :], ALU.subtract))
                    nc.vector.tensor_tensor(d4[:, :, 1, :], b4[:, :, 1, :], ref, ALU.subtract).then_inc(hg["d"], 1)
                    if l == 0:
                        take(0, 7)
                    if l >= 2:
                        take(l - 1, l - 2)
                    if l == 3:
                        dve.wait_ge(hg["u"], i + 2)
                        dve.wait_ge(hg["eb"], i + 2)
                        dve.wait_ge(hg["s_stored"], i * 16 + 16)
                        u = ps[:, 6, :].rearrange("p (c v) -> p c v", c=TT)
                        nc.vector.tensor_copy(St[:, 0, :], u[:, 0, :]).then_inc(hg["s"], 1)
                        for c in range(1, TT):
                            dve.wait_ge(hg["s"], i * 4 + c + 1)
                            nc.vector.scalar_tensor_tensor(out=St[:, c, :], in0=St[:, c - 1, :],
                                                           scalar=EB[:, P * c + P - 1:P * c + P], in1=u[:, c, :],
                                                           op0=ALU.mult, op1=ALU.add).then_inc(hg["s"], 1)
                take(6, 5)
                take(7, 6)
                dve.wait_ge(hg["prod_taken"], i * 8 + 12)
                dve.sem_inc(hg["at"], 1)
            with ch.loop(heads // 2, 6) as i:
                for p in range(2):
                    g = 2 * i + p
                    dve.wait_ge(hs["f"], g + 2)
                    dve.wait_ge(hs["o"], g + 1)
                    ch.add(nc.vector.tensor_scalar(Ks, Fs, -1.0, 1.0, ALU.mult, ALU.add))
                    ch.add(nc.vector.tensor_copy(Vs8, row(big, 2 * i + 2 * KD + p)[:, T:N]))
                    nc.vector.tensor_copy(Q8, row(big, 2 * i + p)[:, T:N]).then_inc(hs["kv"], 1)
                    dve.wait_ge(hs["turned"], g + 2)
                    nc.vector.tensor_copy(Ktok8, ps[0:B, 4, 0:P])
                    nc.vector.tensor_tensor(
                        Vsel, ps[0:B, 4:5, P:2 * P].to_broadcast([B, B, P]),
                        ident[0:B, 0:B].unsqueeze(2).to_broadcast([B, B, P]), ALU.mult).then_inc(hs["tok"], 1)
                    dve.wait_ge(hs[f"s_in{p}"], 16 * i + 16 + 16)
                    ch.link(nc.vector.tensor_tensor(S0[p], S0[p], Fs.unsqueeze(2).to_broadcast([P, B, P]), ALU.mult))
                    dve.wait_ge(hs["outer"], g + 2)
                    nc.vector.tensor_tensor(S0[p].rearrange("p (a b) v -> p a (b v)", a=2),
                                            S0[p].rearrange("p (a b) v -> p a (b v)", a=2), ps[:, 5:7, :],
                                            ALU.add).then_inc(hs["state"], 1)
            for k in range(heads):
                dve.wait_ge(on["sqrt"], k + 1)
                ch.link(nc.vector.reciprocal(big[:, KD + k, :], big[:, KD + k, :]))
                ch.link(nc.vector.scalar_tensor_tensor(out=h[:, k, :], in0=h[:, k, :],
                                                       scalar=vec[:, GAIN_O + k:GAIN_O + k + 1],
                                                       in1=big[:, KD + k, :], op0=ALU.mult, op1=ALU.mult))
                nc.vector.tensor_tensor(h[:, k, :], h[:, k, :], big[:, 3 * KD + k, :], ALU.mult)\
                    .then_inc(on["out"], 1)

            def residual(name):
                with dve.Fori(0, KD // 2) as i:
                    for p in range(2):
                        c = chunk_base[name] + p
                        dve.wait_ge(chunk_ready, 2 * i + c + 1)
                        xk = halves(row(x, 2 * i + p))
                        nc.vector.tensor_tensor(xk, xk, pair(c), ALU.add).then_inc(chunk_taken[c % 2], 1)
                for p in range(2):
                    dve.wait_ge(chunk_taken[p], taken(p, chunk_base[name] + KD))

            def squared_relu(name):
                with dve.Fori(0, KF // 2) as i:
                    for p in range(2):
                        c = chunk_base[name] + p
                        dve.wait_ge(chunk_ready, 2 * i + c + 1)
                        ch_t = halves(Mz[p])
                        nc.vector.tensor_scalar(ch_t, pair(c), 0.0, None, ALU.max).then_inc(relu_done, 1)
                        dve.wait_ge(relu_done, 2 * i + relu_base[name] + p + 1)
                        nc.vector.tensor_tensor(row(big, 2 * i + p), Mz[p], Mz[p], ALU.mult)\
                            .then_inc(chunk_taken[c % 2], 1)

            residual("out")
            norm_dve("mlp0", h, [(GAIN_MLP, h)])
            squared_relu("up0")
            residual("down0")
            norm_dve("attn", h, [(GAIN_KV, h), (GAIN_MIX + KD, h2)])
            dve.wait_ge(gate_ready, 1)
            nc.vector.tensor_scalar(gT, gT, 0.5, 0.5, ALU.mult, ALU.add).then_inc(gate_done, 1)
            for p in range(2):
                dve.wait_ge(chunk_taken[p], taken(p, chunk_base["nsa_out"]))
            dve.wait_ge(attn_const, 1)
            start_counts(dve, pa, ("cmax", "csum", "max", "es", "ect", "mixed"))
            start_counts(dve, pa, ("ce", "cs", "s", "ts", "tw", "o", "ct", "oc", "ot", "k"))
            for u in range(0, 3 * TT, 2):
                dve.wait_ge(kt_ready, u + 1)
                nc.vector.tensor_copy(kvtok[:, u // 3, 512 * (u % 3):512 * (u % 3) + 512], ps[:, u % 4, :])\
                    .then_inc(kt_taken[0], 1)
            for g in range(2, 4):
                for dup in range(2):
                    m = nc.vector.tensor_copy(KD2[DK * dup:DK * dup + DK, g, :, :],
                                              KVT[DK * (g % 2):DK * (g % 2) + DK, 4 + g // 2:9 + g // 2:4, 0:T])
            m.then_inc(kd_ready, 1)
            dve.wait_ge(kvs_turned, 1)
            nc.vector.tensor_copy(kvs.rearrange("p (c n) -> p c n", c=3), ps[0:B, 4:7, :]).then_inc(kvs_ready, 1)
            dve.wait_ge(gturned, 1)
            nc.vector.tensor_copy(gtok.rearrange("p a n -> p (a n)"), ps[:, 7, 0:TT * 3 * HEADS]).then_inc(gtaken, 1)
            nc.vector.tensor_copy(GS.rearrange("p r b -> p (r b)"), ps[0:HEADS, 7, 192:192 + 3 * B]).then_inc(gtaken, 1)
            for g in range(G):
                for par in range(2):
                    src = QT[DK * par:DK * par + DK, 2 * g:2 * g + 2, T:N].rearrange("p c b -> p b c")
                    lo = HPG * g + par
                    r = DK * (g % 2)
                    ch.add(nc.vector.tensor_scalar(QP[r:r + DK, :, g // 2, lo:lo + 3:2], src, SCALE, None, ALU.mult))
                    ch.add(nc.vector.tensor_scalar(QZ[:, :, g, lo:lo + 3:2], src, SCALE, None, ALU.mult))
            ch.link(nc.vector.tensor_copy(KN[:], KVT[:, 4:6, T:N]))
            dve.wait_ge(pc["pe_turned"], 1)
            nc.vector.tensor_copy(pe_cols.rearrange("p a k -> p (a k)"), ps[:, 4, 0:32]).then_inc(pc["pe_cols"], 1)
            dve.wait_ge(pc["bias_ready"], 1)
            nc.vector.tensor_copy(cbias[0:DK, :], ps[0:DK, 5, 0:2]).then_inc(pc["bias"], 1)
            for u in range(1, 8, 2):
                dve.wait_ge(pc["turned"], u + 1)
                if u >= 2:
                    dve.wait_ge(pc["mul"], u - 1)
                nc.vector.tensor_copy(TK[1].rearrange("p (g s) -> p g s", g=G)[:, :, 0:T // HT],
                                      ps[:, 1, :].rearrange("p (g s) -> p g s", g=G)[:, :, 0:T // HT])\
                    .then_inc(pc["ev1"], 1)
            dve.wait_ge(pc["bias"], 1)
            for kv in range(2):
                dve.wait_ge(pc["mul"], 4 * kv + 4)
                nc.vector.tensor_scalar(At[:, G * kv:G * kv + G, 0:T // SUB],
                                        ps[0:DK, 2 + kv, 0:G * T // SUB].rearrange("p (g s) -> p g s", g=G),
                                        cbias[0:DK, kv:kv + 1], None, ALU.add).then_inc(pc["ab_a"], 1)
            dve.wait_ge(pc["ab_a"], 2)
            dve.wait_ge(pc["ab_b"], 2)
            nc.vector.tensor_tensor(Zp, At[:, :, 0:NB_P], Bt[:, :, 1:NB_P + 1], ALU.add).then_inc(pc["z"], 1)
            dve.wait_ge(pc["tanh"], 1)
            nc.vector.scalar_tensor_tensor(out=Hp, in0=Hp, scalar=1.0, in1=Zp, op0=ALU.add, op1=ALU.mult).then_inc(pc["h"], 1)
            dve.wait_ge(pc["kc"], 1)
            nc.vector.tensor_scalar(Vc, ps[0:NB_P, 5, 0:GD], 0.5, None, ALU.mult).then_inc(pc["vc_taken"], 1)
            dve.wait_ge(kd_ready, 3)
            dve.wait_ge(gtaken, 2)
            with ch.loop(G, 1 + 16 * 2 + 4 * 3 + 4 * 7) as g:
                dve.wait_ge(pa["o"], g * 16 + 1)
                dve.wait_ge(pa["oc"], g * TT + 1)
                dve.sem_inc(passed, 1)
                ch.add(nc.vector.tensor_copy(gg, gtok.rearrange("p a (r j) -> p a r j", r=3)[:, :, :, ds(g * HPG, HPG)]))
                nc.vector.tensor_copy(Vc_g, Vc[:, ds(g * DK, DK)]).then_inc(pa["k"], 1)

                def maxes(u):
                    t, j = u // HPG, u % HPG
                    if j == 0:
                        dve.wait_ge(pa["cs"], g * TT + t + 2)
                        dve.wait_ge(pa["ct"], g * TT + t + 1)
                        ch.link(nc.vector.tensor_tensor(
                            Scm[0], ps[:, 7, 0:32 * HPG].rearrange("p (j s) -> p j s", j=HPG)[:, :, 0:NB_P],
                            cm_add[:, t:t + 1, :].to_broadcast([P, HPG, NB_P]), ALU.add))
                        ch.link(nc.vector.tensor_reduce(cmx, Scm[0], AX.X, ALU.max))
                        nc.vector.tensor_tensor(Scm[0], Scm[0], cmx.unsqueeze(2).to_broadcast([P, HPG, NB_P]),
                                                ALU.subtract).then_inc(pa["cmax"], 1)
                    dve.wait_ge(pa["s"], g * 16 + u + 2)
                    sc = ps[:, 2 * (u % 2):2 * (u % 2) + 2, :]
                    ch.link(nc.vector.tensor_tensor(sc[:, :, P * t:P * t + P], sc[:, :, P * t:P * t + P],
                                                    diag.unsqueeze(1).to_broadcast([P, 2, P]), ALU.add))
                    dve.wait_ge(pa["p"], g * 16 + max(u, 1))
                    ch.link(nc.vector.tensor_reduce(nmax[u % 2], sc[:, :, 0:P * (t + 1)], AX.X, ALU.max))
                    nc.vector.tensor_scalar(nmax[u % 2], nmax[u % 2], -1.0, None, ALU.mult).then_inc(pa["max"], 1)
                    if j == 0:
                        dve.wait_ge(pa["cexp"], g * TT + t + 2)
                        ch.link(nc.vector.tensor_tensor(Scm[0], Scm[0], cm_one[:, t:t + 1, :].to_broadcast([P, HPG, NB_P]),
                                                        ALU.mult))
                        nc.vector.tensor_reduce(csum, Scm[0], AX.X, ALU.add).then_inc(pa["csum"], 1)

                maxes(0)
                for u in range(4 * HPG):
                    t, j = u // HPG, u % HPG
                    last = j == HPG - 1
                    if u + 1 < 4 * HPG and not last:
                        maxes(u + 1)
                    dve.wait_ge(pa["ts"], g * 16 + u + 2)
                    dve.wait_ge(pa["o"], g * 16 + max(u, 1))
                    nc.vector.tensor_copy(PT[u % 2][:, 0, 0:t + 1, :],
                                          ps[:, 4, 0:P * (t + 1)].rearrange("p (s t) -> p s t", t=P)).then_inc(pa["es"], 1)
                    if last:
                        dve.wait_ge(pa["ct"], g * TT + t + 2)
                        nc.vector.tensor_copy(PcT, ps[0:NB_P, 4, :]).then_inc(pa["ect"], 1)
                        dve.wait_ge(pa["csum"], g * TT + t + 2)
                        dve.wait_ge(pa["p"], g * 16 + u + 2)
                        ch.add(nc.vector.tensor_scalar(wts[:, 0, :], csum, TINY, None, ALU.max))
                        ch.link(nc.vector.tensor_scalar(wts[:, 1:3, :], sums, TINY, None, ALU.max))
                        ch.link(nc.vector.reciprocal(wts, wts))
                        ch.link(nc.vector.tensor_tensor(wts, wts, gg[:, t, :, :], ALU.mult))
                        dve.wait_ge(pa["o"], g * 16 + u + 2)
                        dve.wait_ge(pa["oc"], g * TT + t + 2)
                        dve.wait_ge(pa["ot"], g * TT + t + 1)
                        ch.add(nc.vector.tensor_tensor(
                            mix[:, 0, :, :], ps[:, 7, 256:512].rearrange("p (j d) -> p j d", j=HPG),
                            wts[:, 0, :].unsqueeze(2).to_broadcast([P, HPG, DK]), ALU.mult))
                        ch.link(nc.vector.tensor_tensor(
                            mix[:, 1:3, :, :].rearrange("p r j d -> p (r j) d"),
                            ps[:, 6, :].rearrange("p (j d) -> p j d", d=DK),
                            wts[:, 1:3, :].rearrange("p r j -> p (r j)").unsqueeze(2).to_broadcast([P, 2 * HPG, DK]),
                            ALU.mult))
                        ch.link(nc.vector.tensor_tensor(mix[:, 0, :, :], mix[:, 0, :, :], mix[:, 1, :, :], ALU.add))
                        nc.vector.tensor_tensor(otok, mix[:, 0, :, :], mix[:, 2, :, :], ALU.add).then_inc(pa["mixed"], 1)
                        if u + 1 < 4 * HPG:
                            maxes(u + 1)

            dve.wait_ge(pa["h"], G * TT + 1)
            dve.sem_inc(sa["os"], 1)
            dve.wait_ge(attn_const, 2)
            with ch.loop(B, 25) as b:
                hold(dve, sa["os"], b + 1 + past["os"])
                ch.add(nc.vector.tensor_copy(Qp, QP[:, ds(b, 1), :, :].rearrange("p a r h -> p (a r) h")))
                ch.add(nc.vector.tensor_copy(Qz, QZ[:, ds(b, 1), :, :].rearrange("p a r h -> p (a r) h")))
                ch.add(nc.vector.tensor_copy(sw[:, 0:3], GS[:, :, ds(b, 1)].rearrange("p r b -> p (r b)")))
                nc.vector.tensor_copy(Kn, KN[:, :, ds(b, 1)].rearrange("p r b -> p (r b)")).then_inc(sa["own"], 1)

                def evac(u):
                    dve.wait_ge(sa["turned"], b * 26 + u + 2 + past["turned"])
                    dve.wait_ge(sa["mul"], b * 26 + u + past["mul"])
                    nc.vector.tensor_copy(TK[1], ps[:, 1, :]).then_inc(sa["ev1"], 1)

                def part_a(e):
                    dve.wait_ge(sa["mul"], b * 26 + 4 * e + 5 + past["mul"])
                    o = G * (e % 2)
                    nc.vector.tensor_scalar(At[:, o:o + G, 64 * (e // 2):64 * (e // 2) + 64],
                                            ps[0:DK, 2 + e % 2, 0:256].rearrange("p (g s) -> p g s", g=G),
                                            cbias[0:DK, e % 2:e % 2 + 1], None, ALU.add).then_inc(sa["ab_a"], 1)

                for u in range(1, 18, 2):
                    evac(u)
                    if u % 4 == 1 and u >= 5:
                        part_a(u // 4 - 1)
                dve.wait_ge(sa["ab_a"], b * 4 + 5 + past["ab_a"])
                dve.wait_ge(sa["ab_b"], b * 4 + 5 + past["ab_b"])
                nc.vector.tensor_tensor(Zs, At[:, :, 0:NB_S], Bt[:, :, 1:NB_S + 1], ALU.add).then_inc(sa["z"], 1)
                evac(19)
                dve.wait_ge(sa["tanh"], b + 2 + past["tanh"])
                nc.vector.scalar_tensor_tensor(out=Hs, in0=Hs, scalar=1.0, in1=Zs, op0=ALU.add, op1=ALU.mult)\
                    .then_inc(sa["h"], 1)
                evac(21)
                dve.wait_ge(sa["kc"], b + 2 + past["kc"])
                nc.vector.tensor_scalar(VcS, ps[0:NB_S, 3, 0:GD], 0.5, None, ALU.mult).then_inc(sa["vc_taken"], 1)
                evac(23)
                dve.wait_ge(sa["cs"], b + 2 + past["cs"])
                ch.link(nc.vector.tensor_reduce(smax[:, 0:1], ps[0:HEADS, 2, 0:NB_S], AX.X, ALU.max))
                nc.vector.tensor_scalar(smax[:, 0:1], smax[:, 0:1], -1.0, None, ALU.mult).then_inc(sa["cmax"], 1)
                nc.vector.tensor_copy(S[:, PAST:NK], ps[0:HEADS, 2, 240:241]).then_inc(sa["new"], 1)
                dve.wait_ge(sa["cexp"], b + 2 + past["cexp"])
                ch.link(nc.vector.tensor_scalar(ssum[:, 0:1], ssum[:, 0:1], TINY, None, ALU.max))
                ch.link(nc.vector.reciprocal(ssum[:, 0:1], ssum[:, 0:1]))
                nc.vector.tensor_scalar(Pc[:, 0:NB_S], Pc[:, 0:NB_S], ssum[:, 0:1], None, ALU.mult).then_inc(sa["pn"], 1)
                evac(25)
                dve.wait_ge(sa["mul"], b * 26 + 27 + past["mul"])
                ch.link(nc.vector.tensor_reduce(smax[:, 2:3], ps[0:HEADS, 3, :], AX.X, ALU.max))
                nc.vector.tensor_scalar(smax[:, 2:3], smax[:, 2:3], -1.0, None, ALU.mult).then_inc(sa["wmax"], 1)
                dve.wait_ge(sa["pnt"], b + 2 + past["pnt"])
                nc.vector.tensor_copy(PnT, ps[0:NB_S, 2, 128:128 + HEADS]).then_inc(sa["pnt_taken"], 1)
                dve.wait_ge(sa["u"], b + 2 + past["u"])
                nc.vector.tensor_copy(U, ps[0:HEADS, 2, 160:160 + NSLC]).then_inc(sa["u_taken"], 1)
                dve.wait_ge(sa["imp"], b + 2 + past["imp"])
                ch.link(nc.vector.tensor_copy(score, ps[0:HEADS, 2, 200:200 + NSLC]))
                ch.add(nc.vector.memset(score[:, 0:1], FORCED_SCORE))
                ch.link(nc.vector.memset(score[:, NSLC - 2:NSLC], FORCED_SCORE))
                for a_, (src, dst) in enumerate(((score, score2), (score2, score))):
                    dve.sem_inc(passed, 1)
                    ch.link(nc.vector.max(top[a_], src))
                    dve.sem_inc(passed, 1)
                    ch.link(nc.vector.match_replace(dst, top[a_], src, -2.0))
                ch.link(nc.vector.tensor_scalar(madd, score, -1.5, NEG_INF, ALU.is_gt, ALU.mult))
                for q in range(4):
                    v = [a_.rearrange("p (r j i) -> p r j i", r=4, i=8) for a_ in (S[:, 512 * q:512 * q + 512], ps[0:HEADS, 4 + q, :])]
                    jj = 16 * (q // 2)
                    ch.add(nc.vector.tensor_tensor(v[0], v[1], madd[:, jj:jj + 16].unsqueeze(1).unsqueeze(3)
                                                   .to_broadcast([HEADS, 4, 16, 8]), ALU.add))
                ch.settle()
                dve.wait_ge(sa["new"], b + 2 + past["new"])
                ch.link(nc.vector.tensor_reduce(smax[:, 1:2], S[:, 0:NK], AX.X, ALU.max))
                nc.vector.tensor_scalar(smax[:, 1:2], smax[:, 1:2], -1.0, None, ALU.mult).then_inc(sa["smax"], 1)
                dve.wait_ge(sa["wexp"], b + 2 + past["wexp"])
                dve.wait_ge(sa["sexp"], b + 2 + past["sexp"])
                ch.link(nc.vector.tensor_scalar(ssum[:, 1:3], ssum[:, 1:3], TINY, None, ALU.max))
                ch.link(nc.vector.reciprocal(ssum[:, 1:3], ssum[:, 1:3]))
                ch.link(nc.vector.tensor_tensor(sw[:, 1:3], sw[:, 1:3], ssum[:, 1:3], ALU.mult))
                nc.vector.tensor_tensor(Dg, ident[0:HEADS, 0:HEADS].unsqueeze(1).to_broadcast([HEADS, 3, HEADS]),
                                        sw[:, 0:3].unsqueeze(2).to_broadcast([HEADS, 3, HEADS]), ALU.mult)\
                    .then_inc(sa["dg"], 1)
                dve.wait_ge(sa["pt"], b + 2 + past["pt"])
                ch.add(nc.vector.tensor_copy(PTs[:, 0:320], ps[:, 0, 0:320]))
                ch.add(nc.vector.tensor_copy(PTs[0:1, 320:336], ps[0:1, 0, 320:336]))
                nc.vector.tensor_copy(PTs[0:NB_S, 336:352], ps[0:NB_S, 0, 336:352]).then_inc(sa["pt_taken"], 1)
                hold(dve, sa["o"], b + 2 + past["o"])
                nc.vector.tensor_copy(OS[:, ds(b, 1), :, :].rearrange("p b a h -> p (b a h)"), ps[:, 2, 256:256 + 2 * HEADS])\
                    .then_inc(sa["os"], 1)
            dve.wait_ge(sa["os"], B + 1 + past["os"])
            for g in range(G):
                r = DK * (g % 2)
                for par in range(2):
                    lo = HPG * g + par
                    nc.vector.tensor_copy(h[DK * par:DK * par + DK, 2 * g:2 * g + 2, T:N],
                                          OS[r:r + DK, :, g // 2, lo:lo + 3:2].rearrange("p b c -> p c b"))\
                        .then_inc(hready, 1)
            residual("nsa_out")
            norm_dve("mlp1", h, [(GAIN_MLP + KD, h)])
            squared_relu("up1")
            residual("down1")
            norm_dve("final", h, [(GAIN_FINAL, h)])
            for u in range(0, 2 * TT, 2):
                dve.wait_ge(yturned, u + 1)
                nc.vector.tensor_copy(yrows[:, u // 2, 512 * (u % 2):512 * (u % 2) + 512], ps[:, u % 4, :])\
                    .then_inc(ydone[0], 1)
            dve.wait_ge(yturned, 2 * TT + 1)
            nc.vector.tensor_copy(ysrows.rearrange("p (c n) -> p c n", c=2), ps[0:B, 4:6, :]).then_inc(ysdone, 1)


_INS = ["x_prompt", "x_sample", "cache_nsa_kv", "cache_win_kv", "state_hgrn", "page_table", "norm_mix", "norm_mlp",
        "w_mlp_up", "w_mlp_down", "w_hgrn_in", "hgrn_lb_logits", "hgrn_onorm", "w_hgrn_out", "norm_kv", "w_kv",
        "cmp_pe_k", "cmp_w1_k", "cmp_w2_k", "cmp_pe_v", "cmp_w1_v", "cmp_w2_v", "w_nsa_q", "w_nsa_out", "norm_final"]
_OUTS = [(1, 512, 1024), (8, 1, 1024), (1, 512, 4, 4, 64), (8, 1, 4, 4, 64), (1, 512, 2, 4, 64), (8, 512, 2, 4, 64),
         (1, 1, 8, 128, 128), (1, 8, 8, 128, 128)]


def kernel(**inputs):
    import numpy as _np
    import concourse.bacc as _bacc
    from concourse import mybir as _mybir
    from concourse.bass_utils import run_bass_kernel_spmd as _run

    nc = _bacc.Bacc("TRN2", target_bir_lowering=False, num_devices=1)
    arrays, args = {}, {}
    for name in _INS:
        a = _np.ascontiguousarray(inputs[name])
        arrays[f"in_{name}"] = a
        args[name] = nc.dram_tensor(f"in_{name}", a.shape, _mybir.dt.from_np(a.dtype), kind="ExternalInput").ap()
    outs = [nc.dram_tensor(f"out_{i}", s, _mybir.dt.float32, kind="ExternalOutput").ap() for i, s in enumerate(_OUTS)]
    hybrid_step(nc, args, outs)
    r = _run(nc, [arrays], core_ids=[0])
    return tuple(r.results[0][f"out_{i}"] for i in range(len(_OUTS)))
```

```python
from contextlib import ExitStack, contextmanager

import concourse.bass as bass
from concourse import mybir

F32 = mybir.dt.float32
I32 = mybir.dt.int32
ALU = mybir.AluOpType
ACT = mybir.ActivationFunctionType
AX = mybir.AxisListType
ds = bass.ds

P = 128
EPS = 1e-6
NEG_INF = -1e30
TINY = 1e-30
FORCED_SCORE = 1e4


class Chain:

    def __init__(self, eng, sem):
        self.eng, self.sem, self.n, self.turn = eng, sem, 0, 0

    def add(self, ins):
        ins.then_inc(self.sem, 1)
        self.n += 1

    def settle(self):
        self.eng.wait_ge(self.sem, self.turn + self.n)

    def link(self, ins):
        self.add(ins)
        self.settle()

    @contextmanager
    def loop(self, turns, steps):
        start = self.n
        with self.eng.Fori(0, turns) as i:
            self.turn = i * steps
            yield i
        assert self.n - start == steps, (self.n - start, steps)
        self.turn, self.n = 0, start + steps * turns


def hybrid_step(nc, ins, outs):
    x_prompt, x_sample = ins["x_prompt"], ins["x_sample"]
    T = x_prompt.shape[1]
    B = x_sample.shape[0]
    D = x_prompt.shape[2]
    KD = D // P
    N = T + B
    NH = N // 2
    TT = T // P
    heads = ins["state_hgrn"].shape[2]
    FF = ins["w_mlp_up"].shape[2]
    KF = FF // P
    assert heads == KD and N % 2 == 0
    G, DK = ins["w_kv"].shape[1] // 6 // 64, 64
    HEADS = D // DK
    HPG = HEADS // G
    GD = G * DK
    SCALE = DK ** -0.5
    SUB = 16
    PAGE = ins["cache_nsa_kv"].shape[1]
    PAGES = ins["page_table"].shape[1]
    PAST = PAGES * PAGE
    HT = 8
    HALF = P * HT
    NB_P, NB_S = T // SUB - 1, PAST // SUB - 1
    NSLC = PAST // 64 + 1
    assert T // 64 <= 16 and T <= ins["cache_win_kv"].shape[1] and PAST == 2 * HALF

    ctx = ExitStack()
    with ctx:
        def sb(name, shape, dt=F32):
            return ctx.enter_context(nc.sbuf_tensor(name, shape, dt))

        def sem(name):
            return ctx.enter_context(nc.semaphore(name))

        x = sb("x", [P, KD, N])
        h = sb("h", [P, KD, N])
        big = sb("big", [P, 4 * KD, N])
        stream = sb("stream", [P, 4, 8 * 512])
        scratch = sb("scratch", [P, 8736])
        ident = sb("ident", [P, P])
        ones = sb("ones", [P, P])
        eps = sb("eps", [P, 1])
        vec = sb("vec", [P, 64])
        lnb = sb("lnb", [P, 4, KD])
        rstd = sb("rstd", [P, N])
        ps = ctx.enter_context(nc.psum_tensor("ps", [P, 8, 512], F32))

        GAIN_MIX, GAIN_MLP, GAIN_KV, GAIN_FINAL, GAIN_O, LOGITS = 0, 16, 32, 40, 48, 56

        slot = [stream[:, s, :] for s in range(4)]

        def halves(ap):
            return ap.rearrange("p (a t) -> p a t", a=2)

        def pair(c):
            return ps[:, 2 * (c % 2):2 * (c % 2) + 2, 0:NH]

        def row(buf, k):
            return buf[:, ds(k, 1), :].rearrange("p a t -> p (a t)")

        at = [0]

        def cut(n, *shape):
            a = scratch[:, at[0]:at[0] + n]
            at[0] += n
            assert at[0] <= 8736, at[0]
            if len(shape) == 2:
                return a.rearrange("p (a b) -> p a b", a=shape[0])
            return a

        reset = cut(T)
        masks = cut(8 * P, 8, P)
        Fb = cut(N)
        Kb = cut(N)
        Bc = cut(T)
        EB = cut(T)
        Dr = [cut(T) for _ in range(2)]
        Lv = [cut(T) for _ in range(2)]
        AT = cut(T)
        Vs = cut(T)
        vtok = cut(T)
        ktok = cut(T)
        kd = cut(T)
        qd = cut(T)
        at_end = at[0]
        at[0] = at_end - 5 * T
        Mz = [cut(N), cut(N)]
        Nz = [cut(N), cut(N)]
        at[0] = at_end
        St = sb("St", [P, TT, P])
        Er = [slot[2][:, 1024 + T * i:1024 + T * i + T] for i in range(2)]

        Eend, Dend = (slot[2][:, 2048 + T * i:2048 + T * i + T] for i in range(2))
        S0 = [slot[2 + p][:, 0:B * P].rearrange("p (b v) -> p b v", b=B) for p in range(2)]
        small = slot[3]
        Fs, Ks, Vs8, Q8 = (small[:, 1024 + 16 * i:1032 + 16 * i] for i in range(4))
        Ktok8 = small[0:B, 1200:1200 + P]
        Vsel = small[0:B, 1400:1400 + B * P].rearrange("p (b v) -> p b v", b=B)

        KVT = big[:, 0:12, :]
        QT = big[:, 12:20, :]
        h2 = big[:, 20:28, :]
        kvtok = big[:, 20:32, :].rearrange("p k t -> p (k t)")[:, 0:TT * 6 * GD].rearrange("p (a n) -> p a n", a=TT)
        W1 = [big[:, 2 * i:2 * i + 2, :].rearrange("p k t -> p (k t)")[:, 0:8 * P].rearrange("p (k a n) -> p k a n", k=8, a=2)
              for i in range(2)]
        KD2 = slot[2].rearrange("p (g b t) -> p g b t", g=G, b=2)
        psrc = slot[3][0:T // HT, :].rearrange("p (r n) -> p r n", r=HT)
        at[0] = 0
        W2 = [cut(DK)[0:DK, :] for _ in range(2)]
        pe_rows, pe_cols, cbias = cut(2 * P, 2, P), cut(2 * 16, 2, 16), cut(2)
        gT = cut(N)[0:3 * HEADS, :]
        kvs = cut(6 * GD)[0:B, :]
        TK = [cut(512) for _ in range(2)]
        RG = [cut(512, G, P) for _ in range(2)]
        At = cut(2 * G * P)[0:DK, :].rearrange("p (a s) -> p a s", s=P)
        Bt = cut(2 * G * P)[0:DK, :].rearrange("p (a s) -> p a s", s=P)
        QP = cut(B * 2 * HEADS).rearrange("p (b a h) -> p b a h", b=B, a=2)
        QZ = cut(B * G * HEADS)[0:DK, :].rearrange("p (b g h) -> p b g h", b=B, g=G)
        GS = cut(3 * B)[0:HEADS, :].rearrange("p (r b) -> p r b", r=3)
        KN = cut(2 * B, 2, B)
        kcT = cut(G * NB_P, G, NB_P)
        Vc = cut(GD)
        diag = cut(P)
        cm_add, cm_one = cut(TT * NB_P, TT, NB_P), cut(TT * NB_P, TT, NB_P)
        gtok = cut(TT * 3 * HEADS, TT, 3 * HEADS)
        PcT, Vblk = TK[0][:, 0:P], TK[0][:, P:3 * P]
        gg = cut(TT * 3 * HPG).rearrange("p (a r j) -> p a r j", a=TT, r=3)
        nmax = [cut(2) for _ in range(2)]
        sums = [cut(2 * HPG, 2, HPG) for _ in range(2)]
        csum, cmx = cut(HPG), cut(HPG)
        wts = cut(3 * HPG, 3, HPG)
        free_b = big[:, 4:12, :].rearrange("p k t -> p (k t)")
        Pb = [free_b[:, 1024 * i:1024 * i + 1024].rearrange("p (b s) -> p b s", b=2) for i in range(2)]
        Kg, kcg = free_b[:, 3072:4096].rearrange("p (b s) -> p b s", b=2), cut(NB_P)
        PT = [free_b[:, 2048:3072].rearrange("p (b s t) -> p b s t", b=2, s=TT),
              slot[3][:, 1024:2048].rearrange("p (b s t) -> p b s t", b=2, s=TT)]
        qg = slot[3][:, 0:1024].rearrange("p (c t) -> p c t", c=2)
        mix = slot[3][:, 2560:3328].rearrange("p (r j d) -> p r j d", r=3, j=HPG)
        otok = slot[3][:, 3328:3584].rearrange("p (j d) -> p j d", j=HPG)
        Scm_all = slot[3][:, 3584:3584 + P]
        Scm = Scm_all.rearrange("p (j s) -> p j s", j=HPG)[:, :, 0:NB_P]
        Zp = slot[3][0:DK, 0:2 * G * NB_P].rearrange("p (a s) -> p a s", s=NB_P)
        Hp = slot[3][0:DK, 1024:1024 + 2 * G * NB_P].rearrange("p (a s) -> p a s", s=NB_P)
        free_s = big[:, 4:32, :].rearrange("p k t -> p (k t)")
        sat = [0]

        def cut_s(n):
            sat[0] += n
            assert sat[0] <= 28 * N
            return free_s[:, sat[0] - n:sat[0]]

        NK = PAST + 1
        S = cut_s(NK + 7)[0:HEADS, :]
        Sw = cut_s(512)[0:HEADS, :]
        Wt = cut_s(4 * 512).rearrange("p (j n) -> p j n", j=4)
        Zs = cut_s(2 * G * NB_S)[0:DK, :].rearrange("p (a s) -> p a s", s=NB_S)
        Hs = cut_s(2 * G * NB_S)[0:DK, :].rearrange("p (a s) -> p a s", s=NB_S)
        kcS = cut_s(G * NB_S)[0:DK, :].rearrange("p (g s) -> p g s", g=G)
        VcS = cut_s(GD)[0:NB_S, :]
        PTs = cut_s(22 * HEADS)
        PnT = cut_s(HEADS)[0:NB_S, :]
        Pc = cut_s(P)[0:HEADS, :]
        Qp, Qz = cut_s(2 * HEADS).rearrange("p (a h) -> p a h", a=2), cut_s(G * HEADS)[0:DK, :].rearrange("p (g h) -> p g h", g=G)
        Kn, Vn = cut_s(2), cut_s(GD)[0:1, :]
        Msel, Gsel = cut_s(NSLC)[0:NB_S, :], cut_s(HEADS)[0:HEADS, :]
        U, score, score2, madd = (cut_s(NSLC)[0:HEADS, :] for _ in range(4))
        top = [cut_s(8)[0:HEADS, :] for _ in range(2)]
        smax, ssum, sw = (cut_s(4)[0:HEADS, :] for _ in range(3))
        Dg = cut_s(3 * HEADS)[0:HEADS, :].rearrange("p (r h) -> p r h", r=3)
        RGs = RG + [cut_s(512).rearrange("p (g n) -> p g n", g=G) for _ in range(2)]
        Osb = cut_s(B * GD)[0:HEADS, :].rearrange("p (b n) -> p b n", b=B)
        OS = cut_s(B * 2 * HEADS).rearrange("p (b a h) -> p b a h", b=B, a=2)

        x_in, xs_in, vec_in = sem("x_in"), sem("xs_in"), sem("vec_in")
        const_ready = sem("const_ready")
        turned, turn_taken = sem("turned"), sem("turn_taken")
        lb_done = sem("lb_done")
        slab_in = [sem(f"slab_in{s}") for s in range(4)]
        chunk_ready = sem("chunk_ready")
        chunk_taken = [sem(f"chunk_taken{s}") for s in range(2)]
        pool_chain, act_chain, dve_chain = sem("pool_chain"), sem("act_chain"), sem("dve_chain")
        stored = sem("stored")
        relu_done = sem("relu_done")
        relu_base = {"up0": 0, "up1": KF}

        norm = {k: sem("norm_" + k) for k in ("sq", "sum", "sqrt", "out")}
        turn_of = {name: n for n, name in enumerate(("mix0", "mlp0", "attn", "mlp1", "final"))}
        out_count = {"mix0": KD, "mlp0": 2 * KD, "kv": 3 * KD, "attn": 4 * KD, "mlp1": 5 * KD, "final": 6 * KD}
        squares = scratch[:, 0:KD * N].rearrange("p (k t) -> p k t", k=KD)
        squares_in = big[:, 12:12 + KD, :]

        fz_ready, fe_ready = sem("fz_ready"), sem("fe_ready")
        gz_ready, ge_ready = sem("gz_ready"), sem("ge_ready")
        hg = {k: sem("hg_" + k) for k in (
            "scan", "f", "vs", "k", "d", "e", "dend", "eend", "eb", "kd", "lv", "vt", "kt", "vtok", "ktok",
            "prod", "prod_taken", "u", "s", "at", "o", "o_taken", "qd", "s_stored", "take")}
        hs = {k: sem("hs_" + k) for k in (
            "f", "kv", "turned", "tok", "outer", "state", "o", "o_taken", "s_in0", "s_in1", "s_out0", "s_out1")}
        on = {k: sem("on_" + k) for k in ("sq", "sum", "sqrt", "out")}

        passed = sem("passed")

        def hold(eng, s, value):
            eng.wait_ge(s, value)
            eng.sem_inc(passed, 1)

        kt_ready = sem("kt_ready")
        kt_taken = [sem("kt_taken0"), sem("kt_taken1")]
        gate_ready, gate_done, gturned, gtaken = sem("gate_ready"), sem("gate_done"), sem("gturned"), sem("gtaken")
        kvs_turned, kvs_ready, kv_stored, kvs_stored = (sem(n) for n in ("kvs_turned", "kvs_ready", "kv_stored", "kvs_stored"))
        w1_in, small_in, psrc_in = sem("w1_in"), sem("small_in"), sem("psrc_in")
        attn_const, kd_ready = sem("attn_const"), sem("kd_ready")
        pc = {k: sem("pc_" + k) for k in ("rg", "pe_turned", "pe_cols", "bias_ready", "bias", "turned", "ev0", "ev1", "mul",
                                          "ab_a", "ab_b", "z", "tanh", "h", "kc", "kc_taken", "vc_taken")}
        pa = {k: sem("pa_" + k) for k in ("ce", "k", "q", "cs", "cmax", "cexp", "csum", "s", "max", "p", "ts", "tw", "es", "ew",
                                          "o", "ct", "ect", "oc", "mixed", "ot", "h")}
        taken_over = {
            "own": (hg["d"], 7 * heads + 1), "turned": (hg["e"], 7 * heads + 1),
            "ev0": (hg["lv"], 7 * heads + 1), "ev1": (hg["prod"], 8 * heads + 1),
            "mul": (hg["s"], 4 * heads + 1), "ab_a": (hg["prod_taken"], 8 * heads + 4),
            "ab_b": (hg["scan"], heads + 1), "z": (hg["f"], heads + 1), "tanh": (hg["vs"], heads + 1),
            "h": (hg["k"], heads + 1), "kc": (hg["dend"], heads + 1), "kc_taken": (hg["eend"], heads + 1),
            "vc_taken": (hg["eb"], heads + 1), "cs": (hg["kd"], heads + 1), "cmax": (hg["vt"], heads + 1),
            "cexp": (hg["kt"], heads + 1), "pn": (hg["vtok"], heads + 1), "pnt": (hg["ktok"], heads + 1),
            "pnt_taken": (hg["u"], heads + 1), "u": (hg["at"], heads + 1), "u_taken": (hg["o"], heads + 1),
            "imp": (hg["o_taken"], heads + 1), "smax": (hg["qd"], heads + 1), "sexp": (hs["f"], heads + 1),
            "wmax": (hs["kv"], heads + 1), "wexp": (hs["turned"], heads + 1), "new": (hs["tok"], heads + 1),
            "dg": (hs["outer"], heads + 1), "pt": (hs["state"], heads + 1), "pt_taken": (hs["o"], heads + 1),
            "o": (hs["o_taken"], heads + 1),
        }
        sa = {k: s_ for k, (s_, _) in taken_over.items()} | {"os": sem("os_done"), "rg": sem("sa_rg"), "qs": pa["ce"]}
        past = {k: end - 1 for k, (_, end) in taken_over.items()} | {"os": 0, "rg": 0, "qs": G * TT}
        cmp_in = [sem("cmp_in0"), sem("cmp_in1")]
        keys_in, vals_in = sem("keys_in"), sem("vals_in")
        win_in, own_in, vn_in = sem("win_in"), sem("own_in"), sem("vn_in")
        pages_in = sem("pages_in")

        def start_counts(eng, sems, names):
            for name in names:
                eng.sem_inc(sems[name], 1)

        block = ctx.enter_context(nc.Block())

        hready = sem("hready")
        ydone, ysdone = [sem("ydone0"), sem("ydone1")], sem("ysdone")
        yturned = sem("yturned")
        yrows = big[:, 0:8, :].rearrange("p k t -> p (k t)")[:, 0:TT * D].rearrange("p (a n) -> p a n", a=TT)
        ysrows = big[0:B, 8:10, :].rearrange("p k t -> p (k t)")[:, 0:D]
        pages = sb("pages", [1, B * PAGES], I32)
        cmp_slot = [slot[i].rearrange("p (r n) -> p r n", r=HT) for i in range(2)]
        key_slot, val_slot = (slot[2 + i].rearrange("p (a n) -> p a n", a=2 * HT) for i in range(2))

        slabs = []
        chunk_base, slab_base = {}, {}
        chunks = [0]

        def plan(name, w, cols, k_rows, order=None):
            slab_base[name], chunk_base[name] = len(slabs), chunks[0]
            n = -(-w.shape[1] // cols) if order is None else len(order)
            for s in (range(n) if order is None else order):
                c0, c1 = s * cols, min((s + 1) * cols, w.shape[1])
                src = w[:, c0:c1].rearrange("(k p) n -> p k n", p=P)
                chunks[0] += -(-(c1 - c0) // P)
                slabs.append((src, k_rows, c1 - c0, chunks[0]))

        plan("in", ins["w_hgrn_in"][0], 512, KD, order=(2, 3, 6, 7, 0, 1, 4, 5))
        plan("out", ins["w_hgrn_out"][0], 512, KD)
        plan("up0", ins["w_mlp_up"][0], 512, KD)
        plan("down0", ins["w_mlp_down"][0], P, KF)
        wq = ins["w_nsa_q"][0]
        plan("kv", ins["w_kv"], 512, KD)
        plan("gate", wq[:, D:D + 3 * HEADS], 3 * HEADS, KD)
        plan("q", wq[:, 0:D], 512, KD)
        plan("nsa_out", ins["w_nsa_out"][0], 512, KD)
        plan("up1", ins["w_mlp_up"][1], 512, KD)
        plan("down1", ins["w_mlp_down"][1], P, KF)

        def taken(p, n):
            return (n + 1 - p) // 2 + 1

        def slab_slot(j):
            return j % 2

        def slab_count(j):
            return 16 * (j // 2 + 1)

        state = ins["state_hgrn"]
        y_prompt, y_sample, kv_prompt, kv_sample, win_prompt, win_sample, state_prompt, state_sample = outs

        @block.sync
        def _(sp):
            sp.dma_start(big[:, 0:8, :].rearrange("p k t -> p (k t)")[:, 0:TT * D].rearrange("p (a n) -> p a n", a=TT),
                         x_prompt[0].rearrange("(a p) n -> p a n", p=P)).then_inc(x_in, 16)
            sp.dma_start(big[0:B, 8:10, :].rearrange("p k t -> p (k t)")[:, 0:D],
                         x_sample.rearrange("b a n -> (b a) n")).then_inc(xs_in, 16)
            for r, src in ((GAIN_MIX, ins["norm_mix"]), (GAIN_MLP, ins["norm_mlp"])):
                sp.dma_start(big[r:r + 16, 10, 0:P], src.rearrange("l (k n) -> (l k) n", n=P)).then_inc(vec_in, 16)
            for r, src in ((GAIN_KV, ins["norm_kv"]), (GAIN_FINAL, ins["norm_final"]),
                           (GAIN_O, ins["hgrn_onorm"][0]), (LOGITS, ins["hgrn_lb_logits"][0])):
                sp.dma_start(big[r:r + 8, 10, 0:P], src.rearrange("(k n) -> k n", n=P)).then_inc(vec_in, 16)

            def load_slabs(first, last):
                for j in range(first, last):
                    src, k_rows, cols, _ = slabs[j]
                    if j >= 2:
                        sp.wait_ge(chunk_ready, slabs[j - 2][3])
                    dst = slot[slab_slot(j)][:, 0:k_rows * cols].rearrange("p (k n) -> p k n", k=k_rows)
                    sp.dma_start(dst, src).then_inc(slab_in[slab_slot(j)], 16)

            load_slabs(0, slab_base["out"] + 2)
            with sp.Fori(0, heads) as i:
                at_h = sp.snap(i)
                sp.wait_ge(hg["s"], 4 * at_h + 4 + 1)
                sp.dma_start(state_prompt[0, 0, ds(at_h, 1), :, :].rearrange("a k v -> k (a v)"),
                             St[:, TT - 1, :]).then_inc(hg["s_stored"], 16)
            for g in range(heads + 2):
                if g >= 2:
                    sp.wait_ge(hs["state"], g )
                    sp.dma_start(state_sample[0, :, g - 2, :, :].rearrange("b k v -> k b v"), S0[g % 2])\
                      .then_inc(hs[f"s_out{g % 2}"], 16)
                if g < heads:
                    if g >= 2:
                        sp.wait_ge(hs["o"], g )
                        sp.wait_ge(hs[f"s_out{g % 2}"], 16 * (g // 2) + 16)
                    sp.dma_start(S0[g % 2], state[0, :, g, :, :].rearrange("b k v -> k b v"))\
                      .then_inc(hs[f"s_in{g % 2}"], 16)
            sp.wait_ge(hg["s_stored"], 16 * heads + 16)
            load_slabs(slab_base["out"] + 2, slab_base["nsa_out"])
            cache_win = ins["cache_win_kv"]
            W = cache_win.shape[1]
            for b in range(B):
                sp.dma_start(win_sample[b].rearrange("w c g d -> (w c g d)")[0:(W - 1) * 2 * GD].rearrange("(a n) -> a n", a=16),
                             cache_win[b].rearrange("w c g d -> (w c g d)")[2 * GD:W * 2 * GD].rearrange("(a n) -> a n", a=16))\
                  .then_inc(stored, 16)
            sp.dma_start(pages[:], ins["page_table"].rearrange("b n -> (b n)").rearrange("(a n) -> a n", a=1))\
              .then_inc(pages_in, 16)
            sp.wait_ge(kt_taken[0], 6)
            sp.wait_ge(kt_taken[1], 6)
            kv_rows = kv_prompt[0].rearrange("(a p) c g d -> p a (c g d)", p=P)
            sp.dma_start(kv_rows[:, :, 0:2 * GD], kvtok[:, :, 0:2 * GD]).then_inc(kv_stored, 16)
            sp.wait_ge(kvs_ready, 1)
            for i, name in enumerate("kv"):
                sp.dma_start(W2[i], ins["cmp_w2_" + name]).then_inc(small_in, 16)
                sp.dma_start(pe_rows[0:16, i, :], ins["cmp_pe_" + name].rearrange("(k r) d -> k (r d)", r=2))\
                  .then_inc(small_in, 16)
            for i, name in enumerate("kv"):
                for a in range(2):
                    sp.dma_start(W1[i][:, :, a, :], ins["cmp_w1_" + name][a * 1024:a * 1024 + 1024, :]
                                 .rearrange("(k p) n -> p k n", p=P)).then_inc(w1_in, 16)
            sp.wait_ge(kv_stored, 16)
            sp.dma_start(psrc, kv_prompt[0, :, 0:2, :, :].rearrange("(i r) c g d -> i r (c g d)", r=HT))\
              .then_inc(psrc_in, 16)
            sp.dma_start(kv_rows[:, :, 2 * GD:4 * GD], kvtok[:, :, 2 * GD:4 * GD]).then_inc(stored, 16)
            sp.dma_start(win_prompt[0].rearrange("(a p) c g d -> p a (c g d)", p=P), kvtok[:, :, 4 * GD:6 * GD])\
              .then_inc(stored, 16)
            sp.dma_start(kv_sample.rearrange("b a c g d -> (b a) (c g d)"), kvs[:, 0:4 * GD]).then_inc(kvs_stored, 16)
            sp.dma_start(win_sample[:, W - 1, :, :, :].rearrange("b c g d -> b (c g d)"), kvs[:, 4 * GD:6 * GD])\
              .then_inc(kvs_stored, 16)
            sp.wait_ge(pages_in, 16)
            sp.wait_ge(kvs_stored, 32)
            sp.wait_ge(chunk_ready, slabs[slab_base["nsa_out"] - 1][3])
            pool_kv = ins["cache_nsa_kv"]

            def page_numbers(b):
                return [nc.values_load(pages[0:1, ds(b * PAGES + k, 1)], engines=(mybir.EngineType.SP,), min_val=0,
                                       max_val=pool_kv.shape[0] - 1,
                                       skip_runtime_bounds_check_because="a page table holds pages of its pool")
                        for k in range(PAGES)]

            def load_pages(numbers, half, dst, kind, kinds, done):
                for k, page in enumerate(numbers[half * (PAGES // 2):(half + 1) * (PAGES // 2)]):
                    sp.dma_start(dst[16 * k:16 * k + 16], pool_kv[ds(page, 1), :, kind:kind + kinds, :, :]
                                 .rearrange("a (i r) c g d -> (a i) r (c g d)", r=HT)).then_inc(done, 16)

            def load_compressed(b, numbers):
                for half in range(2):
                    hold(sp, sa["rg"], b * 16 - 8 + 8 * half + 1 + past["rg"])
                    load_pages(numbers, half, cmp_slot[half], 0, 2, cmp_in[half])

            def load_keys(numbers):
                for half in range(2):
                    load_pages(numbers, half, key_slot[:, HT * half:HT * half + HT, :], 2, 1, keys_in)

            def load_rest(b, numbers):
                sp.dma_start(Vn, kv_sample[ds(b, 1), 0, 3, :, :].rearrange("b g d -> b (g d)")).then_inc(vn_in, 16)
                sp.dma_start(Wt, cache_win[ds(b, 1)].rearrange("a (p j) c g d -> (a p) j (c g d)", j=4)).then_inc(win_in, 16)
                for half in range(2):
                    load_pages(numbers, half, val_slot[:, HT * half:HT * half + HT, :], 3, 1, vals_in)
                hold(sp, win_in, b * 16 + 16)
                sp.dma_start(Wt[0:1, 0, :], win_sample[ds(b, 1), W - 1, :, :, :].rearrange("a c g d -> a (c g d)"))\
                  .then_inc(own_in, 16)

            sp.wait_ge(pc["rg"], 8)
            numbers = page_numbers(0)
            for half in range(2):
                load_pages(numbers, half, cmp_slot[half], 0, 2, cmp_in[half])
            sp.wait_ge(sa["os"], 1 + past["os"])
            load_keys(numbers)
            load_rest(0, numbers)
            load_compressed(1, page_numbers(1))

            def load_sample(b, last):
                numbers = page_numbers(b)
                hold(sp, sa["turned"], b * 26 - 10 + 8 + 1 + past["turned"])
                load_keys(numbers)
                if not last:
                    load_compressed(b + 1, page_numbers(b + 1))
                hold(sp, sa["os"], b + 1 + past["os"])
                load_rest(b, numbers)

            with sp.Fori(0, B - 2) as b:
                load_sample(b + 1, False)
            load_sample(B - 1, True)
            sp.wait_ge(sa["rg"], B * 16 + 1)
            load_slabs(slab_base["nsa_out"], len(slabs))
            for half in range(2):
                for p in range(2):
                    sp.wait_ge(ydone[p], TT // 2 * (half + 1))
                sp.dma_start(y_prompt[0].rearrange("(a p) n -> p a n", p=P)[:, :, D // 2 * half:D // 2 * half + D // 2],
                             yrows[:, :, D // 2 * half:D // 2 * half + D // 2]).then_inc(stored, 16)
            sp.wait_ge(ysdone, 1)
            sp.dma_start(y_sample.rearrange("b a n -> (b a) n"), ysrows).then_inc(stored, 16)
            for p in range(2):
                sp.wait_ge(hs[f"s_out{p}"], 16 * heads // 2 + 16)
            sp.wait_ge(stored, 16 * (B + 5))

        @block.gpsimd
        def _(pool):
            ch = Chain(pool, pool_chain)
            start_counts(pool, hg, ("kd", "lv", "qd"))
            start_counts(pool, sa, ("rg",))
            ch.add(nc.gpsimd.memset(ident[:], 0.0))
            ch.add(nc.gpsimd.memset(eps[:], EPS))
            ch.add(nc.gpsimd.memset(masks, 1.0))
            ch.add(nc.gpsimd.memset(AT, 0.0))
            ch.add(nc.gpsimd.memset(reset, 1.0))
            ch.add(nc.gpsimd.memset(ones[:], 1.0))
            ch.settle()
            ch.add(nc.gpsimd.affine_select(out=ident[:], in_=ident[:], compare_op=ALU.not_equal, fill=1.0, base=0,
                                           pattern=[[-1, P]], channel_multiplier=1))
            ch.add(nc.gpsimd.memset(reset.rearrange("p (c t) -> p c t", c=TT)[:, :, 0:1], 0.0))
            ch.settle()
            pool.sem_inc(const_ready, 1)
            for l in range(7):
                m = 64 >> l
                v = masks[:, l, :].rearrange("p (j u) -> p j u", u=2 * m)
                nb = P // (2 * m)
                for base, pat, mul in ((0, [[-2 * m, nb], [0, 2 * m]], 1),
                                       (m - 1, [[2 * m, nb], [0, 2 * m]], -1),
                                       (-m, [[0, nb], [1, 2 * m]], 0)):
                    ch.link(nc.gpsimd.affine_select(out=v, in_=v, compare_op=ALU.is_ge, fill=0.0, base=base,
                                                    pattern=pat, channel_multiplier=mul))
            ch.add(nc.gpsimd.affine_select(out=masks[:, 7, :], in_=masks[:, 7, :], compare_op=ALU.is_equal, fill=0.0,
                                           base=0, pattern=[[-1, P]], channel_multiplier=1))
            ch.settle()
            pool.sem_inc(const_ready, 1)

            with pool.Fori(0, heads) as i:
                q = row(big, i)[:, 0:T]
                pool.wait_ge(hg["k"], i + 2)
                pool.wait_ge(hg["eend"], i + 2)
                pool.wait_ge(hg["kt"], i + 1)
                nc.gpsimd.tensor_tensor(kd, Kb[:, 0:T], Eend, ALU.mult).then_inc(hg["kd"], 1)
                for l in range(7):
                    m = 64 >> l
                    ev = Er[l % 2].rearrange("p (j a u) -> p j a u", a=2, u=m)
                    lv = Lv[l % 2].rearrange("p (j a u) -> p j a u", a=2, u=m)
                    kv = Kb[:, 0:T].rearrange("p (j a u) -> p j a u", a=2, u=m)
                    qv = q.rearrange("p (j a u) -> p j a u", a=2, u=m)
                    pool.wait_ge(hg["e"], i * 7 + l + 2)
                    pool.wait_ge(hg["prod"], i * 8 + (l if l >= 2 else 0) + 1)
                    nc.gpsimd.tensor_tensor(lv[:, :, 0, :], kv[:, :, 0, :], ev[:, :, 0, :], ALU.mult)
                    nc.gpsimd.tensor_tensor(lv[:, :, 1, :], qv[:, :, 1, :], ev[:, :, 1, :], ALU.mult)\
                        .then_inc(hg["lv"], 1)
                    if l == 2:
                        pool.wait_ge(hg["eb"], i + 2)
                        pool.wait_ge(hg["o"], i + 1)
                        nc.gpsimd.tensor_tensor(qd, q, EB, ALU.mult).then_inc(hg["qd"], 1)

            pool.wait_ge(norm["out"], out_count["attn"])
            pool.wait_ge(norm["sum"], turn_of["attn"] + 1)
            ch.add(nc.gpsimd.memset(diag, 0.0))
            ch.add(nc.gpsimd.memset(cm_one, 1.0))
            ch.add(nc.gpsimd.memset(cm_add, 0.0))
            ch.add(nc.gpsimd.memset(QP[:], 0.0))
            ch.add(nc.gpsimd.memset(QZ[:], 0.0))
            ch.settle()
            ch.add(nc.gpsimd.affine_select(out=diag, in_=diag, compare_op=ALU.is_ge, fill=NEG_INF, base=0,
                                           pattern=[[-1, P]], channel_multiplier=1))
            for m, fill in ((cm_one, 0.0), (cm_add, NEG_INF)):
                ch.add(nc.gpsimd.affine_select(out=m, in_=m, compare_op=ALU.is_ge, fill=fill, base=-(2 * SUB - 1),
                                               pattern=[[P, TT], [-SUB, NB_P]], channel_multiplier=1))
            ch.settle()
            pool.sem_inc(attn_const, 1)
            def regroup(src, n, kv, rp, out):
                return nc.gpsimd.tensor_copy(
                    out[0:n].rearrange("p g (r d) -> p g r d", r=2),
                    src[0:n, 2 * rp:2 * rp + 2, kv * GD:kv * GD + GD].rearrange("p r (g d) -> p g r d", g=G))

            pool.wait_ge(psrc_in, 16)
            for u in range(8):
                if u >= 2:
                    pool.wait_ge(pc["turned"], u - 1)
                regroup(psrc, T // HT, u // 4, u % 4, RG[u % 2]).then_inc(pc["rg"], 1)
            pool.wait_ge(pc["kc_taken"], 1)
            pool.wait_ge(pc["vc_taken"], 1)
            pool.wait_ge(kd_ready, 3)
            with pool.Fori(0, G) as g:
                hold(pool, pa["s"], g * 16 + 1)
                hold(pool, pa["cs"], g * TT + 1)
                nc.gpsimd.tensor_copy(Kg[:, 0, :], KD2[:, ds(g, 1), 0, :].rearrange("p a t -> p (a t)"))
                nc.gpsimd.tensor_copy(kcg, kcT[:, ds(g, 1), :].rearrange("p a s -> p (a s)")).then_inc(pa["k"], 1)
            pool.wait_ge(pa["h"], G * TT + 1)
            ch.add(nc.gpsimd.memset(Msel, 1.0))
            ch.add(nc.gpsimd.memset(Gsel, 1.0))
            ch.settle()
            ch.link(nc.gpsimd.affine_select(out=Msel, in_=Msel, compare_op=ALU.is_ge, fill=0.0, base=1,
                                            pattern=[[-4, NSLC]], channel_multiplier=1))
            ch.add(nc.gpsimd.affine_select(out=Msel, in_=Msel, compare_op=ALU.is_ge, fill=0.0, base=3,
                                           pattern=[[4, NSLC]], channel_multiplier=-1))
            gv = Gsel.rearrange("p (g j) -> p g j", g=G)
            ch.link(nc.gpsimd.affine_select(out=gv, in_=gv, compare_op=ALU.is_ge, fill=0.0, base=0,
                                            pattern=[[-HPG, G], [0, HPG]], channel_multiplier=1))
            ch.add(nc.gpsimd.affine_select(out=gv, in_=gv, compare_op=ALU.is_ge, fill=0.0, base=HPG - 1,
                                           pattern=[[HPG, G], [0, HPG]], channel_multiplier=-1))
            ch.settle()
            pool.sem_inc(attn_const, 1)
            def regroups(b):
                for e in range(16):
                    if e % 8 == 0:
                        hold(pool, cmp_in[e // 8], (b + 2) * (16 * (PAGES // 2)))
                    hold(pool, sa["turned"], b * 26 + 16 + (e - 2 if e < 4 else e + 8) + past["turned"])
                    regroup(cmp_slot[e // 8], P, e % 8 // 4, e % 4, RGs[e % 4]).then_inc(sa["rg"], 1)

            regroups(-1)
            with pool.Fori(0, B - 1) as b:
                regroups(b)

        @block.tensor
        def _(pe):
            start_counts(pe, hg, ("vt", "kt", "prod", "u", "o"))
            start_counts(pe, hs, ("turned", "outer", "o"))
            pe.wait_ge(const_ready, 1)
            pe.wait_ge(vec_in, 16 * 6)
            nc.tensor.transpose(ps[:, 7, 0:64], big[0:64, 10, 0:P], ident[0:64, 0:64]).then_inc(turned, 1)
            pe.wait_ge(xs_in, 16)
            xs_rows = big[0:B, 8:10, :].rearrange("p k t -> p (k t)")
            for k in range(KD):
                m = nc.tensor.transpose(ps[:, 6, B * k:B * k + B], xs_rows[:, P * k:P * k + P], ident[0:B, 0:B])
            m.then_inc(turned, 1)
            pe.wait_ge(x_in, 16)
            x_rows = big[:, 0:8, :].rearrange("p k t -> p (k t)")[:, 0:TT * D].rearrange("p (a n) -> p a n", a=TT)
            for k in range(KD):
                if k >= 4:
                    pe.wait_ge(turn_taken, 2 + k - 3)
                for a in range(TT):
                    m = nc.tensor.transpose(ps[:, k % 4, P * a:P * a + P], x_rows[:, a, P * k:P * k + P], ident[:])
                m.then_inc(turned, 1)

            def norm_sum(name, sq):
                n = turn_of[name]
                for k in range(KD):
                    pe.wait_ge(norm["sq"], n * KD + k + 1)
                    for a in range(2):
                        m = nc.tensor.matmul(ps[:, 6 + a, 0:NH], ones[:], sq[:, k, NH * a:NH * a + NH],
                                             start=(k == 0), stop=(k == KD - 1))
                m.then_inc(norm["sum"], 1)

            def chunk_products(slab, cols, k_rows, rhs, c_local, c, before):
                pe.wait_ge(chunk_taken[c % 2], before + c // 2 + 1)
                w = slab[:, 0:k_rows * cols].rearrange("p (k n) -> p k n", k=k_rows)
                n1 = min(P, cols - P * c_local)
                for a in range(2):
                    for k in range(k_rows):
                        m = nc.tensor.matmul(pair(c)[0:n1, a, :], w[:, k, P * c_local:P * c_local + n1],
                                             rhs[:, k, NH * a:NH * a + NH], start=(k == 0), stop=(k == k_rows - 1))
                m.then_inc(chunk_ready, 1)

            def dense(name, count, rhs, k_rows, cols, turns=1):
                per = count // turns
                c_slab = -(-cols // P)
                c_per = c_slab * per

                def body(i):
                    for s in range(per):
                        j = slab_base[name] + s
                        got = slab_count(j)
                        pe.wait_ge(slab_in[slab_slot(j)], got if i is None else i * (16 * per // 2) + got)
                        for n in range(c_slab):
                            c = chunk_base[name] + s * c_slab + n
                            chunk_products(slot[slab_slot(j)], cols, k_rows, rhs, n, c,
                                           0 if i is None else i * (c_per // 2))
                if turns == 1:
                    body(None)
                else:
                    assert per % 2 == 0 and c_per % 2 == 0
                    with pe.Fori(0, turns) as i:
                        body(i)

            norm_sum("mix0", squares_in)
            pe.wait_ge(norm["out"], out_count["mix0"])
            dense("in", 8, h, KD, 512, turns=4)

            pe.wait_ge(chunk_taken[0], 16 + 1)
            pe.wait_ge(chunk_taken[1], 16 + 1)
            pe.wait_ge(const_ready, 2)
            with pe.Fori(0, heads) as i:
                pe.wait_ge(hg["vs"], i + 2)
                pe.wait_ge(hg["vtok"], i + 1)
                for c in range(TT):
                    m = nc.tensor.transpose(ps[:, 4, P * c:P * c + P], Vs[:, P * c:P * c + P], ident[:])
                m.then_inc(hg["vt"], 1)
                pe.wait_ge(hg["k"], i + 2)
                pe.wait_ge(hg["prod_taken"], i * 8 + 1)
                for c in range(TT):
                    m = nc.tensor.matmul(ps[:, 0, P * c:P * c + P], Kb[:, P * c:P * c + P],
                                         row(big, i)[:, P * c:P * c + P], start=True, stop=True)
                m.then_inc(hg["prod"], 1)
                pe.wait_ge(hg["kd"], i + 2)
                pe.wait_ge(hg["ktok"], i + 1)
                for c in range(TT):
                    m = nc.tensor.transpose(ps[:, 5, P * c:P * c + P], kd[:, P * c:P * c + P], ident[:])
                m.then_inc(hg["kt"], 1)
                for l in range(7):
                    pe.wait_ge(hg["lv"], i * 7 + l + 2)
                    pe.wait_ge(hg["prod_taken"], i * 8 + l + 2)
                    for c in range(TT):
                        m = nc.tensor.matmul(ps[:, (l + 1) % 4, P * c:P * c + P], Lv[l % 2][:, P * c:P * c + P],
                                             Lv[l % 2][:, P * c:P * c + P], start=True, stop=True)
                    m.then_inc(hg["prod"], 1)
                    if l == 1:
                        pe.wait_ge(hg["vtok"], i + 2)
                        pe.wait_ge(hg["ktok"], i + 2)
                        pe.wait_ge(hg["s"], i * 4 + 1)
                        for c in range(TT):
                            m = nc.tensor.matmul(ps[:, 6, P * c:P * c + P], ktok[:, P * c:P * c + P],
                                                 vtok[:, P * c:P * c + P], start=True, stop=True)
                        m.then_inc(hg["u"], 1)
                pe.wait_ge(hg["o_taken"], i + 1)
                pe.wait_ge(hg["at"], i + 2)
                pe.wait_ge(hg["qd"], i + 2)
                pe.wait_ge(hg["s"], i * 4 + 4 + 1)
                for c in range(TT):
                    m = nc.tensor.matmul(ps[:, 7, P * c:P * c + P], vtok[:, P * c:P * c + P],
                                         AT[:, P * c:P * c + P], start=True, stop=(c == 0))
                    if c:
                        m = nc.tensor.matmul(ps[:, 7, P * c:P * c + P], St[:, c - 1, :],
                                             qd[:, P * c:P * c + P], start=False, stop=True)
                m.then_inc(hg["o"], 1)

            with pe.Fori(0, heads // 2) as i:
                for p in range(2):
                    g = 2 * i + p
                    pe.wait_ge(hs["kv"], g + 2)
                    nc.tensor.transpose(ps[0:B, 4, 0:P], Ks, ident[:])
                    nc.tensor.transpose(ps[0:B, 4, P:2 * P], Vs8, ident[:]).then_inc(hs["turned"], 1)
                    pe.wait_ge(on["sq"], g + 1)
                    nc.tensor.matmul(ps[:, p, 0:T], ones[:], row(big, KD + g)[:, 0:T], start=True, stop=True)\
                        .then_inc(on["sum"], 1)
                    pe.wait_ge(hs["tok"], g + 2)
                    for a in range(2):
                        m = nc.tensor.matmul(ps[:, 5 + a, 0:4 * P], Ktok8,
                                             Vsel[:, 4 * a:4 * a + 4, :].rearrange("p b v -> p (b v)"),
                                             start=True, stop=True)
                    m.then_inc(hs["outer"], 1)
                    pe.wait_ge(hs["state"], g + 2)
                    pe.wait_ge(hs["o_taken"], g + 1)
                    for b in range(B):
                        m = nc.tensor.matmul(ps[:, 7, b:b + 1], S0[p][:, b, :], Q8[:, b:b + 1],
                                             start=True, stop=True)
                    m.then_inc(hs["o"], 1)

            pe.wait_ge(on["sq"], heads + 1)
            nc.tensor.matmul(ps[:, 2, 0:heads * B].rearrange("p (k b) -> p k b", k=heads), ones[:],
                             big[:, KD:2 * KD, T:N], start=True, stop=True).then_inc(on["sum"], 1)
            pe.wait_ge(on["out"], heads + 1)
            dense("out", 2, h, KD, 512)
            norm_sum("mlp0", squares)
            pe.wait_ge(norm["out"], out_count["mlp0"])
            dense("up0", 8, h, KD, 512, turns=4)
            for c in range(2):
                pe.wait_ge(chunk_taken[c], chunk_base["down0"] // 2 + 1)
            dense("down0", 8, big, KF, P, turns=4)

            norm_sum("attn", squares)
            pe.wait_ge(norm["out"], out_count["kv"])
            dense("kv", 3, h, KD, 512)
            pe.wait_ge(norm["out"], out_count["attn"])
            dense("gate", 1, h2, KD, 3 * HEADS)
            dense("q", 2, h2, KD, 512)
            n_chunks = chunk_base["nsa_out"]
            for p in range(2):
                pe.wait_ge(chunk_taken[p], taken(p, n_chunks))
            for u in range(3 * TT):
                a, cg = u // 3, u % 3
                if u >= 4:
                    pe.wait_ge(kt_taken[u % 2], (u - 4) // 2 + 1)
                for c in range(4):
                    m = nc.tensor.transpose(ps[:, u % 4, P * c:P * c + P], KVT[:, 4 * cg + c, P * a:P * a + P], ident[:])
                m.then_inc(kt_ready, 1)
            for c in range(12):
                m = nc.tensor.transpose(ps[0:B, 4 + c // 4, P * (c % 4):P * (c % 4) + P], KVT[:, c, T:N], ident[:])
            m.then_inc(kvs_turned, 1)
            pe.wait_ge(gate_done, 1)
            for a in range(TT):
                nc.tensor.transpose(ps[:, 7, 3 * HEADS * a:3 * HEADS * a + 3 * HEADS], gT[:, P * a:P * a + P],
                                    ident[0:3 * HEADS, 0:3 * HEADS])
            for r in range(3):
                m = nc.tensor.matmul(ps[0:HEADS, 7, 192 + B * r:192 + B * r + B],
                                     ident[0:3 * HEADS, HEADS * r:HEADS * r + HEADS], gT[:, T:N], start=True, stop=True)
            m.then_inc(gturned, 1)

            def comp_turn(src, n, bank):
                for g in range(G):
                    m = nc.tensor.transpose(ps[:, bank, P * g:P * g + n], src[0:n, g, :], ident[0:n, 0:n])
                return m

            def comp_mul(tk, n, kv, rp, bank):
                for par in range(2):
                    kk = 4 * par + rp
                    m = nc.tensor.matmul(ps[:, bank, 0:G * n // 2], W1[kv][:, kk, :, :].rearrange("p a n -> p (a n)"),
                                         tk.rearrange("p (g s a) -> p g s a", g=G, a=2)[:, :, 0:n // 2, par],
                                         start=(rp == 0 and par == 0), stop=(rp == 3 and par == 1),
                                         skip_group_check=True)
                return m

            pe.wait_ge(small_in, 64)
            pe.wait_ge(kvs_ready, 1)
            for i in range(2):
                m = nc.tensor.transpose(ps[:, 4, 16 * i:16 * i + 16], pe_rows[0:16, i, :], ident[0:16, 0:16])
            m.then_inc(pc["pe_turned"], 1)
            pe.wait_ge(pc["pe_cols"], 1)
            pe.wait_ge(w1_in, 64)
            for i in range(2):
                for k in range(16):
                    m = nc.tensor.matmul(ps[0:DK, 5, i:i + 1], W1[i][:, k % 8, k // 8, :], pe_cols[:, i, k:k + 1],
                                         start=(k == 0), stop=(k == 15))
            m.then_inc(pc["bias_ready"], 1)
            n_p = T // HT
            pe.wait_ge(psrc_in, 16)
            for p in range(2):
                pe.wait_ge(kt_taken[p], 6)
            for u in range(9):
                if u < 8:
                    if u >= 2:
                        pe.wait_ge(pc[f"ev{u % 2}"], (u - 2) // 2 + 1)
                    pe.wait_ge(pc["rg"], u + 1)
                    comp_turn(RG[u % 2], n_p, u % 2).then_inc(pc["turned"], 1)
                if u:
                    v = u - 1
                    pe.wait_ge(pc[f"ev{v % 2}"], v // 2 + 1)
                    comp_mul(TK[v % 2], n_p, v // 4, v % 4, 2 + v // 4).then_inc(pc["mul"], 1)
            pe.wait_ge(pc["h"], 1)
            nc.tensor.matmul(ps[0:DK, 4, 0:G * NB_P], W2[0], Hp[:, 0:G, :].rearrange("p g s -> p (g s)"), start=True, stop=True)
            for g in range(G):
                m = nc.tensor.matmul(ps[0:NB_P, 5, DK * g:DK * g + DK], Hp[:, G + g, :], W2[1], start=True, stop=True)
            m.then_inc(pc["kc"], 1)

            pe.wait_ge(kd_ready, 3)
            pe.wait_ge(gtaken, 2)
            with pe.Fori(0, G) as g:
                pe.wait_ge(pa["k"], g * 2 + 3)
                hold(pe, pa["q"], g + 2)

                def scores(u):
                    t, j = u // HPG, u % HPG
                    o, w = DK * (j % 2), P * (t + 1)
                    hold(pe, pa["p"], g * 16 + max(u, 1))
                    for br in range(2):
                        m = nc.tensor.matmul(ps[:, 2 * (u % 2) + br, 0:w], qg[o:o + DK, j // 2, P * t:P * t + P],
                                             Kg[o:o + DK, br, 0:w],
                                             start=True, stop=True)
                    m.then_inc(pa["s"], 1)

                def turn(u):
                    t = u // HPG
                    pe.wait_ge(pa["p"], g * 16 + u + 2)
                    for br, (rd, ev) in enumerate((("ts", "es"), ("tw", "ew"))):
                        pe.wait_ge(pa[ev], g * 16 + u + 1)
                        for s_ in range(t + 1):
                            m = nc.tensor.transpose(ps[:, 4 + br, P * s_:P * s_ + P], Pb[u % 2][:, br, P * s_:P * s_ + P],
                                                    ident[:])
                        m.then_inc(pa[rd], 1)

                def values(u):
                    t, j = u // HPG, u % HPG
                    pe.wait_ge(pa["es"], g * 16 + u + 2)
                    pe.wait_ge(pa["ew"], g * 16 + u + 2)
                    if j == 0:
                        hold(pe, pa["mixed"], g * TT + t + 1)
                    for br, f in enumerate((3 * GD, 5 * GD)):
                        for s_ in range(t + 1):
                            m = nc.tensor.matmul(ps[:, 6, 256 * br + DK * j:256 * br + DK * j + DK], PT[u % 2][:, br, s_, :],
                                                 kvtok[:, s_, ds(g * DK + f, DK)], start=(s_ == 0), stop=(s_ == t))
                    m.then_inc(pa["o"], 1)

                def comp_scores(t):
                    hold(pe, pa["h"], g * TT + t + 1)
                    for par in range(2):
                        for j in range(par, HPG, 2):
                            m = nc.tensor.matmul(ps[:, 7, 32 * j:32 * j + NB_P],
                                                 qg[DK * par:DK * par + DK, j // 2, P * t:P * t + P],
                                                 kcg[DK * par:DK * par + DK, :],
                                                 start=True, stop=True)
                        if par == 0:
                            m.then_inc(pa["ce"], 1)
                            hold(pe, pa["ce"], g * TT + t + 2)
                    m.then_inc(pa["cs"], 1)

                def comp_turn_p(t):
                    pe.wait_ge(pa["csum"], g * TT + t + 2)
                    nc.tensor.transpose(ps[:, 7, P:2 * P], Scm_all, ident[:]).then_inc(pa["ct"], 1)

                def comp_values(t):
                    pe.wait_ge(pa["ect"], g * TT + t + 2)
                    nc.tensor.matmul(ps[:, 7, 256:512], PcT, Vblk, start=True, stop=True).then_inc(pa["oc"], 1)

                def out_turn(t):
                    pe.wait_ge(pa["mixed"], g * TT + t + 2)
                    for cc in range(2):
                        m = nc.tensor.transpose(ps[:, 7, P * cc:P * cc + P], otok[:, 2 * cc:2 * cc + 2, :], ident[:])
                    m.then_inc(pa["ot"], 1)

                for u in range(-1, 4 * HPG + 2):
                    if u + 1 < 4 * HPG:
                        scores(u + 1)
                    if 0 <= u < 4 * HPG:
                        turn(u)
                    if u >= HPG and u % HPG == 1:
                        out_turn(u // HPG - 1)
                    if 1 <= u <= 4 * HPG:
                        values(u - 1)
                    if u >= HPG and u % HPG == 0:
                        comp_values(u // HPG - 1)
                    if u < 4 * HPG and u % HPG == 1:
                        comp_scores(u // HPG)
                    if 0 <= u and u % HPG == HPG - 1:
                        comp_turn_p(u // HPG)

            pe.wait_ge(attn_const, 2)

            def sample_turn(b, attend, compress):
                first, last = (0 if attend else 10), (26 if compress else 10)

                def turn_step(v):
                    pe.wait_ge(sa[f"ev{v % 2}"], b * 13 + 8 + v // 2 + 1 + past[f"ev{v % 2}"])
                    if v >= 10:
                        pe.wait_ge(sa["rg"], b * 16 + 16 + v - 10 + 2 + past["rg"])
                        m = comp_turn(RGs[(v - 10) % 4], P, v % 2)
                    elif v < 8:
                        if v in (0, 4):
                            pe.wait_ge(keys_in, b * (16 * PAGES) + 16 * PAGES)
                        for c in range(4):
                            m = nc.tensor.transpose(ps[:, v % 2, P * c:P * c + P],
                                                    key_slot[:, 4 * (v // 2) + c, P * (v % 2):P * (v % 2) + P], ident[:])
                    else:
                        if v == 8:
                            pe.wait_ge(own_in, b * 16 + 16)
                        for c in range(4):
                            m = nc.tensor.transpose(ps[:, v % 2, P * c:P * c + P],
                                                    Wt[:, c, P * (v % 2):P * (v % 2) + P], ident[:])
                    m.then_inc(sa["turned"], 1)

                def mul_step(v):
                    pe.wait_ge(sa[f"ev{v % 2}"], b * 13 + 8 + v // 2 + 2 + past[f"ev{v % 2}"])
                    if v >= 10:
                        e = v - 10
                        if e % 4 == 0:
                            pe.wait_ge(sa["ab_a"], b * 4 + 4 + e // 4 + past["ab_a"])
                            pe.wait_ge(sa["ab_b"], b * 4 + 4 + e // 4 + past["ab_b"])
                        m = comp_mul(TK[v % 2], P, e // 4 % 2, e % 4, 2 + e // 4 % 2)
                    elif v < 8:
                        q, pr = v // 2, v % 2
                        if pr == 0:
                            hold(pe, sa["qs"], b * 4 + q + past["qs"])
                        m = nc.tensor.matmul(ps[0:HEADS, 4 + q % 2, :], Qp[:, pr, :], TK[v % 2], start=(pr == 0), stop=(pr == 1))
                    else:
                        m = nc.tensor.matmul(ps[0:HEADS, 6, :], Qp[:, v % 2, :], TK[v % 2], start=(v == 8), stop=(v == 9))
                    m.then_inc(sa["mul"], 1)

                def compressed_kv():
                    hold(pe, sa["h"], b + 2 + past["h"])
                    hold(pe, sa["os"], b + 1 + past["os"])
                    nc.tensor.matmul(ps[0:DK, 7, 0:G * NB_S], W2[0], Hs[:, 0:G, :].rearrange("p g s -> p (g s)"),
                                     start=True, stop=True)
                    for g in range(G):
                        m = nc.tensor.matmul(ps[0:NB_S, 6, DK * g:DK * g + DK], Hs[:, G + g, :], W2[1],
                                             start=True, stop=True)
                    m.then_inc(sa["kc"], 1)

                def compressed_scores():
                    hold(pe, sa["kc_taken"], b + 2 + past["kc_taken"])
                    for g in range(G):
                        m = nc.tensor.matmul(ps[0:HEADS, 7, 0:NB_S], Qz[:, g, :], kcS[:, g, :],
                                             start=(g == 0), stop=(g == G - 1))
                    for pr in range(2):
                        m = nc.tensor.matmul(ps[0:HEADS, 7, 240:241], Qp[:, pr, :], Kn[:, pr:pr + 1],
                                             start=(pr == 0), stop=(pr == 1))
                    m.then_inc(sa["cs"], 1)

                def turned_probs():
                    hold(pe, sa["pn"], b + 2 + past["pn"])
                    nc.tensor.transpose(ps[0:NB_S, 7, 128:128 + HEADS], Pc[:, 0:NB_S], ident[0:HEADS, 0:HEADS])\
                        .then_inc(sa["pnt"], 1)

                def block_scores():
                    pe.wait_ge(sa["pnt_taken"], b + 2 + past["pnt_taken"])
                    nc.tensor.matmul(ps[0:HEADS, 7, 160:160 + NSLC], PnT, Msel, start=True, stop=True).then_inc(sa["u"], 1)

                def group_scores():
                    hold(pe, sa["u_taken"], b + 2 + past["u_taken"])
                    nc.tensor.matmul(ps[0:HEADS, 7, 200:200 + NSLC], Gsel, U, start=True, stop=True).then_inc(sa["imp"], 1)

                def scaled_probs():
                    pe.wait_ge(sa["dg"], b + 2 + past["dg"])
                    for n in range(16):
                        nc.tensor.matmul(ps[:, 7, HEADS * n:HEADS * n + HEADS], S[:, P * n:P * n + P], Dg[:, 1, :],
                                         start=True, stop=True)
                    for n in range(4):
                        nc.tensor.matmul(ps[:, 7, 256 + HEADS * n:256 + HEADS * n + HEADS], Sw[:, P * n:P * n + P],
                                         Dg[:, 2, :], start=True, stop=True)
                    nc.tensor.matmul(ps[0:1, 7, 320:320 + HEADS], S[:, PAST:PAST + 1], Dg[:, 1, :], start=True, stop=True)
                    nc.tensor.matmul(ps[0:NB_S, 7, 336:336 + HEADS], Pc[:, 0:NB_S], Dg[:, 0, :], start=True, stop=True)\
                        .then_inc(sa["pt"], 1)

                def values():
                    pe.wait_ge(sa["pt_taken"], b + 2 + past["pt_taken"])
                    pe.wait_ge(vn_in, b * 16 + 16)
                    pe.wait_ge(vals_in, b * (16 * PAGES) + 16 * PAGES)
                    o = ps[0:HEADS, 6, 0:GD]
                    for n in range(16):
                        nc.tensor.matmul(o, PTs[:, HEADS * n:HEADS * n + HEADS], val_slot[:, n, :],
                                         start=(n == 0), stop=False)
                    for n in range(4):
                        nc.tensor.matmul(o, PTs[:, 256 + HEADS * n:256 + HEADS * n + HEADS], Wt[:, n, GD:2 * GD],
                                         start=False, stop=False)
                    nc.tensor.matmul(o, PTs[0:1, 320:320 + HEADS], Vn, start=False, stop=False)
                    nc.tensor.matmul(o, PTs[0:NB_S, 336:336 + HEADS], VcS, start=False, stop=True).then_inc(sa["o"], 1)

                after = {3: compressed_kv, 7: compressed_scores, 9: turned_probs, 11: block_scores, 12: group_scores,
                         20: scaled_probs, 22: values}
                turn_step(first)
                for v in range(first, last):
                    if v + 1 < last:
                        turn_step(v + 1)
                    if v == 0:
                        pe.wait_ge(sa["own"], b + 2 + past["own"])
                    mul_step(v)
                    if attend and v in after:
                        after[v]()
                if attend and not compress:
                    for v in sorted(after):
                        if v >= last:
                            after[v]()

            sample_turn(-1, False, True)
            with pe.Fori(0, B - 1) as b:
                sample_turn(b, True, True)
            sample_turn(B - 1, True, False)
            pe.wait_ge(sa["os"], B + 1 + past["os"])
            for b in range(B):
                for pr in range(2):
                    m = nc.tensor.transpose(ps[:, 5, HEADS * (2 * b + pr):HEADS * (2 * b + pr) + HEADS],
                                            Osb[:, b, P * pr:P * pr + P], ident[0:HEADS, 0:HEADS])
            m.then_inc(sa["o"], 1)

            pe.wait_ge(hready, 8)
            pe.wait_ge(pa["h"], G * TT + 1)
            dense("nsa_out", 2, h, KD, 512)
            norm_sum("mlp1", squares)
            pe.wait_ge(norm["out"], out_count["mlp1"])
            dense("up1", 8, h, KD, 512, turns=4)
            for p in range(2):
                pe.wait_ge(chunk_taken[p], taken(p, chunk_base["down1"]))
            dense("down1", 8, big, KF, P, turns=4)
            norm_sum("final", squares)
            for u in range(2 * TT):
                a, cg = u % TT, u // TT
                if a == 0:
                    pe.wait_ge(norm["out"], out_count["final"] - KD // 2 * (1 - cg))
                if u >= 4:
                    pe.wait_ge(ydone[u % 2], (u - 4) // 2 + 1)
                for c in range(4):
                    m = nc.tensor.transpose(ps[:, u % 4, P * c:P * c + P], h[:, 4 * cg + c, P * a:P * a + P], ident[:])
                m.then_inc(yturned, 1)
            for c in range(KD):
                m = nc.tensor.transpose(ps[0:B, 4 + c // 4, P * (c % 4):P * (c % 4) + P], h[:, c, T:N], ident[:])
            m.then_inc(yturned, 1)

        @block.scalar
        def _(act):
            ch = Chain(act, act_chain)
            start_counts(act, hg, ("f", "vs", "e", "eend", "eb", "vtok", "ktok", "o_taken"))
            start_counts(act, hs, ("f", "o_taken"))
            act.wait_ge(lb_done, 1)
            ch.link(nc.scalar.activation(lnb[:, 1, :], lnb[:, 0, :], ACT.Exp))
            act.sem_inc(lb_done, 1)
            act.wait_ge(lb_done, 3)
            ch.link(nc.scalar.activation(lnb[:, 3, :], lnb[:, 2, :], ACT.Ln))
            act.sem_inc(lb_done, 1)

            def gained(gain, out, k):
                nc.scalar.activation(out[:, k, :], x[:, k, :], ACT.Copy, scale=vec[:, gain + k:gain + k + 1])\
                    .then_inc(norm["out"], 1)

            def norm_act(name, sq, wait_row, early=(), late=()):
                n = turn_of[name]
                for k in range(KD):
                    wait_row(k)
                    nc.scalar.activation(sq[:, k, :], x[:, k, :], ACT.Square).then_inc(norm["sq"], 1)
                    for gain, out in early:
                        gained(gain, out, k)
                for gain, out in late:
                    for k in range(KD):
                        gained(gain, out, k)
                act.wait_ge(norm["sum"], n + 1)
                nc.scalar.activation(halves(rstd[:]), ps[:, 6:8, 0:NH], ACT.Sqrt, bias=eps[:], scale=1.0 / D)\
                    .then_inc(norm["sqrt"], 1)

            def added(name):
                def wait_row(k):
                    c = chunk_base[name] + k
                    act.wait_ge(chunk_taken[c % 2], taken(c % 2, c + 1))
                return wait_row

            norm_act("mix0", squares_in, lambda k: act.wait_ge(turn_taken, 3 + k), early=[(GAIN_MIX, h)])
            with ch.loop(4, 2) as i:
                for p in range(2):
                    act.wait_ge(fz_ready, 2 * i + p + 1)
                    ch.link(nc.scalar.activation(Nz[p], Nz[p], ACT.Exp))
                    nc.scalar.activation(Nz[p], Nz[p], ACT.Ln, bias=1.0).then_inc(fe_ready, 1)
            with act.Fori(0, 4) as i:
                for p in range(2):
                    act.wait_ge(gz_ready, 2 * i + p + 1)
                    nc.scalar.activation(Nz[p], Mz[p], ACT.Tanh, scale=0.5).then_inc(ge_ready, 1)
            act.wait_ge(chunk_taken[0], 17)
            act.wait_ge(chunk_taken[1], 17)
            def take_output(i):
                act.wait_ge(hg["o"], i + 2)
                nc.scalar.activation(row(h, i)[:, 0:T], ps[:, 7, :], ACT.Copy).then_inc(hg["o_taken"], 1)

            def head(i, first):
                act.wait_ge(hg["k"], i + 1)
                nc.scalar.activation(Fb, row(big, KD + i), ACT.Exp).then_inc(hg["f"], 1)
                act.wait_ge(hg["vt"], i + 1)
                nc.scalar.activation(Vs, row(big, 2 * KD + i)[:, 0:T], ACT.Copy).then_inc(hg["vs"], 1)
                act.wait_ge(hg["dend"], i + 2)
                act.wait_ge(hg["kd"], i + 1)
                nc.scalar.activation(Eend, Dend, ACT.Exp).then_inc(hg["eend"], 1)
                for l in range(7):
                    act.wait_ge(hg["d"], i * 7 + l + 2)
                    act.wait_ge(hg["lv"], i * 7 + max(l, 1))
                    nc.scalar.activation(Er[l % 2], Dr[l % 2], ACT.Exp).then_inc(hg["e"], 1)
                    if l == 0:
                        if not first:
                            take_output(i - 1)
                        act.wait_ge(hg["s"], i * 4 + 1)
                        act.wait_ge(hg["qd"], i + 1)
                        nc.scalar.activation(EB, Bc, ACT.Exp).then_inc(hg["eb"], 1)
                    if l == 1:
                        act.wait_ge(hg["vt"], i + 2)
                        act.wait_ge(hg["o"], i + 1)
                        nc.scalar.activation(vtok, ps[:, 4, :], ACT.Copy).then_inc(hg["vtok"], 1)
                        act.wait_ge(hg["kt"], i + 2)
                        nc.scalar.activation(ktok, ps[:, 5, :], ACT.Copy).then_inc(hg["ktok"], 1)

            head(0, True)
            with act.Fori(0, heads - 1) as i:
                head(i + 1, False)
            take_output(heads - 1)
            act.wait_ge(hg["o_taken"], heads + 1)
            with act.Fori(0, heads // 2) as i:
                for p in range(2):
                    g = 2 * i + p
                    f_row = row(big, 2 * i + KD + p)
                    act.wait_ge(hs["state"], g + 1)
                    nc.scalar.activation(Fs, f_row[:, T:N], ACT.Exp).then_inc(hs["f"], 1)
                    nc.scalar.activation(f_row[:, 0:T], row(h, 2 * i + p)[:, 0:T], ACT.Square).then_inc(on["sq"], 1)
                    hold(act, on["sum"], g + 1)
                    nc.scalar.activation(f_row[:, 0:T], ps[:, p, 0:T], ACT.Sqrt, bias=eps[:], scale=1.0 / P)\
                        .then_inc(on["sqrt"], 1)
                    hold(act, hs["o"], g + 2)
                    nc.scalar.activation(row(h, 2 * i + p)[:, T:N], ps[:, 7, 0:B], ACT.Copy).then_inc(hs["o_taken"], 1)
            act.wait_ge(hs["o_taken"], heads + 1)
            nc.scalar.activation(big[:, KD:2 * KD, T:N], h[:, :, T:N], ACT.Square).then_inc(on["sq"], 1)
            act.wait_ge(on["sum"], heads + 1)
            nc.scalar.activation(big[:, KD:2 * KD, T:N], ps[:, 2, 0:heads * B].rearrange("p (k b) -> p k b", k=heads),
                                 ACT.Sqrt, bias=eps[:], scale=1.0 / P).then_inc(on["sqrt"], 1)
            norm_act("mlp0", squares, added("out"), late=[(GAIN_MLP, h)])

            def settle_chunks(eng, n):
                for p in range(2):
                    eng.wait_ge(chunk_taken[p], taken(p, n))

            norm_act("attn", squares, added("down0"), early=[(GAIN_KV, h)], late=[(GAIN_MIX + KD, h2)])
            c = chunk_base["gate"]
            act.wait_ge(chunk_taken[c % 2], taken(c % 2, c + 1))
            nc.scalar.activation(gT, gT, ACT.Tanh, scale=0.5).then_inc(gate_ready, 1)
            settle_chunks(act, chunk_base["nsa_out"])
            start_counts(act, pa, ("q", "cexp", "p", "ew", "h"))
            for u in range(1, 3 * TT, 2):
                act.wait_ge(kt_ready, u + 1)
                nc.scalar.activation(kvtok[:, u // 3, 512 * (u % 3):512 * (u % 3) + 512], ps[:, u % 4, :], ACT.Copy)\
                    .then_inc(kt_taken[1], 1)
            for g in range(2):
                for dup in range(2):
                    m = nc.scalar.activation(KD2[DK * dup:DK * dup + DK, g, :, :],
                                             KVT[DK * (g % 2):DK * (g % 2) + DK, 4 + g // 2:9 + g // 2:4, 0:T], ACT.Copy)
            m.then_inc(kd_ready, 1)
            for u in range(0, 8, 2):
                act.wait_ge(pc["turned"], u + 1)
                if u >= 2:
                    act.wait_ge(pc["mul"], u - 1)
                nc.scalar.activation(TK[0].rearrange("p (g s) -> p g s", g=G)[:, :, 0:T // HT],
                                     ps[:, 0, :].rearrange("p (g s) -> p g s", g=G)[:, :, 0:T // HT], ACT.Copy)\
                    .then_inc(pc["ev0"], 1)
            for kv in range(2):
                act.wait_ge(pc["mul"], 4 * kv + 4)
                nc.scalar.activation(Bt[:, G * kv:G * kv + G, 0:T // SUB],
                                     ps[DK:2 * DK, 2 + kv, 0:G * T // SUB].rearrange("p (g s) -> p g s", g=G), ACT.Copy)\
                    .then_inc(pc["ab_b"], 1)
            act.wait_ge(pc["z"], 1)
            nc.scalar.activation(Hp, Zp, ACT.Tanh, scale=0.5).then_inc(pc["tanh"], 1)
            act.wait_ge(pc["kc"], 1)
            for dup in range(2):
                m = nc.scalar.activation(kcT[DK * dup:DK * dup + DK, :, :],
                                         ps[0:DK, 4, 0:G * NB_P].rearrange("p (g s) -> p g s", g=G), ACT.Copy, scale=0.5)
            m.then_inc(pc["kc_taken"], 1)
            act.wait_ge(pc["kc_taken"], 1)
            act.wait_ge(pc["vc_taken"], 1)
            act.wait_ge(kd_ready, 2)
            act.sem_inc(kd_ready, 1)
            with act.Fori(0, G) as g:
                hold(act, pa["s"], g * 16 + 1)
                hold(act, pa["cs"], g * TT + 1)
                nc.scalar.activation(Kg[:, 1, :], KD2[:, ds(g, 1), 1, :].rearrange("p a t -> p (a t)"), ACT.Copy)
                nc.scalar.activation(qg, QT[:, ds(g * 2, 2), 0:T], ACT.Copy, scale=SCALE).then_inc(pa["q"], 1)

                def exps(u):
                    t, j = u // HPG, u % HPG
                    w = P * (t + 1)
                    act.wait_ge(pa["max"], g * 16 + u + 2)
                    act.wait_ge(pa["tw"], g * 16 + max(u, 1))
                    for br in range(2):
                        m = nc.scalar.activation(Pb[u % 2][:, br, 0:w], ps[:, 2 * (u % 2) + br, 0:w], ACT.Exp,
                                                 bias=nmax[u % 2][:, br:br + 1], accum_out=sums[t % 2][:, br, j:j + 1])
                    m.then_inc(pa["p"], 1)

                for u in range(-1, 4 * HPG + 2):
                    t = u // HPG
                    if u >= HPG and u % HPG == 0:
                        act.wait_ge(pa["ct"], g * TT + t + 1)
                        act.wait_ge(pa["oc"], g * TT + t)
                        nc.scalar.activation(PcT, ps[:, 7, P:2 * P], ACT.Copy).then_inc(pa["ect"], 1)
                    if u + 1 < 4 * HPG:
                        exps(u + 1)
                    if 0 <= u < 4 * HPG:
                        act.wait_ge(pa["tw"], g * 16 + u + 2)
                        act.wait_ge(pa["o"], g * 16 + max(u, 1))
                        nc.scalar.activation(PT[u % 2][:, 1, 0:t + 1, :],
                                             ps[:, 5, 0:P * (t + 1)].rearrange("p (s t) -> p s t", t=P), ACT.Copy)\
                            .then_inc(pa["ew"], 1)
                    if u >= HPG and u % HPG == 1:
                        hold(act, pa["ot"], g * TT + t + 1)
                        nc.scalar.activation(h[:, ds(g * 2, 2), P * (t - 1):P * t],
                                             ps[:, 7, 0:2 * P].rearrange("p (c t) -> p c t", c=2), ACT.Copy)\
                            .then_inc(pa["h"], 1)
                    if u < 4 * HPG and u % HPG == 2:
                        act.wait_ge(pa["cmax"], g * TT + t + 2)
                        nc.scalar.activation(Scm, Scm, ACT.Exp).then_inc(pa["cexp"], 1)

            def sample_turn(b, attend, compress):
                def evac(v):
                    act.wait_ge(sa["turned"], b * 26 + 16 + v + 2 + past["turned"])
                    act.wait_ge(sa["mul"], b * 26 + 16 + v + past["mul"])
                    nc.scalar.activation(TK[0], ps[:, 0, :], ACT.Copy).then_inc(sa["ev0"], 1)

                def take_scores(q):
                    act.wait_ge(sa["mul"], b * 26 + 16 + 2 * q + 3 + past["mul"])
                    if q == 0:
                        act.wait_ge(sa["pt"], b + 1 + past["pt"])
                    nc.scalar.activation(S[:, 512 * q:512 * q + 512], ps[0:HEADS, 4 + q % 2, :], ACT.Copy)\
                        .then_inc(sa["qs"], 1)

                def part_b(e):
                    act.wait_ge(sa["mul"], b * 26 + 16 + 10 + 4 * e + 5 + past["mul"])
                    act.wait_ge(sa["z"], b + 2 + past["z"])
                    o = G * (e % 2)
                    nc.scalar.activation(Bt[:, o:o + G, 64 * (e // 2):64 * (e // 2) + 64],
                                         ps[DK:2 * DK, 2 + e % 2, 0:256].rearrange("p (g s) -> p g s", g=G), ACT.Copy)\
                        .then_inc(sa["ab_b"], 1)

                def exp_selected():
                    act.wait_ge(sa["smax"], b + 2 + past["smax"])
                    nc.scalar.activation(S[:, 0:NK], S[:, 0:NK], ACT.Exp, bias=smax[:, 1:2],
                                         accum_out=ssum[:, 1:2]).then_inc(sa["sexp"], 1)

                if attend:
                    evac(0)
                    act.wait_ge(sa["z"], b + 2 + past["z"])
                    nc.scalar.activation(Hs, Zs, ACT.Tanh, scale=0.5).then_inc(sa["tanh"], 1)
                    evac(2)
                    take_scores(0)
                    evac(4)
                    take_scores(1)
                    act.wait_ge(sa["kc"], b + 2 + past["kc"])
                    nc.scalar.activation(kcS.rearrange("p g s -> p (g s)"), ps[0:DK, 7, 0:G * NB_S], ACT.Copy, scale=0.5)\
                        .then_inc(sa["kc_taken"], 1)
                    evac(6)
                    take_scores(2)
                    evac(8)
                    take_scores(3)
                    act.wait_ge(sa["cmax"], b + 2 + past["cmax"])
                    act.wait_ge(sa["new"], b + 2 + past["new"])
                    nc.scalar.activation(Pc[:, 0:NB_S], ps[0:HEADS, 7, 0:NB_S], ACT.Exp, bias=smax[:, 0:1],
                                         accum_out=ssum[:, 0:1]).then_inc(sa["cexp"], 1)
                if compress:
                    evac(10)
                if attend:
                    act.wait_ge(sa["wmax"], b + 2 + past["wmax"])
                    nc.scalar.activation(Sw, ps[0:HEADS, 6, :], ACT.Exp, bias=smax[:, 2:3],
                                         accum_out=ssum[:, 2:3]).then_inc(sa["wexp"], 1)
                if compress:
                    evac(12)
                    evac(14)
                    part_b(0)
                    evac(16)
                    evac(18)
                    part_b(1)
                    evac(20)
                if attend:
                    exp_selected()
                if compress:
                    evac(22)
                    part_b(2)
                    evac(24)
                    part_b(3)

            sample_turn(-1, False, True)
            with act.Fori(0, B - 1) as b:
                sample_turn(b, True, True)
            sample_turn(B - 1, True, False)

            norm_act("mlp1", squares, added("nsa_out"), late=[(GAIN_MLP + KD, h)])
            norm_act("final", squares, added("down1"))
            for u in range(1, 2 * TT, 2):
                act.wait_ge(yturned, u + 1)
                nc.scalar.activation(yrows[:, u % TT, 512 * (u // TT):512 * (u // TT) + 512], ps[:, u % 4, :], ACT.Copy)\
                    .then_inc(ydone[1], 1)

        @block.vector
        def _(dve):
            ch = Chain(dve, dve_chain)
            start_counts(dve, hg, ("scan", "k", "d", "dend", "s", "at"))
            start_counts(dve, hs, ("kv", "tok", "state"))
            dve.sem_inc(hg["s_stored"], 16)
            for p in range(2):
                dve.sem_inc(hs[f"s_in{p}"], 16)
                dve.sem_inc(hs[f"s_out{p}"], 16)
            dve.sem_inc(chunk_taken[0], 1)
            dve.sem_inc(chunk_taken[1], 1)
            dve.sem_inc(hg["prod_taken"], 4)
            dve.wait_ge(turned, 1)
            nc.vector.tensor_copy(vec[:], ps[:, 7, 0:64]).then_inc(turn_taken, 1)
            dve.wait_ge(turned, 2)
            nc.vector.tensor_copy(x[:, :, T:N], ps[:, 6, 0:B * KD].rearrange("p (k b) -> p k b", k=KD))\
                .then_inc(turn_taken, 1)
            for k in range(KD):
                dve.wait_ge(turned, 3 + k)
                nc.vector.tensor_copy(x[:, k, 0:T], ps[:, k % 4, :]).then_inc(turn_taken, 1)
            dve.wait_ge(turn_taken, 1)
            z = vec[:, LOGITS:LOGITS + KD]
            ch.link(nc.vector.tensor_tensor(lnb[:, 0, :], z, z, ALU.subtract))
            dve.sem_inc(lb_done, 1)
            dve.wait_ge(lb_done, 2)
            ch.link(nc.vector.reciprocal(lnb[:, 2, :], lnb[:, 1, :]))
            ch.link(nc.vector.tensor_tensor(lnb[:, 1, :], lnb[:, 1, :], lnb[:, 2, :], ALU.mult))
            ch.link(nc.vector.tensor_tensor(lnb[:, 1, :], lnb[:, 1, :], lnb[:, 1, :], ALU.subtract))
            ch.link(nc.vector.tensor_scalar(lnb[:, 2, :], lnb[:, 1, :], -1.0, 1.0, ALU.mult, ALU.add))
            dve.sem_inc(lb_done, 1)

            def norm_dve(name):
                dve.wait_ge(norm["sqrt"], turn_of[name] + 1)
                ch.link(nc.vector.reciprocal(rstd[:], rstd[:]))

            def scaled(out, bank_pair):
                return nc.vector.tensor_tensor(halves(out), bank_pair, halves(rstd[:]), ALU.mult)

            norm_dve("mix0")
            dve.wait_ge(lb_done, 4)
            with ch.loop(4, 4) as i:
                for p in range(2):
                    dve.wait_ge(chunk_ready, 2 * i + p + 1)
                    ch.link(scaled(Nz[p], pair(p)))
                    dve.sem_inc(chunk_taken[p], 1)
                    ch.link(nc.vector.tensor_scalar(Mz[p], Nz[p], 0.0, None, ALU.min))
                    nc.vector.scalar_tensor_tensor(out=Nz[p], in0=Mz[p], scalar=2.0, in1=Nz[p],
                                                   op0=ALU.mult, op1=ALU.subtract).then_inc(fz_ready, 1)
                    dve.wait_ge(fe_ready, 2 * i + p + 1)
                    nc.vector.scalar_tensor_tensor(out=row(big, 2 * i + KD + p), in0=Mz[p],
                                                   scalar=lnb[:, 3, ds(2 * i + p, 1)], in1=Nz[p],
                                                   op0=ALU.add, op1=ALU.subtract)
            with ch.loop(4, 2) as i:
                for p in range(2):
                    dve.wait_ge(chunk_ready, 2 * i + 8 + p + 1)
                    scaled(Mz[p], pair(p)).then_inc(gz_ready, 1)
                    dve.wait_ge(gz_ready, 2 * i + p + 1)
                    dve.sem_inc(chunk_taken[p], 1)
                    dve.wait_ge(ge_ready, 2 * i + p + 1)
                    ch.link(nc.vector.tensor_scalar(Nz[p], Nz[p], 0.5, 0.5, ALU.mult, ALU.add))
                    nc.vector.tensor_tensor(row(big, 2 * i + 3 * KD + p), Mz[p], Nz[p], ALU.mult)
            for first, c0 in ((0, 16), (2 * KD, 24)):
                with dve.Fori(0, 4) as i:
                    for p in range(2):
                        dve.wait_ge(chunk_ready, 2 * i + c0 + p + 1)
                        scaled(row(big, 2 * i + first + p), pair(p)).then_inc(chunk_taken[p], 1)
            dve.wait_ge(chunk_taken[0], 17)
            dve.wait_ge(chunk_taken[1], 17)
            bc = Bc.rearrange("p (c t) -> p c t", c=TT)
            with ch.loop(heads, 7) as i:
                dve.wait_ge(hg["eb"], i + 1)
                nc.vector.tensor_tensor_scan(Bc, reset, row(big, KD + i)[:, 0:T], 0.0, ALU.mult, ALU.add)\
                    .then_inc(hg["scan"], 1)
                dve.wait_ge(hg["f"], i + 2)
                dve.wait_ge(hg["lv"], i * 7 + 1)
                nc.vector.tensor_scalar(Kb, Fb, -1.0, 1.0, ALU.mult, ALU.add).then_inc(hg["k"], 1)
                dve.wait_ge(hg["scan"], i + 2)
                dve.wait_ge(hg["eend"], i + 1)
                nc.vector.tensor_tensor(Dend.rearrange("p (c t) -> p c t", c=TT),
                                        bc[:, :, P - 1:P].to_broadcast([P, TT, P]), bc, ALU.subtract)\
                    .then_inc(hg["dend"], 1)

                def take(n, mask):
                    dve.wait_ge(hg["prod"], i * 8 + n + 2)
                    if n == 0:
                        dve.wait_ge(hg["o"], i + 1)
                    dve.wait_ge(hg["prod_taken"], i * 8 + 4 + n)
                    dve.sem_inc(hg["take"], 1)
                    nc.vector.copy_predicated(
                        AT.rearrange("p (c t) -> p c t", c=TT),
                        masks[:, mask:mask + 1, :].to_broadcast([P, TT, P]).bitcast(I32),
                        ps[:, n % 4, :].rearrange("p (c t) -> p c t", c=TT)).then_inc(hg["prod_taken"], 1)

                for l in range(7):
                    m = 64 >> l
                    b4 = Bc.rearrange("p (j a u) -> p j a u", a=2, u=m)
                    d4 = Dr[l % 2].rearrange("p (j a u) -> p j a u", a=2, u=m)
                    nb = T // (2 * m)
                    ref = b4[:, :, 0, m - 1:m].to_broadcast([P, nb, m])
                    if l >= 2:
                        dve.wait_ge(hg["e"], i * 7 + l )
                    ch.add(nc.vector.tensor_tensor(d4[:, :, 0, :], ref, b4[:, :, 0, :], ALU.subtract))
                    nc.vector.tensor_tensor(d4[:, :, 1, :], b4[:, :, 1, :], ref, ALU.subtract).then_inc(hg["d"], 1)
                    if l == 0:
                        take(0, 7)
                    if l >= 2:
                        take(l - 1, l - 2)
                    if l == 3:
                        dve.wait_ge(hg["u"], i + 2)
                        dve.wait_ge(hg["eb"], i + 2)
                        dve.wait_ge(hg["s_stored"], i * 16 + 16)
                        u = ps[:, 6, :].rearrange("p (c v) -> p c v", c=TT)
                        nc.vector.tensor_copy(St[:, 0, :], u[:, 0, :]).then_inc(hg["s"], 1)
                        for c in range(1, TT):
                            dve.wait_ge(hg["s"], i * 4 + c + 1)
                            nc.vector.scalar_tensor_tensor(out=St[:, c, :], in0=St[:, c - 1, :],
                                                           scalar=EB[:, P * c + P - 1:P * c + P], in1=u[:, c, :],
                                                           op0=ALU.mult, op1=ALU.add).then_inc(hg["s"], 1)
                take(6, 5)
                take(7, 6)
                dve.wait_ge(hg["prod_taken"], i * 8 + 12)
                dve.sem_inc(hg["at"], 1)
            with ch.loop(heads // 2, 10) as i:
                for p in range(2):
                    g = 2 * i + p
                    dve.wait_ge(hs["f"], g + 2)
                    dve.wait_ge(hs["o"], g + 1)
                    ch.add(nc.vector.tensor_scalar(Ks, Fs, -1.0, 1.0, ALU.mult, ALU.add))
                    ch.add(nc.vector.tensor_copy(Vs8, row(big, 2 * i + 2 * KD + p)[:, T:N]))
                    nc.vector.tensor_copy(Q8, row(big, 2 * i + p)[:, T:N]).then_inc(hs["kv"], 1)
                    dve.wait_ge(hs["turned"], g + 2)
                    nc.vector.tensor_copy(Ktok8, ps[0:B, 4, 0:P])
                    nc.vector.tensor_tensor(
                        Vsel, ps[0:B, 4:5, P:2 * P].to_broadcast([B, B, P]),
                        ident[0:B, 0:B].unsqueeze(2).to_broadcast([B, B, P]), ALU.mult).then_inc(hs["tok"], 1)
                    dve.wait_ge(hs[f"s_in{p}"], 16 * i + 16 + 16)
                    ch.link(nc.vector.tensor_tensor(S0[p], S0[p], Fs.unsqueeze(2).to_broadcast([P, B, P]), ALU.mult))
                    dve.wait_ge(hs["outer"], g + 2)
                    nc.vector.tensor_tensor(S0[p].rearrange("p (a b) v -> p a (b v)", a=2),
                                            S0[p].rearrange("p (a b) v -> p a (b v)", a=2), ps[:, 5:7, :],
                                            ALU.add).then_inc(hs["state"], 1)
                    r_row, o_row = row(big, 2 * i + KD + p)[:, 0:T], row(h, 2 * i + p)[:, 0:T]
                    hold(dve, on["sqrt"], g + 1)
                    ch.link(nc.vector.reciprocal(r_row, r_row))
                    ch.link(nc.vector.scalar_tensor_tensor(out=o_row, in0=o_row, scalar=vec[:, ds(2 * i + GAIN_O + p, 1)],
                                                           in1=r_row, op0=ALU.mult, op1=ALU.mult))
                    nc.vector.tensor_tensor(o_row, o_row, row(big, 2 * i + 3 * KD + p)[:, 0:T], ALU.mult)\
                        .then_inc(on["out"], 1)
            dve.wait_ge(on["sqrt"], heads + 1)
            r8, o8 = big[:, KD:2 * KD, T:N], h[:, :, T:N]
            ch.link(nc.vector.reciprocal(r8, r8))
            ch.link(nc.vector.tensor_tensor(o8, o8, r8, ALU.mult))
            ch.link(nc.vector.tensor_tensor(o8, o8, vec[:, GAIN_O:GAIN_O + heads].unsqueeze(2)
                                            .to_broadcast([P, heads, B]), ALU.mult))
            nc.vector.tensor_tensor(o8, o8, big[:, 3 * KD:4 * KD, T:N], ALU.mult).then_inc(on["out"], 1)

            def residual(name):
                with dve.Fori(0, KD // 2) as i:
                    for p in range(2):
                        c = chunk_base[name] + p
                        dve.wait_ge(chunk_ready, 2 * i + c + 1)
                        xk = halves(row(x, 2 * i + p))
                        nc.vector.tensor_tensor(xk, xk, pair(c), ALU.add).then_inc(chunk_taken[c % 2], 1)
                for p in range(2):
                    dve.wait_ge(chunk_taken[p], taken(p, chunk_base[name] + KD))

            def squared_relu(name):
                with dve.Fori(0, KF // 2) as i:
                    for p in range(2):
                        c = chunk_base[name] + p
                        dve.wait_ge(chunk_ready, 2 * i + c + 1)
                        nc.vector.scalar_tensor_tensor(out=halves(Mz[p]), in0=pair(c), scalar=0.0, in1=halves(rstd[:]),
                                                       op0=ALU.max, op1=ALU.mult).then_inc(relu_done, 1)
                        dve.wait_ge(relu_done, 2 * i + relu_base[name] + p + 1)
                        nc.vector.tensor_tensor(row(big, 2 * i + p), Mz[p], Mz[p], ALU.mult)\
                            .then_inc(chunk_taken[c % 2], 1)

            residual("out")
            norm_dve("mlp0")
            squared_relu("up0")
            residual("down0")
            norm_dve("attn")
            for n in range(21):
                c = chunk_base["kv"] + n
                dve.wait_ge(chunk_ready, c + 1)
                if c == chunk_base["gate"]:
                    m = nc.vector.tensor_tensor(halves(gT), pair(c)[0:3 * HEADS], halves(rstd[0:3 * HEADS]), ALU.mult)
                else:
                    m = scaled(KVT[:, n, :] if n < 12 else QT[:, n - 13, :], pair(c))
                m.then_inc(chunk_taken[c % 2], 1)
            dve.wait_ge(gate_ready, 1)
            nc.vector.tensor_scalar(gT, gT, 0.5, 0.5, ALU.mult, ALU.add).then_inc(gate_done, 1)
            for p in range(2):
                dve.wait_ge(chunk_taken[p], taken(p, chunk_base["nsa_out"]))
            dve.wait_ge(attn_const, 1)
            start_counts(dve, pa, ("cmax", "csum", "max", "es", "ect", "mixed"))
            start_counts(dve, pa, ("ce", "cs", "s", "ts", "tw", "o", "ct", "oc", "ot", "k"))
            for u in range(0, 3 * TT, 2):
                dve.wait_ge(kt_ready, u + 1)
                nc.vector.tensor_copy(kvtok[:, u // 3, 512 * (u % 3):512 * (u % 3) + 512], ps[:, u % 4, :])\
                    .then_inc(kt_taken[0], 1)
            dve.wait_ge(kvs_turned, 1)
            nc.vector.tensor_copy(kvs.rearrange("p (c n) -> p c n", c=3), ps[0:B, 4:7, :]).then_inc(kvs_ready, 1)
            for g in range(2, 4):
                for dup in range(2):
                    m = nc.vector.tensor_copy(KD2[DK * dup:DK * dup + DK, g, :, :],
                                              KVT[DK * (g % 2):DK * (g % 2) + DK, 4 + g // 2:9 + g // 2:4, 0:T])
            m.then_inc(kd_ready, 1)
            dve.wait_ge(gturned, 1)
            nc.vector.tensor_copy(gtok.rearrange("p a n -> p (a n)"), ps[:, 7, 0:TT * 3 * HEADS]).then_inc(gtaken, 1)
            nc.vector.tensor_copy(GS.rearrange("p r b -> p (r b)"), ps[0:HEADS, 7, 192:192 + 3 * B]).then_inc(gtaken, 1)
            for g in range(G):
                for par in range(2):
                    src = QT[DK * par:DK * par + DK, 2 * g:2 * g + 2, T:N].rearrange("p c b -> p b c")
                    lo = HPG * g + par
                    r = DK * (g % 2)
                    ch.add(nc.vector.tensor_scalar(QP[r:r + DK, :, g // 2, lo:lo + 3:2], src, SCALE, None, ALU.mult))
                    ch.add(nc.vector.tensor_scalar(QZ[:, :, g, lo:lo + 3:2], src, SCALE, None, ALU.mult))
            ch.link(nc.vector.tensor_copy(KN[:], KVT[:, 4:6, T:N]))
            dve.wait_ge(pc["pe_turned"], 1)
            nc.vector.tensor_copy(pe_cols.rearrange("p a k -> p (a k)"), ps[:, 4, 0:32]).then_inc(pc["pe_cols"], 1)
            dve.wait_ge(pc["bias_ready"], 1)
            nc.vector.tensor_copy(cbias[0:DK, :], ps[0:DK, 5, 0:2]).then_inc(pc["bias"], 1)
            for u in range(1, 8, 2):
                dve.wait_ge(pc["turned"], u + 1)
                if u >= 2:
                    dve.wait_ge(pc["mul"], u - 1)
                nc.vector.tensor_copy(TK[1].rearrange("p (g s) -> p g s", g=G)[:, :, 0:T // HT],
                                      ps[:, 1, :].rearrange("p (g s) -> p g s", g=G)[:, :, 0:T // HT])\
                    .then_inc(pc["ev1"], 1)
            dve.wait_ge(pc["bias"], 1)
            for kv in range(2):
                dve.wait_ge(pc["mul"], 4 * kv + 4)
                nc.vector.tensor_scalar(At[:, G * kv:G * kv + G, 0:T // SUB],
                                        ps[0:DK, 2 + kv, 0:G * T // SUB].rearrange("p (g s) -> p g s", g=G),
                                        cbias[0:DK, kv:kv + 1], None, ALU.add).then_inc(pc["ab_a"], 1)
            dve.wait_ge(pc["ab_a"], 2)
            dve.wait_ge(pc["ab_b"], 2)
            nc.vector.tensor_tensor(Zp, At[:, :, 0:NB_P], Bt[:, :, 1:NB_P + 1], ALU.add).then_inc(pc["z"], 1)
            dve.wait_ge(pc["tanh"], 1)
            nc.vector.scalar_tensor_tensor(out=Hp, in0=Hp, scalar=1.0, in1=Zp, op0=ALU.add, op1=ALU.mult).then_inc(pc["h"], 1)
            dve.wait_ge(pc["kc"], 1)
            for j in range(HPG):
                ch.add(nc.vector.tensor_scalar(Vc[32 * j:32 * j + NB_P, :], ps[0:NB_P, 5, 0:GD], 0.5, None, ALU.mult))
            ch.settle()
            dve.sem_inc(pc["vc_taken"], 1)
            dve.wait_ge(pc["rg"], 8)
            ch.add(nc.vector.memset(Scm_all, 0.0))
            ch.add(nc.vector.memset(Vblk, 0.0))
            ch.settle()
            dve.wait_ge(kd_ready, 3)
            dve.wait_ge(gtaken, 2)
            with ch.loop(G, 5 + 4 * HPG + 3 * TT + 7 * TT) as g:
                hold(dve, pa["oc"], g * TT + 1)
                ch.add(nc.vector.tensor_copy(gg, gtok.rearrange("p a (r j) -> p a r j", r=3)[:, :, :, ds(g * HPG, HPG)]))
                for j in range(HPG):
                    ch.add(nc.vector.tensor_copy(Vblk[32 * j:32 * j + NB_P, DK * j:DK * j + DK],
                                                 Vc[32 * j:32 * j + NB_P, ds(g * DK, DK)]))
                ch.settle()
                dve.sem_inc(pa["k"], 1)

                def maxes(u):
                    t = u // HPG
                    dve.wait_ge(pa["s"], g * 16 + u + 2)
                    sc = ps[:, 2 * (u % 2):2 * (u % 2) + 2, :]
                    ch.link(nc.vector.tensor_tensor(sc[:, :, P * t:P * t + P], sc[:, :, P * t:P * t + P],
                                                    diag.unsqueeze(1).to_broadcast([P, 2, P]), ALU.add))
                    dve.wait_ge(pa["p"], g * 16 + max(u, 1))
                    nc.vector.tensor_reduce(nmax[u % 2], sc[:, :, 0:P * (t + 1)], AX.X, ALU.max, negate=True)\
                        .then_inc(pa["max"], 1)

                for u in range(-1, 4 * HPG + 1):
                    t = u // HPG
                    if u + 1 < 4 * HPG:
                        maxes(u + 1)
                    if 0 <= u and u % HPG == HPG - 1:
                        dve.wait_ge(pa["cexp"], g * TT + t + 2)
                        ch.link(nc.vector.tensor_tensor(Scm, Scm, cm_one[:, t:t + 1, :].to_broadcast([P, HPG, NB_P]),
                                                        ALU.mult))
                        nc.vector.tensor_reduce(csum, Scm, AX.X, ALU.add).then_inc(pa["csum"], 1)
                    if 0 <= u < 4 * HPG:
                        dve.wait_ge(pa["ts"], g * 16 + u + 2)
                        dve.wait_ge(pa["o"], g * 16 + max(u, 1))
                        nc.vector.tensor_copy(PT[u % 2][:, 0, 0:t + 1, :],
                                              ps[:, 4, 0:P * (t + 1)].rearrange("p (s t) -> p s t", t=P)).then_inc(pa["es"], 1)
                    if u < 4 * HPG and u % HPG == 2:
                        dve.wait_ge(pa["cs"], g * TT + t + 2)
                        dve.wait_ge(pa["ct"], g * TT + t + 1)
                        ch.link(nc.vector.tensor_tensor(
                            Scm, ps[:, 7, 0:P].rearrange("p (j s) -> p j s", j=HPG)[:, :, 0:NB_P],
                            cm_add[:, t:t + 1, :].to_broadcast([P, HPG, NB_P]), ALU.add))
                        ch.link(nc.vector.tensor_reduce(cmx, Scm, AX.X, ALU.max))
                        nc.vector.tensor_tensor(Scm, Scm, cmx.unsqueeze(2).to_broadcast([P, HPG, NB_P]),
                                                ALU.subtract).then_inc(pa["cmax"], 1)
                    if u >= HPG and u % HPG == 0:
                        dve.wait_ge(pa["csum"], g * TT + t + 1)
                        dve.wait_ge(pa["p"], g * 16 + u + 1)
                        ch.add(nc.vector.tensor_scalar(wts[:, 0, :], csum, TINY, None, ALU.max))
                        ch.link(nc.vector.tensor_scalar(wts[:, 1:3, :], sums[(t - 1) % 2], TINY, None, ALU.max))
                        ch.link(nc.vector.reciprocal(wts, wts))
                        ch.link(nc.vector.tensor_tensor(wts, wts, gg[:, t - 1, :, :], ALU.mult))
                        dve.wait_ge(pa["o"], g * 16 + u + 1)
                        ch.add(nc.vector.tensor_tensor(
                            mix[:, 1:3, :, :].rearrange("p r j d -> p (r j) d"),
                            ps[:, 6, :].rearrange("p (j d) -> p j d", d=DK),
                            wts[:, 1:3, :].rearrange("p r j -> p (r j)").unsqueeze(2).to_broadcast([P, 2 * HPG, DK]),
                            ALU.mult))
                        dve.wait_ge(pa["oc"], g * TT + t + 1)
                        dve.wait_ge(pa["ot"], g * TT + t)
                        ch.link(nc.vector.tensor_tensor(
                            mix[:, 0, :, :], ps[:, 7, 256:512].rearrange("p (j d) -> p j d", j=HPG),
                            wts[:, 0, :].unsqueeze(2).to_broadcast([P, HPG, DK]), ALU.mult))
                        ch.link(nc.vector.tensor_tensor(mix[:, 0, :, :], mix[:, 0, :, :], mix[:, 1, :, :], ALU.add))
                        nc.vector.tensor_tensor(otok, mix[:, 0, :, :], mix[:, 2, :, :], ALU.add).then_inc(pa["mixed"], 1)

            dve.wait_ge(pa["h"], G * TT + 1)
            dve.sem_inc(sa["os"], 1)
            dve.wait_ge(attn_const, 2)
            def sample_turn(b, attend, compress):
                def evac(v):
                    if compress or v < 10:
                        dve.wait_ge(sa["turned"], b * 26 + 16 + v + 2 + past["turned"])
                        dve.wait_ge(sa["mul"], b * 26 + 16 + v + past["mul"])
                        nc.vector.tensor_copy(TK[1], ps[:, 1, :]).then_inc(sa["ev1"], 1)

                def part_a(e):
                    if compress:
                        dve.wait_ge(sa["mul"], b * 26 + 16 + 10 + 4 * e + 5 + past["mul"])
                        o = G * (e % 2)
                        nc.vector.tensor_scalar(At[:, o:o + G, 64 * (e // 2):64 * (e // 2) + 64],
                                                ps[0:DK, 2 + e % 2, 0:256].rearrange("p (g s) -> p g s", g=G),
                                                cbias[0:DK, e % 2:e % 2 + 1], None, ALU.add).then_inc(sa["ab_a"], 1)

                def own_rows(b):
                    ch.add(nc.vector.tensor_copy(Qp, QP[:, ds(b, 1), :, :].rearrange("p a r h -> p (a r) h")))
                    ch.add(nc.vector.tensor_copy(Qz, QZ[:, ds(b, 1), :, :].rearrange("p a r h -> p (a r) h")))
                    ch.add(nc.vector.tensor_copy(sw[:, 0:3], GS[:, :, ds(b, 1)].rearrange("p r b -> p (r b)")))
                    nc.vector.tensor_copy(Kn, KN[:, :, ds(b, 1)].rearrange("p r b -> p (r b)")).then_inc(sa["own"], 1)

                def take_compressed_values():
                    dve.wait_ge(sa["kc"], b + 2 + past["kc"])
                    nc.vector.tensor_scalar(VcS, ps[0:NB_S, 6, 0:GD], 0.5, None, ALU.mult).then_inc(sa["vc_taken"], 1)

                def compressed_max():
                    dve.wait_ge(sa["cs"], b + 2 + past["cs"])
                    nc.vector.tensor_reduce(smax[:, 0:1], ps[0:HEADS, 7, 0:NB_S], AX.X, ALU.max, negate=True)\
                        .then_inc(sa["cmax"], 1)
                    nc.vector.tensor_copy(S[:, PAST:NK], ps[0:HEADS, 7, 240:241]).then_inc(sa["new"], 1)

                def compressed_probs():
                    dve.wait_ge(sa["cexp"], b + 2 + past["cexp"])
                    ch.link(nc.vector.tensor_scalar(ssum[:, 0:1], ssum[:, 0:1], TINY, None, ALU.max))
                    ch.link(nc.vector.reciprocal(ssum[:, 0:1], ssum[:, 0:1]))
                    nc.vector.tensor_scalar(Pc[:, 0:NB_S], Pc[:, 0:NB_S], ssum[:, 0:1], None, ALU.mult).then_inc(sa["pn"], 1)

                def window_max():
                    dve.wait_ge(sa["mul"], b * 26 + 16 + 11 + past["mul"])
                    nc.vector.tensor_reduce(smax[:, 2:3], ps[0:HEADS, 6, :], AX.X, ALU.max, negate=True)\
                        .then_inc(sa["wmax"], 1)

                def take_turned_probs():
                    dve.wait_ge(sa["pnt"], b + 2 + past["pnt"])
                    nc.vector.tensor_copy(PnT, ps[0:NB_S, 7, 128:128 + HEADS]).then_inc(sa["pnt_taken"], 1)

                def take_block_scores():
                    dve.wait_ge(sa["u"], b + 2 + past["u"])
                    nc.vector.tensor_copy(U, ps[0:HEADS, 7, 160:160 + NSLC]).then_inc(sa["u_taken"], 1)

                def select():
                    dve.wait_ge(sa["imp"], b + 2 + past["imp"])
                    ch.link(nc.vector.tensor_copy(score, ps[0:HEADS, 7, 200:200 + NSLC]))
                    ch.add(nc.vector.memset(score[:, 0:1], FORCED_SCORE))
                    ch.link(nc.vector.memset(score[:, NSLC - 2:NSLC], FORCED_SCORE))
                    for a_, (src, dst) in enumerate(((score, score2), (score2, score))):
                        dve.sem_inc(passed, 1)
                        ch.link(nc.vector.max(top[a_], src))
                        dve.sem_inc(passed, 1)
                        ch.link(nc.vector.match_replace(dst, top[a_], src, -2.0))
                    ch.link(nc.vector.tensor_scalar(madd, score, -1.5, NEG_INF, ALU.is_gt, ALU.mult))

                def mask_scores(qs):
                    for q in qs:
                        dve.wait_ge(sa["qs"], b * 4 + q + 2 + past["qs"])
                        v = S[:, 512 * q:512 * q + 512].rearrange("p (r j i) -> p r j i", r=4, i=8)
                        jj = 16 * (q // 2)
                        ch.add(nc.vector.tensor_tensor(v, v, madd[:, jj:jj + 16].unsqueeze(1).unsqueeze(3)
                                                       .to_broadcast([HEADS, 4, 16, 8]), ALU.add))

                def selected_max():
                    ch.settle()
                    dve.wait_ge(sa["new"], b + 2 + past["new"])
                    nc.vector.tensor_reduce(smax[:, 1:2], S[:, 0:NK], AX.X, ALU.max, negate=True).then_inc(sa["smax"], 1)

                def scales():
                    dve.wait_ge(sa["wexp"], b + 2 + past["wexp"])
                    dve.wait_ge(sa["sexp"], b + 2 + past["sexp"])
                    ch.link(nc.vector.tensor_scalar(ssum[:, 1:3], ssum[:, 1:3], TINY, None, ALU.max))
                    ch.link(nc.vector.reciprocal(ssum[:, 1:3], ssum[:, 1:3]))
                    ch.link(nc.vector.tensor_tensor(sw[:, 1:3], sw[:, 1:3], ssum[:, 1:3], ALU.mult))
                    nc.vector.tensor_tensor(Dg, ident[0:HEADS, 0:HEADS].unsqueeze(1).to_broadcast([HEADS, 3, HEADS]),
                                            sw[:, 0:3].unsqueeze(2).to_broadcast([HEADS, 3, HEADS]), ALU.mult)\
                        .then_inc(sa["dg"], 1)

                def take_scaled_probs():
                    dve.wait_ge(sa["pt"], b + 2 + past["pt"])
                    ch.add(nc.vector.tensor_copy(PTs[:, 0:320], ps[:, 7, 0:320]))
                    ch.add(nc.vector.tensor_copy(PTs[0:1, 320:336], ps[0:1, 7, 320:336]))
                    nc.vector.tensor_copy(PTs[0:NB_S, 336:352], ps[0:NB_S, 7, 336:352]).then_inc(sa["pt_taken"], 1)

                def take_values():
                    hold(dve, sa["o"], b + 2 + past["o"])
                    nc.vector.tensor_copy(Osb[:, ds(b, 1), :].rearrange("p b n -> p (b n)"), ps[0:HEADS, 6, 0:GD])\
                        .then_inc(sa["os"], 1)

                if attend:
                    evac(1)
                    dve.wait_ge(sa["tanh"], b + 2 + past["tanh"])
                    nc.vector.scalar_tensor_tensor(out=Hs, in0=Hs, scalar=1.0, in1=Zs, op0=ALU.add, op1=ALU.mult)\
                        .then_inc(sa["h"], 1)
                    evac(3)
                    take_compressed_values()
                    evac(5)
                    evac(7)
                    compressed_max()
                    evac(9)
                    compressed_probs()
                    window_max()
                    take_turned_probs()
                evac(11)
                if attend:
                    take_block_scores()
                evac(13)
                if attend:
                    select()
                evac(15)
                part_a(0)
                if attend:
                    mask_scores((0, 1))
                evac(17)
                if attend:
                    mask_scores((2, 3))
                evac(19)
                if attend:
                    selected_max()
                part_a(1)
                evac(21)
                if attend:
                    scales()
                    take_scaled_probs()
                if compress:
                    own_rows(b + 1)
                evac(23)
                part_a(2)
                if attend:
                    take_values()
                evac(25)
                part_a(3)
                if compress:
                    dve.wait_ge(sa["ab_a"], b * 4 + 9 + past["ab_a"])
                    dve.wait_ge(sa["ab_b"], b * 4 + 9 + past["ab_b"])
                    nc.vector.tensor_tensor(Zs, At[:, :, 0:NB_S], Bt[:, :, 1:NB_S + 1], ALU.add).then_inc(sa["z"], 1)

            sample_turn(-1, False, True)
            with ch.loop(B - 1, 22) as b:
                sample_turn(b, True, True)
            sample_turn(B - 1, True, False)
            dve.wait_ge(sa["o"], B + 2 + past["o"])
            ch.link(nc.vector.tensor_copy(OS.rearrange("p b a h -> p (b a h)"), ps[:, 5, 0:B * 2 * HEADS]))
            for g in range(G):
                r = DK * (g % 2)
                for par in range(2):
                    lo = HPG * g + par
                    nc.vector.tensor_copy(h[DK * par:DK * par + DK, 2 * g:2 * g + 2, T:N],
                                          OS[r:r + DK, :, g // 2, lo:lo + 3:2].rearrange("p b c -> p c b"))\
                        .then_inc(hready, 1)
            residual("nsa_out")
            norm_dve("mlp1")
            squared_relu("up1")
            residual("down1")
            norm_dve("final")
            for k in range(KD):
                nc.vector.scalar_tensor_tensor(out=h[:, k, :], in0=x[:, k, :],
                                               scalar=vec[:, GAIN_FINAL + k:GAIN_FINAL + k + 1], in1=rstd[:],
                                               op0=ALU.mult, op1=ALU.mult).then_inc(norm["out"], 1)
            for u in range(0, 2 * TT, 2):
                dve.wait_ge(yturned, u + 1)
                nc.vector.tensor_copy(yrows[:, u % TT, 512 * (u // TT):512 * (u // TT) + 512], ps[:, u % 4, :])\
                    .then_inc(ydone[0], 1)
            dve.wait_ge(yturned, 2 * TT + 1)
            nc.vector.tensor_copy(ysrows.rearrange("p (c n) -> p c n", c=2), ps[0:B, 4:6, :]).then_inc(ysdone, 1)


_INS = ["x_prompt", "x_sample", "cache_nsa_kv", "cache_win_kv", "state_hgrn", "page_table", "norm_mix", "norm_mlp",
        "w_mlp_up", "w_mlp_down", "w_hgrn_in", "hgrn_lb_logits", "hgrn_onorm", "w_hgrn_out", "norm_kv", "w_kv",
        "cmp_pe_k", "cmp_w1_k", "cmp_w2_k", "cmp_pe_v", "cmp_w1_v", "cmp_w2_v", "w_nsa_q", "w_nsa_out", "norm_final"]
_OUTS = [(1, 512, 1024), (8, 1, 1024), (1, 512, 4, 4, 64), (8, 1, 4, 4, 64), (1, 512, 2, 4, 64), (8, 512, 2, 4, 64),
         (1, 1, 8, 128, 128), (1, 8, 8, 128, 128)]


def kernel(**inputs):
    import numpy as _np
    import concourse.bacc as _bacc
    from concourse import mybir as _mybir
    from concourse.bass_utils import run_bass_kernel_spmd as _run

    nc = _bacc.Bacc("TRN2", target_bir_lowering=False, num_devices=1)
    arrays, args = {}, {}
    for name in _INS:
        a = _np.ascontiguousarray(inputs[name])
        arrays[f"in_{name}"] = a
        args[name] = nc.dram_tensor(f"in_{name}", a.shape, _mybir.dt.from_np(a.dtype), kind="ExternalInput").ap()
    outs = [nc.dram_tensor(f"out_{i}", s, _mybir.dt.float32, kind="ExternalOutput").ap() for i, s in enumerate(_OUTS)]
    hybrid_step(nc, args, outs)
    r = _run(nc, [arrays], core_ids=[0])
    return tuple(r.results[0][f"out_{i}"] for i in range(len(_OUTS)))
```
